# Optimizing a Trainium2 kernel written in Bass

```python
import math
import jax, jax.numpy as jnp
from jax import lax
import numpy as np
import jax
import jax.numpy as jnp

D_MODEL = 1024
BATCH = 1
SEQ = 512
DEPTH = 1

D_MIX = D_MODEL
GLA_WIDTH = D_MIX // 2
S5_WIDTH = D_MIX - GLA_WIDTH
GLA_HEADS = 4
GLA_DV = GLA_WIDTH // GLA_HEADS
GLA_DK = GLA_DV // 2
GLA_LOWRANK = 16
GLA_TAU = 16.0
GLA_CHUNK = 64
S5_CH = 16
S5_GROUPS = S5_WIDTH // S5_CH
S5_STATE = 64
DT_MIN = 1e-3
DT_MAX = 1e-1
N_EXPERTS = 32
TOP_K = 4
D_FF = D_MODEL
SWIGLU_ALPHA = 1.702
SWIGLU_LIMIT = 7.0
MOE_BLOCK = 128
EPS = 1e-6
Q_COLS = GLA_HEADS * GLA_DK
K_COLS = GLA_HEADS * GLA_DK
V_COLS = GLA_WIDTH
G_COLS = GLA_WIDTH
A_COLS = GLA_LOWRANK
U_COLS = S5_WIDTH
N_IN = Q_COLS + K_COLS + V_COLS + G_COLS + A_COLS + U_COLS
SPLITS = [Q_COLS, Q_COLS + K_COLS, Q_COLS + K_COLS + V_COLS, Q_COLS + K_COLS + V_COLS + G_COLS,
          Q_COLS + K_COLS + V_COLS + G_COLS + A_COLS]


def rmsnorm(x, g):
    xf = x.astype(jnp.float32)
    r = lax.rsqrt(jnp.mean(xf * xf, axis=-1, keepdims=True) + EPS)
    return (xf * r * g.astype(jnp.float32)).astype(x.dtype)

def gla_chunked(q, k, v, log_a):
    f32 = jnp.float32
    B_, H_, T_, DK_ = q.shape
    DV_ = v.shape[-1]
    C = GLA_CHUNK
    nc = T_ // C
    q = q.astype(f32).reshape(B_, H_, nc, C, DK_) * (DK_ ** -0.5)
    k = k.astype(f32).reshape(B_, H_, nc, C, DK_)
    v = v.astype(f32).reshape(B_, H_, nc, C, DV_)
    b = jnp.cumsum(log_a.astype(f32).reshape(B_, H_, nc, C, DK_), axis=3)
    b_last = b[:, :, :, -1:, :]
    q_dec = q * jnp.exp(b)
    k_inv = k * jnp.exp(-b)
    k_to_end = k * jnp.exp(b_last - b)
    causal = jnp.tril(jnp.ones((C, C), dtype=bool))
    scores = jnp.where(causal, jnp.einsum('bhnik,bhnjk->bhnij', q_dec, k_inv), 0.0)
    o_intra = jnp.einsum('bhnij,bhnjv->bhniv', scores, v)
    delta = jnp.einsum('bhnjk,bhnjv->bhnkv', k_to_end, v)
    decay = jnp.exp(b_last[:, :, :, 0, :])

    def step(S, inp):
        d, dS = inp
        return d[..., None] * S + dS, S

    S0 = jnp.zeros((B_, H_, DK_, DV_), f32)
    _, S_prev = lax.scan(step, S0, (jnp.moveaxis(decay, 2, 0), jnp.moveaxis(delta, 2, 0)))
    S_prev = jnp.moveaxis(S_prev, 0, 2)
    o_inter = jnp.einsum('bhnik,bhnkv->bhniv', q_dec, S_prev)
    return (o_intra + o_inter).reshape(B_, H_, T_, DV_)

def s5_layer(u, lam_re, lam_im, log_dt, b_re, b_im, c_re, c_im, d, glu_w, glu_b):
    f32 = jnp.float32
    B_, T_, _ = u.shape
    uf = u.astype(f32).reshape(B_, T_, S5_GROUPS, S5_CH)
    lr = lam_re.astype(f32)
    li = lam_im.astype(f32)
    dt = jnp.exp(log_dt.astype(f32))[:, None]
    mag = jnp.exp(lr * dt)
    ab_re = mag * jnp.cos(li * dt)
    ab_im = mag * jnp.sin(li * dt)
    den = lr * lr + li * li
    f_re = ((ab_re - 1.0) * lr + ab_im * li) / den
    f_im = (ab_im * lr - (ab_re - 1.0) * li) / den
    br = b_re.astype(f32)
    bi = b_im.astype(f32)
    bb_re = f_re[..., None] * br - f_im[..., None] * bi
    bb_im = f_re[..., None] * bi + f_im[..., None] * br
    bu_re = jnp.einsum('btgh,gph->btgp', uf, bb_re)
    bu_im = jnp.einsum('btgh,gph->btgp', uf, bb_im)
    a_re = jnp.broadcast_to(ab_re, (1, T_, S5_GROUPS, S5_STATE))
    a_im = jnp.broadcast_to(ab_im, (1, T_, S5_GROUPS, S5_STATE))

    def combine(e1, e2):
        a1r, a1i, b1r, b1i = e1
        a2r, a2i, b2r, b2i = e2
        return (a2r * a1r - a2i * a1i,
                a2r * a1i + a2i * a1r,
                a2r * b1r - a2i * b1i + b2r,
                a2r * b1i + a2i * b1r + b2i)

    _, _, xr, xi = lax.associative_scan(combine, (a_re, a_im, bu_re, bu_im), axis=1)
    y = (jnp.einsum('btgp,ghp->btgh', xr, c_re.astype(f32))
         - jnp.einsum('btgp,ghp->btgh', xi, c_im.astype(f32))
         + d.astype(f32) * uf)
    y = jax.nn.gelu(y.reshape(B_, T_, S5_WIDTH))
    return y * jax.nn.sigmoid(y @ glu_w.astype(f32) + glu_b.astype(f32))

def moe_ffn(h, router_w, router_b, w_gu, b_gu, w_down, b_down):
    f32 = jnp.float32
    B_, T_, D_ = h.shape
    N = B_ * T_
    NK = N * TOP_K
    xt = h.reshape(N, D_)
    logits = (xt @ router_w + router_b).astype(f32)
    top_val, top_idx = lax.top_k(logits, TOP_K)
    gate = jax.nn.softmax(top_val, axis=-1)
    flat_e = top_idx.reshape(NK).astype(jnp.int32)
    flat_tok = jnp.arange(NK, dtype=jnp.int32) // TOP_K
    flat_w = gate.reshape(NK)
    order = jnp.argsort(flat_e)
    se, stok, sw = flat_e[order], flat_tok[order], flat_w[order]
    counts = jnp.zeros((N_EXPERTS,), jnp.int32).at[flat_e].add(1)
    starts = jnp.cumsum(counts) - counts
    padded = (counts + MOE_BLOCK - 1) // MOE_BLOCK * MOE_BLOCK
    pends = jnp.cumsum(padded)
    pstarts = pends - padded
    dest = pstarts[se] + jnp.arange(NK, dtype=jnp.int32) - starts[se]
    n_blocks = -(-NK // MOE_BLOCK) + N_EXPERTS
    cap = n_blocks * MOE_BLOCK
    tok_buf = jnp.full((cap,), N, jnp.int32).at[dest].set(stok)
    w_buf = jnp.zeros((cap,), f32).at[dest].set(sw)
    block_e = jnp.minimum(
        jnp.searchsorted(pends, jnp.arange(n_blocks, dtype=jnp.int32) * MOE_BLOCK, side='right'),
        N_EXPERTS - 1).astype(jnp.int32)
    x_pad = jnp.concatenate([xt, jnp.zeros((1, D_), xt.dtype)], axis=0)
    xb = x_pad[tok_buf].reshape(n_blocks, MOE_BLOCK, D_)

    def expert_block(args):
        xblk, e = args
        gu = xblk @ w_gu[e] + b_gu[e]
        g, up = gu[:, :D_FF], gu[:, D_FF:]
        g = jnp.minimum(g, SWIGLU_LIMIT)
        up = jnp.clip(up, -SWIGLU_LIMIT, SWIGLU_LIMIT)
        act = (up + 1.0) * (g * jax.nn.sigmoid(SWIGLU_ALPHA * g))
        return act @ w_down[e] + b_down[e]

    yb = lax.map(expert_block, (xb, block_e)).reshape(cap, D_)
    out = jnp.zeros((N + 1, D_), f32).at[tok_buf].add(yb.astype(f32) * w_buf[:, None])[:N]
    return out.reshape(B_, T_, D_).astype(h.dtype)

def first_inputs(seed: int = 0) -> dict:
    key = jax.random.key(seed)
    ks = jax.random.split(key, 32)
    f32 = jnp.float32
    L, D = DEPTH, D_MODEL

    def nrm(k, shape, scale):
        return jax.random.normal(k, shape, f32) * scale

    n_idx = jnp.arange(S5_STATE, dtype=f32)
    return {
        "x": nrm(ks[0], (BATCH, SEQ, D), 1.0),
        "c": nrm(ks[1], (BATCH, D), 1.0),
        "ada_w": nrm(ks[2], (L, D, 6 * D), 0.02),
        "ada_b": nrm(ks[3], (L, 6 * D), 0.02),
        "mix_pre_g": 1.0 + nrm(ks[4], (L, D), 0.05),
        "mix_post_g": 1.0 + nrm(ks[5], (L, D), 0.05),
        "ffn_pre_g": 1.0 + nrm(ks[6], (L, D), 0.05),
        "ffn_post_g": 1.0 + nrm(ks[7], (L, D), 0.05),
        "w_in": nrm(ks[8], (L, D, N_IN), D ** -0.5),
        "w_alpha": nrm(ks[9], (L, GLA_LOWRANK, GLA_HEADS * GLA_DK), GLA_LOWRANK ** -0.5),
        "b_alpha": nrm(ks[10], (L, GLA_HEADS * GLA_DK), 0.1),
        "gla_norm_g": 1.0 + nrm(ks[11], (L, GLA_DV), 0.05),
        "s5_lambda_re": -0.5 + nrm(ks[12], (L, S5_GROUPS, S5_STATE), 0.01),
        "s5_lambda_im": math.pi * n_idx + nrm(ks[13], (L, S5_GROUPS, S5_STATE), 0.01),
        "s5_log_dt": jax.random.uniform(ks[14], (L, S5_GROUPS), f32, math.log(DT_MIN), math.log(DT_MAX)),
        "s5_b_re": nrm(ks[15], (L, S5_GROUPS, S5_STATE, S5_CH), (2 * S5_CH) ** -0.5),
        "s5_b_im": nrm(ks[16], (L, S5_GROUPS, S5_STATE, S5_CH), (2 * S5_CH) ** -0.5),
        "s5_c_re": nrm(ks[17], (L, S5_GROUPS, S5_CH, S5_STATE), S5_STATE ** -0.5),
        "s5_c_im": nrm(ks[18], (L, S5_GROUPS, S5_CH, S5_STATE), S5_STATE ** -0.5),
        "s5_d": nrm(ks[19], (L, S5_GROUPS, S5_CH), 1.0),
        "s5_glu_w": nrm(ks[20], (L, S5_WIDTH, S5_WIDTH), S5_WIDTH ** -0.5),
        "s5_glu_b": nrm(ks[21], (L, S5_WIDTH), 0.01),
        "w_out": nrm(ks[22], (L, D_MIX, D), D_MIX ** -0.5),
        "router_w": nrm(ks[23], (L, D, N_EXPERTS), D ** -0.5),
        "router_b": nrm(ks[24], (L, N_EXPERTS), 0.01),
        "exp_w_gu": nrm(ks[25], (L, N_EXPERTS, D, 2 * D_FF), D ** -0.5),
        "exp_b_gu": nrm(ks[26], (L, N_EXPERTS, 2 * D_FF), 0.01),
        "exp_w_down": nrm(ks[27], (L, N_EXPERTS, D_FF, D), D_FF ** -0.5),
        "exp_b_down": nrm(ks[28], (L, N_EXPERTS, D), 0.01),
    }

def first_block(x, c, ada_w, ada_b, mix_pre_g, mix_post_g, ffn_pre_g, ffn_post_g, w_in, w_alpha, b_alpha,
              gla_norm_g, s5_lambda_re, s5_lambda_im, s5_log_dt, s5_b_re, s5_b_im, s5_c_re, s5_c_im, s5_d,
              s5_glu_w, s5_glu_b, w_out, router_w, router_b, exp_w_gu, exp_b_gu, exp_w_down, exp_b_down):
    B_, T_, D_ = x.shape
    h = x
    for l in range(DEPTH):
        mod = jax.nn.silu(c) @ ada_w[l] + ada_b[l]
        sh1, sc1, g1, sh2, sc2, g2 = jnp.split(mod, 6, axis=-1)

        hn = rmsnorm(h, mix_pre_g[l]) * (1.0 + sc1[:, None, :]) + sh1[:, None, :]
        proj = hn @ w_in[l]
        q, k, v, og, a_lr, u = jnp.split(proj, SPLITS, axis=-1)

        def heads(t, dh):
            return t.reshape(B_, T_, GLA_HEADS, dh).transpose(0, 2, 1, 3)

        log_a = jax.nn.log_sigmoid((a_lr @ w_alpha[l] + b_alpha[l]).astype(jnp.float32)) / GLA_TAU
        o = gla_chunked(heads(q, GLA_DK), heads(k, GLA_DK), heads(v, GLA_DV), heads(log_a, GLA_DK))
        o = rmsnorm(o, gla_norm_g[l]).transpose(0, 2, 1, 3)
        gla_out = (o * jax.nn.silu(og.astype(jnp.float32)).reshape(B_, T_, GLA_HEADS, GLA_DV))
        gla_out = gla_out.reshape(B_, T_, GLA_WIDTH).astype(hn.dtype)

        s5_out = s5_layer(u, s5_lambda_re[l], s5_lambda_im[l], s5_log_dt[l], s5_b_re[l], s5_b_im[l],
                          s5_c_re[l], s5_c_im[l], s5_d[l], s5_glu_w[l], s5_glu_b[l]).astype(hn.dtype)

        mix = jnp.concatenate([gla_out, s5_out], axis=-1) @ w_out[l]
        h = h + g1[:, None, :] * rmsnorm(mix, mix_post_g[l])

        hn2 = rmsnorm(h, ffn_pre_g[l]) * (1.0 + sc2[:, None, :]) + sh2[:, None, :]
        ff = moe_ffn(hn2, router_w[l], router_b[l], exp_w_gu[l], exp_b_gu[l], exp_w_down[l], exp_b_down[l])
        h = h + g2[:, None, :] * rmsnorm(ff, ffn_post_g[l])
    return h


GRID_W = 64
CTX_LEN = 256
HEAD_DIM = 64
ROPE_BASE = 10000.0
BLK = 128
A_HEADS = 8
A_KV_HEADS = 2
WINDOW = 128
SSM_HEADS = 16
SSM_HEADDIM = 64
SSM_INNER = SSM_HEADS * SSM_HEADDIM
SSM_GROUPS = 2
SSM_STATE = 128
SSM_CONV = 3
SSM_CHUNK = 128
SSM_BC = SSM_GROUPS * SSM_STATE
SSM_XBC = SSM_INNER + 2 * SSM_BC
C_HEADS = 8
C_KV_HEADS = 2
D_FF_2 = 2816
FFN_CONV = 3
A_Q_W = A_HEADS * HEAD_DIM
A_KV_W = A_KV_HEADS * HEAD_DIM
C_Q_W = C_HEADS * HEAD_DIM
C_KV_W = C_KV_HEADS * HEAD_DIM
IN_WIDTH = (A_Q_W + 2 * A_KV_W) + (SSM_INNER + SSM_XBC + 2 * SSM_HEADS) + (C_Q_W + 2 * C_KV_W) + 3 * D_MODEL


def _in_spans():
    sizes = (('a_q', A_Q_W), ('a_k', A_KV_W), ('a_v', A_KV_W),
             ('b_z', SSM_INNER), ('b_xbc', SSM_XBC), ('b_dt', 2 * SSM_HEADS),
             ('c_q', C_Q_W), ('c_k', C_KV_W), ('c_v', C_KV_W),
             ('gates', 3 * D_MODEL))
    spans, start = {}, 0
    for name, n in sizes:
        spans[name] = (start, start + n)
        start += n
    return spans

def rms_norm(x, g):
    xf = x.astype(jnp.float32)
    y = xf * lax.rsqrt(jnp.mean(xf * xf, axis=-1, keepdims=True) + EPS)
    return (y * g.astype(jnp.float32)).astype(x.dtype)

def modulate(h, shift, scale):
    return h * (1 + scale) + shift

def grid_rope(rows):
    t_row = jnp.repeat(jnp.arange(rows), GRID_W).astype(jnp.float32)
    t_col = jnp.tile(jnp.arange(GRID_W), rows).astype(jnp.float32)
    n = HEAD_DIM // 4
    inv = ROPE_BASE ** (-jnp.arange(n, dtype=jnp.float32) / n)
    ang = jnp.concatenate([t_row[:, None] * inv, t_col[:, None] * inv], axis=-1)
    return jnp.cos(ang), jnp.sin(ang)

def apply_rope(x, cos, sin):
    b, L, h, dh = x.shape
    xr = x.astype(jnp.float32).reshape(b, L, h, dh // 2, 2)
    c = cos[None, :, None, :]
    s = sin[None, :, None, :]
    x1, x2 = xr[..., 0], xr[..., 1]
    out = jnp.stack([x1 * c - x2 * s, x1 * s + x2 * c], axis=-1)
    return out.reshape(b, L, h, dh).astype(x.dtype)

def dwconv(u, w, bias):
    k = w.shape[0]
    pad = k // 2
    y = lax.conv_general_dilated(u, w[:, None, :].astype(u.dtype), window_strides=(1,),
                                 padding=[(pad, pad)], dimension_numbers=('NWC', 'WIO', 'NWC'),
                                 feature_group_count=u.shape[-1])
    return y + bias.astype(u.dtype)

def dense_attention(q, k, v, sink):
    b, lq, hq, dh = q.shape
    hkv = k.shape[2]
    g = hq // hkv
    qg = q.reshape(b, lq, hkv, g, dh)
    s = jnp.einsum('bqhgd,bkhd->bhgqk', qg, k).astype(jnp.float32) * (dh ** -0.5)
    if sink is not None:
        s_sink = jnp.broadcast_to(sink.astype(jnp.float32).reshape(1, hkv, g, 1, 1), s.shape[:-1] + (1,))
        s = jnp.concatenate([s, s_sink], axis=-1)
    p = jax.nn.softmax(s, axis=-1)
    if sink is not None:
        p = p[..., :-1]
    o = jnp.einsum('bhgqk,bkhd->bqhgd', p.astype(v.dtype), v)
    return o.reshape(b, lq, hq * dh)

def window_attention(q, k, v, kc, vc, sink):
    b, L, hq, dh = q.shape
    hkv = k.shape[2]
    g = hq // hkv
    nb = L // BLK
    lc = kc.shape[1]
    qb = q.reshape(b, nb, BLK, hkv, g, dh)
    pad = ((0, 0), (BLK, BLK), (0, 0), (0, 0))
    kp = jnp.pad(k, pad).reshape(b, nb + 2, BLK, hkv, dh)
    vp = jnp.pad(v, pad).reshape(b, nb + 2, BLK, hkv, dh)
    kw = jnp.concatenate([kp[:, :-2], kp[:, 1:-1], kp[:, 2:]], axis=2)
    vw = jnp.concatenate([vp[:, :-2], vp[:, 1:-1], vp[:, 2:]], axis=2)
    scale = dh ** -0.5
    s_loc = jnp.einsum('bnqhgd,bnjhd->bnhgqj', qb, kw).astype(jnp.float32) * scale
    s_ctx = jnp.einsum('bnqhgd,bchd->bnhgqc', qb, kc).astype(jnp.float32) * scale
    q_pos = (jnp.arange(nb) * BLK)[:, None] + jnp.arange(BLK)[None, :]
    k_pos = (jnp.arange(nb) * BLK - BLK)[:, None] + jnp.arange(3 * BLK)[None, :]
    rel = q_pos[:, :, None] - k_pos[:, None, :]
    valid = (jnp.abs(rel) <= WINDOW) & (k_pos[:, None, :] >= 0) & (k_pos[:, None, :] < L)
    s_loc = jnp.where(valid[None, :, None, None], s_loc, -jnp.inf)
    s_sink = jnp.broadcast_to(sink.astype(jnp.float32).reshape(1, 1, hkv, g, 1, 1), s_loc.shape[:-1] + (1,))
    p = jax.nn.softmax(jnp.concatenate([s_loc, s_ctx, s_sink], axis=-1), axis=-1)
    nloc = 3 * BLK
    p_loc = p[..., :nloc].astype(v.dtype)
    p_ctx = p[..., nloc:nloc + lc].astype(v.dtype)
    o = jnp.einsum('bnhgqj,bnjhd->bnqhgd', p_loc, vw) + jnp.einsum('bnhgqc,bchd->bnqhgd', p_ctx, vc)
    return o.reshape(b, L, hq * dh)

def grid_attention(q, k, v, kc, vc):
    b, L, hq, dh = q.shape
    nb = L // BLK
    k_all = jnp.concatenate([k, kc], axis=1)
    v_all = jnp.concatenate([v, vc], axis=1)
    qb = jnp.moveaxis(q.reshape(b, nb, BLK, hq, dh), 1, 0)
    ob = lax.map(lambda qi: dense_attention(qi, k_all, v_all, None), qb)
    return jnp.moveaxis(ob, 0, 1).reshape(b, L, hq * dh)

def ssm_inputs(xbc_raw, dt_raw, conv_w, conv_b, dt_bias):
    b, L, _ = xbc_raw.shape
    xbc = jax.nn.silu(dwconv(xbc_raw, conv_w, conv_b))
    xs = xbc[..., :SSM_INNER].reshape(b, L, SSM_HEADS, SSM_HEADDIM)
    bm = xbc[..., SSM_INNER:SSM_INNER + SSM_BC].reshape(b, L, SSM_GROUPS, SSM_STATE)
    cm = xbc[..., SSM_INNER + SSM_BC:].reshape(b, L, SSM_GROUPS, SSM_STATE)
    dt = jax.nn.softplus(dt_raw.astype(jnp.float32).reshape(b, L, 2, SSM_HEADS) + dt_bias.astype(jnp.float32))
    return xs, bm, cm, dt

def ssd_scan(xh, dt, a_coef, bm, cm, h0, want_y):
    b, L, H, P = xh.shape
    G, N = bm.shape[2], bm.shape[3]
    hg = H // G
    q = SSM_CHUNK
    nc = L // q
    f32 = jnp.float32
    xdt = (xh.astype(f32) * dt[..., None]).reshape(b, nc, q, G, hg, P)
    bc = bm.astype(f32).reshape(b, nc, q, G, N)
    cc = cm.astype(f32).reshape(b, nc, q, G, N)
    acs = jnp.cumsum((dt * a_coef.astype(f32)).reshape(b, nc, q, G, hg), axis=2)
    decay_end = jnp.exp(acs[:, :, -1:] - acs)
    states = jnp.einsum('bcjgn,bcjghp->bcghpn', bc, xdt * decay_end[..., None])
    chunk_decay = jnp.exp(acs[:, :, -1])

    def step(h, inp):
        st, dec = inp
        return h * dec[..., None, None] + st, h

    h_last, h_in = lax.scan(step, h0.reshape(b, G, hg, P, N),
                            (jnp.moveaxis(states, 1, 0), jnp.moveaxis(chunk_decay, 1, 0)))
    h_last = h_last.reshape(b, H, P, N)
    if not want_y:
        return None, h_last
    h_in = jnp.moveaxis(h_in, 0, 1)
    seg = acs[:, :, :, None] - acs[:, :, None, :]
    tri = jnp.tril(jnp.ones((q, q), dtype=bool))
    lmat = jnp.exp(jnp.where(tri[:, :, None, None], seg, -jnp.inf))
    cb = jnp.einsum('bcign,bcjgn->bcijg', cc, bc)
    y_diag = jnp.einsum('bcijgh,bcjghp->bcighp', cb[..., None] * lmat, xdt)
    y_off = jnp.einsum('bcign,bcghpn->bcighp', cc, h_in) * jnp.exp(acs)[..., None]
    y = (y_diag + y_off).reshape(b, L, H, P).astype(xh.dtype)
    return y, h_last

def ssm_output(yf, yb, xs, z, d_skip, norm_g):
    b, L = xs.shape[0], xs.shape[1]
    y = yf + yb + xs * d_skip[:, None].astype(xs.dtype)
    y = y.reshape(b, L, SSM_INNER)
    return rms_norm(y * jax.nn.silu(z), norm_g)

def merge_branches(ya, yb, yc, g_raw, w_oa, w_ob, w_oc, w_out):
    g = jax.nn.sigmoid(g_raw.astype(jnp.float32)).astype(ya.dtype)
    ga, gb, gc = jnp.split(g, 3, axis=-1)
    m = ga * (ya @ w_oa) + gb * (yb @ w_ob) + gc * (yc @ w_oc)
    return m @ w_out

def conv_ffn(h, w_up, w_gate, conv_w, conv_b, w_down):
    up = h @ w_up
    gt = dwconv(h @ w_gate, conv_w, conv_b)
    return (jax.nn.silu(gt) * up) @ w_down

def hybrid_layer(x, xc, c_mod, cc_mod, cos, sin, w_in, norm1, norm2, a_sink, ssm_conv_w, ssm_conv_b,
                 ssm_a_log, ssm_dt_bias, ssm_d, ssm_norm, c_q_norm, c_k_norm, w_oa, w_ob, w_oc, w_out,
                 ffn_w_up, ffn_w_gate, ffn_conv_w, ffn_conv_b, ffn_w_down, need_ctx_out):
    b, L, _ = x.shape
    lc = xc.shape[1]
    sp = _in_spans()
    shift1, scale1, gate1, shift2, scale2, gate2 = jnp.split(c_mod[:, None, :], 6, axis=-1)
    h = modulate(rms_norm(x, norm1), shift1, scale1)
    hc = modulate(rms_norm(xc, norm1), cc_mod[:D_MODEL], cc_mod[D_MODEL:2 * D_MODEL])
    u = h @ w_in

    def lat(name):
        return u[..., sp[name][0]:sp[name][1]]

    def ctxp(name):
        return hc @ w_in[:, sp[name][0]:sp[name][1]]

    qa = apply_rope(lat('a_q').reshape(b, L, A_HEADS, HEAD_DIM), cos, sin)
    ka = apply_rope(lat('a_k').reshape(b, L, A_KV_HEADS, HEAD_DIM), cos, sin)
    va = lat('a_v').reshape(b, L, A_KV_HEADS, HEAD_DIM)
    kac = ctxp('a_k').reshape(b, lc, A_KV_HEADS, HEAD_DIM)
    vac = ctxp('a_v').reshape(b, lc, A_KV_HEADS, HEAD_DIM)
    ya = window_attention(qa, ka, va, kac, vac, a_sink)

    qg = apply_rope(rms_norm(lat('c_q').reshape(b, L, C_HEADS, HEAD_DIM), c_q_norm), cos, sin)
    kg = apply_rope(rms_norm(lat('c_k').reshape(b, L, C_KV_HEADS, HEAD_DIM), c_k_norm), cos, sin)
    vg = lat('c_v').reshape(b, L, C_KV_HEADS, HEAD_DIM)
    kgc = rms_norm(ctxp('c_k').reshape(b, lc, C_KV_HEADS, HEAD_DIM), c_k_norm)
    vgc = ctxp('c_v').reshape(b, lc, C_KV_HEADS, HEAD_DIM)
    yg = grid_attention(qg, kg, vg, kgc, vgc)

    a_coef = -jnp.exp(ssm_a_log.astype(jnp.float32))
    xs_c, bm_c, cm_c, dt_c = ssm_inputs(ctxp('b_xbc'), ctxp('b_dt'), ssm_conv_w, ssm_conv_b, ssm_dt_bias)
    h0 = jnp.zeros((b, SSM_HEADS, SSM_HEADDIM, SSM_STATE), jnp.float32)
    yf_c, hf_c = ssd_scan(xs_c, dt_c[:, :, 0], a_coef[0], bm_c, cm_c, h0, need_ctx_out)
    yb_c, hb_c = ssd_scan(jnp.flip(xs_c, 1), jnp.flip(dt_c[:, :, 1], 1), a_coef[1],
                          jnp.flip(bm_c, 1), jnp.flip(cm_c, 1), h0, need_ctx_out)
    xs, bm, cm, dt = ssm_inputs(lat('b_xbc'), lat('b_dt'), ssm_conv_w, ssm_conv_b, ssm_dt_bias)
    yf, _ = ssd_scan(xs, dt[:, :, 0], a_coef[0], bm, cm, hf_c, True)
    yb, _ = ssd_scan(jnp.flip(xs, 1), jnp.flip(dt[:, :, 1], 1), a_coef[1],
                     jnp.flip(bm, 1), jnp.flip(cm, 1), hb_c, True)
    ys = ssm_output(yf, jnp.flip(yb, 1), xs, lat('b_z'), ssm_d, ssm_norm)

    x = x + gate1 * merge_branches(ya, ys, yg, lat('gates'), w_oa, w_ob, w_oc, w_out)
    h2 = modulate(rms_norm(x, norm2), shift2, scale2)
    x = x + gate2 * conv_ffn(h2, ffn_w_up, ffn_w_gate, ffn_conv_w, ffn_conv_b, ffn_w_down)
    if not need_ctx_out:
        return x, None

    cgate1 = cc_mod[2 * D_MODEL:3 * D_MODEL]
    cshift2 = cc_mod[3 * D_MODEL:4 * D_MODEL]
    cscale2 = cc_mod[4 * D_MODEL:5 * D_MODEL]
    cgate2 = cc_mod[5 * D_MODEL:]
    yac = dense_attention(ctxp('a_q').reshape(b, lc, A_HEADS, HEAD_DIM), kac, vac, a_sink)
    ygc = dense_attention(rms_norm(ctxp('c_q').reshape(b, lc, C_HEADS, HEAD_DIM), c_q_norm), kgc, vgc, None)
    ysc = ssm_output(yf_c, jnp.flip(yb_c, 1), xs_c, ctxp('b_z'), ssm_d, ssm_norm)
    xc = xc + cgate1 * merge_branches(yac, ysc, ygc, ctxp('gates'), w_oa, w_ob, w_oc, w_out)
    h2c = modulate(rms_norm(xc, norm2), cshift2, cscale2)
    xc = xc + cgate2 * conv_ffn(h2c, ffn_w_up, ffn_w_gate, ffn_conv_w, ffn_conv_b, ffn_w_down)
    return x, xc

def second_inputs(seed: int = 0) -> dict:
    key = jax.random.key(seed)
    ks = jax.random.split(key, 32)
    f32 = jnp.float32

    def nrm(k, shape, scale):
        return jax.random.normal(k, shape, f32) * scale

    d = D_MODEL
    dt0 = jnp.exp(jax.random.uniform(ks[11], (DEPTH, 2, SSM_HEADS), f32, math.log(1e-3), math.log(1e-1)))
    return {
        'x': nrm(ks[0], (BATCH, SEQ, d), 1.0),
        'c': nrm(ks[1], (BATCH, d), 1.0),
        'ctx': nrm(ks[2], (BATCH, CTX_LEN, d), 1.0),
        'c_ctx': nrm(ks[3], (d,), 1.0),
        'w_mod': nrm(ks[4], (DEPTH, d, 6 * d), 0.5 * d ** -0.5),
        'b_mod': nrm(ks[5], (DEPTH, 6 * d), 0.02),
        'norm1': 1.0 + nrm(ks[6], (DEPTH, d), 0.05),
        'norm2': 1.0 + nrm(ks[7], (DEPTH, d), 0.05),
        'w_in': nrm(ks[8], (DEPTH, d, IN_WIDTH), d ** -0.5),
        'a_sink': nrm(ks[9], (DEPTH, A_HEADS), 0.5),
        'ssm_conv_w': nrm(ks[10], (DEPTH, SSM_CONV, SSM_XBC), SSM_CONV ** -0.5),
        'ssm_conv_b': nrm(ks[12], (DEPTH, SSM_XBC), 0.02),
        'ssm_A_log': jnp.log(jax.random.uniform(ks[13], (DEPTH, 2, SSM_HEADS), f32, 1.0, 16.0)),
        'ssm_dt_bias': dt0 + jnp.log(-jnp.expm1(-dt0)),
        'ssm_D': 1.0 + nrm(ks[14], (DEPTH, SSM_HEADS), 0.1),
        'ssm_norm': 1.0 + nrm(ks[15], (DEPTH, SSM_INNER), 0.05),
        'c_q_norm': 1.0 + nrm(ks[16], (DEPTH, HEAD_DIM), 0.05),
        'c_k_norm': 1.0 + nrm(ks[17], (DEPTH, HEAD_DIM), 0.05),
        'w_oa': nrm(ks[18], (DEPTH, A_Q_W, d), A_Q_W ** -0.5),
        'w_ob': nrm(ks[19], (DEPTH, SSM_INNER, d), SSM_INNER ** -0.5),
        'w_oc': nrm(ks[20], (DEPTH, C_Q_W, d), C_Q_W ** -0.5),
        'w_out': nrm(ks[21], (DEPTH, d, d), d ** -0.5),
        'ffn_w_up': nrm(ks[22], (DEPTH, d, D_FF_2), d ** -0.5),
        'ffn_w_gate': nrm(ks[23], (DEPTH, d, D_FF_2), d ** -0.5),
        'ffn_conv_w': nrm(ks[24], (DEPTH, FFN_CONV, D_FF_2), FFN_CONV ** -0.5),
        'ffn_conv_b': nrm(ks[25], (DEPTH, D_FF_2), 0.02),
        'ffn_w_down': nrm(ks[26], (DEPTH, D_FF_2, d), D_FF_2 ** -0.5),
        'final_norm': 1.0 + nrm(ks[27], (d,), 0.05),
    }

def second_block(x, c, ctx, c_ctx, w_mod, b_mod, norm1, norm2, w_in, a_sink, ssm_conv_w, ssm_conv_b,
              ssm_A_log, ssm_dt_bias, ssm_D, ssm_norm, c_q_norm, c_k_norm, w_oa, w_ob, w_oc, w_out,
              ffn_w_up, ffn_w_gate, ffn_conv_w, ffn_conv_b, ffn_w_down, final_norm):
    rows = x.shape[1] // GRID_W
    cos, sin = grid_rope(rows)
    xc = ctx
    sc = jax.nn.silu(c)
    scc = jax.nn.silu(c_ctx)
    for l in range(DEPTH):
        need_ctx_out = l < DEPTH - 1
        n_cmod = 6 * D_MODEL if need_ctx_out else 2 * D_MODEL
        c_mod = sc @ w_mod[l] + b_mod[l]
        cc_mod = scc @ w_mod[l][:, :n_cmod] + b_mod[l][:n_cmod]
        x, xc = hybrid_layer(x, xc, c_mod, cc_mod, cos, sin, w_in[l], norm1[l], norm2[l], a_sink[l],
                             ssm_conv_w[l], ssm_conv_b[l], ssm_A_log[l], ssm_dt_bias[l], ssm_D[l],
                             ssm_norm[l], c_q_norm[l], c_k_norm[l], w_oa[l], w_ob[l], w_oc[l], w_out[l],
                             ffn_w_up[l], ffn_w_gate[l], ffn_conv_w[l], ffn_conv_b[l], ffn_w_down[l],
                             need_ctx_out)
    return rms_norm(x, final_norm)


def setup_inputs(seed=0):
    out = dict(first_inputs(seed))
    for name, value in second_inputs(seed + 1).items():
        if name != "x":
            out[name + "_2"] = value
    return out


def reference(
    x, c, ada_w, ada_b, mix_pre_g, mix_post_g, ffn_pre_g, ffn_post_g, w_in, w_alpha, b_alpha,
    gla_norm_g, s5_lambda_re, s5_lambda_im, s5_log_dt, s5_b_re, s5_b_im, s5_c_re, s5_c_im, s5_d,
    s5_glu_w, s5_glu_b, w_out, router_w, router_b, exp_w_gu, exp_b_gu, exp_w_down, exp_b_down,
    c_2, ctx_2, c_ctx_2, w_mod_2, b_mod_2, norm1_2, norm2_2, w_in_2, a_sink_2, ssm_conv_w_2,
    ssm_conv_b_2, ssm_A_log_2, ssm_dt_bias_2, ssm_D_2, ssm_norm_2, c_q_norm_2, c_k_norm_2,
    w_oa_2, w_ob_2, w_oc_2, w_out_2, ffn_w_up_2, ffn_w_gate_2, ffn_conv_w_2, ffn_conv_b_2,
    ffn_w_down_2, final_norm_2,
):
    x = first_block(
        x, c, ada_w, ada_b, mix_pre_g, mix_post_g, ffn_pre_g, ffn_post_g, w_in, w_alpha,
        b_alpha, gla_norm_g, s5_lambda_re, s5_lambda_im, s5_log_dt, s5_b_re, s5_b_im, s5_c_re,
        s5_c_im, s5_d, s5_glu_w, s5_glu_b, w_out, router_w, router_b, exp_w_gu, exp_b_gu,
        exp_w_down, exp_b_down,
    )
    return second_block(
        x, c_2, ctx_2, c_ctx_2, w_mod_2, b_mod_2, norm1_2, norm2_2, w_in_2, a_sink_2,
        ssm_conv_w_2, ssm_conv_b_2, ssm_A_log_2, ssm_dt_bias_2, ssm_D_2, ssm_norm_2, c_q_norm_2,
        c_k_norm_2, w_oa_2, w_ob_2, w_oc_2, w_out_2, ffn_w_up_2, ffn_w_gate_2, ffn_conv_w_2,
        ffn_conv_b_2, ffn_w_down_2, final_norm_2,
    )


_drawn_inputs = setup_inputs


def setup_inputs(seed=0):
    import zlib

    import numpy as np

    out = dict(_drawn_inputs(seed))
    spreads = {}
    factors = {'ffn_post_g': 3.291,
     's5_lambda_re': 8.0,
     's5_glu_b': 7.341,
     'exp_b_gu': 8.0,
     'exp_b_down': 8.0,
     'ctx_2': 5.052,
     'b_mod_2': 2.922,
     'norm1_2': 5.361,
     'norm2_2': 4.141,
     'a_sink_2': 8.0,
     'ssm_conv_b_2': 8.0,
     'ssm_D_2': 8.0,
     'ssm_norm_2': 8.0,
     'c_q_norm_2': 8.0,
     'c_k_norm_2': 8.0,
     'ffn_conv_b_2': 8.0}
    for name, (base, spread) in spreads.items():
        noise = np.random.default_rng([zlib.crc32(name.encode()), seed]).standard_normal(out[name].shape)
        drawn = base * np.exp(spread * noise) if base else spread * noise
        out[name] = jnp.asarray(drawn.astype(out[name].dtype))
    for name, factor in factors.items():
        out[name] = (out[name] * factor).astype(out[name].dtype)
    return out
```

```python
from contextlib import ExitStack

import numpy as np

import concourse.bass as bass
from concourse import mybir

F32 = mybir.dt.float32
I32 = mybir.dt.int32
ALU = mybir.AluOpType
ACT = mybir.ActivationFunctionType
AX_X = mybir.AxisListType.X

P = 128
T = 512
TT = T // P
D = 1024
DT = D // P
EPS = 1e-6

GLA_HEADS, DK, DV, CHUNK = 4, 64, 128, 64
NCHUNK = T // CHUNK
TAU = 16.0
S5_PAIRS = 16
NE, TOPK, DFF = 32, 4, 1024
S = 128
XBLOCKS = T // S
ALPHA, LIMIT = 1.702, 7.0
NEG = -1.0e30

CTX = 256
CT = CTX // P
HD = 64
ATT_HEADS, SSM_HEADS, SSM_P = 8, 16, 64
DFF2 = 2816
FT2 = DFF2 // P

SLOTS = 6
PANEL = DT * 512


class Count:

    def __init__(self):
        self.n, self.turn, self.index = 0, 0, None

    def add(self, k=1):
        self.n += k
        return self.value()

    def value(self, less=0):
        if self.index is None:
            return self.n - less
        return self.index * self.turn + (self.n - less)

    def enter(self, index, turn):
        self.index, self.turn, self.start = index, turn, self.n

    def leave(self, turns):
        assert self.n - self.start == self.turn, (self.n - self.start, self.turn)
        self.n, self.index = self.start + self.turn * turns, None


class Signal:

    def __init__(self, sem):
        self.sem, self.seen = sem, {}

    def count(self, eng):
        return self.seen.setdefault(eng.engine, Count())

    def next(self, eng, k=1):
        return self.count(eng).add(k)


class Order:

    def __init__(self):
        self.count = Count()

    def next(self):
        return self.count.add()


class TurnOrder:

    def __init__(self, j, n):
        self.j, self.n, self.at = j, n, 0

    def next(self):
        self.at += 1
        return self.j * self.n + self.at

    def end(self):
        assert self.at == self.n, (self.at, self.n)


class Banks:

    def __init__(self, banks, full, free):
        self.banks, self.full, self.free = banks, full, free
        self.sent, self.read = Count(), Count()
        self.at_write = self.at_read = 0

    def room(self):
        return self.sent.value(less=-1)

    def fill(self):
        self.sent.add()
        self.at_write += 1
        return self.banks[(self.at_write - 1) % len(self.banks)]

    def next_full(self):
        return self.read.value(less=-1)

    def take(self):
        self.read.add()
        self.at_read += 1
        return self.banks[(self.at_read - 1) % len(self.banks)]

    def all_sent(self):
        return self.sent.value(less=-len(self.banks))

    def own_reads(self):
        return self.read.value(less=-len(self.banks))


class Panels:

    def __init__(self, slots, loaded, used):
        self.slots, self.loaded, self.used = slots, loaded, used
        self.loads = [Count() for _ in slots]
        self.arrivals = [Count() for _ in slots]
        self.at_load = self.at_use = 0

    def load(self, sp, src):
        s = self.at_load % len(self.slots)
        self.at_load += 1
        c = self.loads[s]
        if c.index is not None or c.n > 0:
            sp.wait_ge(self.used[s], c.value())
        c.add()
        rows, cols = src.shape
        k = rows // P
        dst = self.slots[s][:, 0:k * cols].rearrange("p (k c) -> p k c", k=k)
        sp.dma_start(dst, src.rearrange("(k p) c -> p k c", p=P)).then_inc(self.loaded[s], 16)

    def use(self, k, cols):
        s = self.at_use % len(self.slots)
        self.at_use += 1
        return s, self.slots[s][:, 0:k * cols].rearrange("p (k c) -> p k c", k=k)

    def arrived(self, s):
        return self.arrivals[s].add(16)


class Matmuls:

    def __init__(self, pe):
        self.pe, self.owed = pe, None

    def __call__(self, out, lhsT, rhs, start=True, stop=True):
        if stop:
            self.settle()
        ins = self.pe.matmul(out, lhsT, rhs, start=start, stop=stop)
        if self.owed is not None:
            ins.then_inc(self.owed, 1)
            self.owed = None
        return ins

    def transpose(self, out, in_, ident):
        self.settle()
        return self.pe.transpose(out, in_, ident)

    def done(self, sem):
        self.settle()
        self.owed = sem

    def settle(self):
        if self.owed is not None:
            self.pe.drain().then_inc(self.owed, 1)
            self.owed = None


def constants():
    a, b = np.arange(P)[:, None], np.arange(P)[None, :]
    parts = {}
    parts["ident"] = a == b
    parts["ones"] = np.ones((P, P))
    parts["upper"] = a <= b
    parts["lower"] = a >= b
    parts["gla_mask"] = (a <= b) & (a // CHUNK == b // CHUNK)
    parts["rotate"] = np.where((a == b + 1) & (b % 2 == 0), -1.0, 0.0) + ((a == b - 1) & (b % 2 == 1))
    parts["swap"] = a == (b + HD) % P
    parts["head_sum"] = a // HD == b // HD
    parts["prev_mask"] = np.where(a <= b, 0.0, NEG)
    parts["next_mask"] = np.where(b <= a, 0.0, NEG)
    parts["chunk_keep"] = np.broadcast_to((np.arange(T) % CHUNK != 0)[None, :], (P, T))
    parts["iota"] = np.broadcast_to(b, (P, P))
    parts["block_start"] = np.broadcast_to(S * np.arange(XBLOCKS)[None, :], (P, XBLOCKS))
    rows = T // 64
    inv = 10000.0 ** (-np.arange(HD // 4, dtype=np.float32) / (HD // 4))
    t_row = np.repeat(np.arange(rows), 64).astype(np.float32)
    t_col = np.tile(np.arange(64), rows).astype(np.float32)
    ang = np.concatenate([t_row[:, None] * inv, t_col[:, None] * inv], axis=-1).astype(np.float32)
    per_feature = np.tile(np.repeat(ang.T, 2, axis=0), (2, 1))
    rope = np.concatenate([np.cos(per_feature), np.sin(per_feature)], axis=1).astype(np.float32)
    where, at = {}, 0
    for name, v in parts.items():
        where[name] = (at, v.shape[1])
        at += v.shape[1]
    table = np.concatenate([np.asarray(v, np.float32) for v in parts.values()], axis=1)
    return np.ascontiguousarray(table), where, np.ascontiguousarray(rope)


VECTOR_TILES = [
    [("ada_b", 48), ("b_mod_2", 48), ("c", 8), ("c_2", 8), ("c_ctx_2", 8)],
    [("mix_pre_g", 8), ("mix_post_g", 8), ("ffn_pre_g", 8), ("ffn_post_g", 8), ("norm1_2", 8),
     ("norm2_2", 8), ("ssm_norm_2", 8), ("final_norm_2", 8), ("ssm_conv_w_2", 36), ("ssm_conv_b_2", 12), ("s5_d", 4)],
    [("ffn_conv_w_2", 66), ("ffn_conv_b_2", 22), ("s5_glu_b", 4), ("b_alpha", 2), ("gla_norm_g", 1),
     ("s5_lambda_re", 16), ("s5_lambda_im", 16)],
]
QK_NORMS = ["c_q_norm_2", "c_k_norm_2"]


def build(nc, a, table, where, out):
    ctx = ExitStack()
    with ctx:
        def sb(name, shape, dt=F32):
            return ctx.enter_context(nc.sbuf_tensor(name, shape, dt))

        def sem(name):
            return ctx.enter_context(nc.semaphore(name))

        def signal(name):
            return Signal(sem(name))

        resid = sb("resid", [P, DT, T])
        hidden = sb("hidden", [P, DT, T])
        slots = [sb(f"panel{i}", [P, PANEL]) for i in range(SLOTS)]
        const = sb("const", [P, table.shape[1]])
        cols = sb("cols", [P, 3, P])
        mods = sb("mods", [P, 48, 1])
        mods2 = sb("mods2", [P, 48, 2])
        small = sb("small", [P, 96])
        SCRATCH = 16384
        s5c = sb("s5_columns", [P, 32, S5_PAIRS])
        s5_dd = sb("s5_d_diagonals", [P, 4, P])
        eps_col = sb("eps_col", [P, 1])
        scratch = sb("scratch", [P, SCRATCH])

        def part(at, *shape):
            n = int(np.prod(shape))
            assert at + n <= SCRATCH, (at, shape)
            v = scratch[:, at:at + n]
            if len(shape) == 2:
                v = v.rearrange("p (a b) -> p a b", b=shape[1])
            if len(shape) == 3:
                v = v.rearrange("p (a b c) -> p a b c", b=shape[1], c=shape[2])
            return v

        def con(name, width=None):
            at, n = where[name]
            return const[:, at:at + (width or n)]

        column_at = {}
        for tile_no, rows in enumerate(VECTOR_TILES):
            at = 0
            for name, n in rows:
                column_at[name] = (tile_no, at, n)
                at += n

        def col(name, first=0, n=None):
            tile_no, at, k = column_at[name]
            n = k - first if n is None else n
            return cols[:, tile_no, at + first:at + first + n]

        ident = con("ident")
        ones = con("ones")

        psum_all = ctx.enter_context(nc.psum_tensor("psum_all", [P, 8, 512], F32))
        psum = [psum_all[:, i, :] for i in range(8)]
        to_act = Banks(psum[0:4], sem("act_banks_full"), sem("act_banks_free"))
        to_dve = Banks(psum[4:8], sem("dve_banks_full"), sem("dve_banks_free"))
        panels = Panels(slots, [sem(f"panel{i}_loaded") for i in range(SLOTS)],
                        [sem(f"panel{i}_used") for i in range(SLOTS)])

        act_done = sem("act_done")
        dve_done = sem("dve_done")
        pool_done = sem("pool_done")
        x_loaded = signal("x_loaded")
        const_loaded = signal("const_loaded")
        rows_loaded = signal("rows_loaded")
        s5_loaded = signal("s5_loaded")
        gla_loaded = signal("gla_loaded")
        small_loaded = signal("small_loaded")
        cols_ready = signal("cols_ready")
        silu_ready = signal("silu_ready")
        mods_ready = signal("mods_ready")
        sq_ready = signal("sq_ready")
        std_ready = signal("std_ready")
        scale_ready = signal("scale_ready")
        scaled = signal("scaled")
        normed = signal("normed")
        resid_ready = signal("resid_ready")
        alr_ready = signal("alr_ready")
        gla_act = signal("gla_act")
        gla_dve = signal("gla_dve")
        kte_ready = signal("kte_ready")
        state_ready = signal("state_ready")
        probs_ready = signal("probs_ready")
        o_ready = signal("o_ready")
        osq_ready = signal("osq_ready")
        ostd_ready = signal("ostd_ready")
        gla_out = signal("gla_out")
        s5_cols = signal("s5_cols")
        s5_dve = signal("s5_dve")
        s5_blocks = signal("s5_blocks")
        s5_table = signal("s5_table")
        s5_tab_ready = signal("s5_tab_ready")
        s5_table_used = signal("s5_table_used")
        s5_x = signal("s5_x")
        s5_y = signal("s5_y")
        s5_gelu = signal("s5_gelu")
        s5_gate = signal("s5_gate")
        s5_out = signal("s5_out")
        pe_mark = signal("pe_mark")


        def act_norm(act, step, src, sq, std, n, kt, dim, shifts=None, dst=None):
            act.activation(sq, src, ACT.Square).then_inc(act_done, 1)
            act.wait_ge(act_done, step.next())
            act.sem_inc(sq_ready.sem, 1)
            act.wait_ge(to_act.full, to_act.next_full())
            bank = to_act.take()
            act.activation(std, bank[:, 0:n], ACT.Sqrt, scale=1.0 / dim, bias=eps_col[:, 0:1]).then_inc(to_act.free, 1)
            act.wait_ge(to_act.free, to_act.own_reads())
            act.sem_inc(std_ready.sem, 1)
            if shifts is not None:
                for k in range(kt):
                    act.wait_ge(scaled.sem, scaled.next(act))
                    act.activation(dst[:, k, :], dst[:, k, :], ACT.Identity, bias=shifts[k]).then_inc(normed.sem, 1)

        def pe_norm(pe, mm, sq, n, kt):
            pe.wait_ge(sq_ready.sem, sq_ready.next(pe))
            pe.wait_ge(to_act.free, to_act.room())
            bank = to_act.fill()
            for k in range(kt):
                ins = mm(bank[:, 0:n], ones, sq[:, k, :], k == 0, k == kt - 1)
                if k == kt - 1:
                    ins.then_inc(to_act.full, 1)

        def dve_norm(dve, step, src, dst, std, kt, factors):
            dve.wait_ge(std_ready.sem, std_ready.next(dve))
            dve.reciprocal(std, std).then_inc(dve_done, 1)
            dve.wait_ge(dve_done, step.next())
            for k in range(kt):
                dve.scalar_tensor_tensor(dst[:, k, :], src[:, k, :], factors[:, k:k + 1], std,
                                         ALU.mult, ALU.mult).then_inc(scaled.sem, 1)

        def pe_linear(pe, mm, banks, x, n, k_tiles, width, col_tiles=None):
            s, w = panels.use(k_tiles, width)
            pe.wait_ge(panels.loaded[s], panels.arrived(s))
            for m in range(-(-width // P)):
                pe.wait_ge(banks.free, banks.room())
                bank = banks.fill()
                c = min(P, width - m * P)
                for k in range(k_tiles):
                    ins = mm(bank[0:c, 0:n], w[:, k, m * P:m * P + c], x[:, k, 0:n], k == 0, k == k_tiles - 1)
                    if k == k_tiles - 1:
                        ins.then_inc(banks.full, 1)
            mm.done(panels.used[s])

        def pe_linear_tokens(pe, mm, banks, x, tok_tiles, k_tiles, width):
            s, w = panels.use(k_tiles, width)
            pe.wait_ge(panels.loaded[s], panels.arrived(s))
            for t in range(tok_tiles):
                pe.wait_ge(banks.free, banks.room())
                bank = banks.fill()
                for k in range(k_tiles):
                    ins = mm(bank[:, 0:width], x[:, k, t * P:(t + 1) * P], w[:, k, :], k == 0, k == k_tiles - 1)
                    if k == k_tiles - 1:
                        ins.then_inc(banks.full, 1)
            mm.done(panels.used[s])

        def pe_mods(pe, mm, vectors, n):
            for _ in range(6 * D // 512):
                s, w = panels.use(DT, 512)
                pe.wait_ge(panels.loaded[s], panels.arrived(s))
                pe.wait_ge(to_dve.free, to_dve.room())
                bank = to_dve.fill()
                for m in range(4):
                    for k in range(DT):
                        last = m == 3 and k == DT - 1
                        ins = mm(bank[:, m * n:(m + 1) * n], w[:, k, m * P:(m + 1) * P],
                                 vectors[:, k, :], k == 0, k == DT - 1)
                        if last:
                            ins.then_inc(to_dve.full, 1)
                mm.done(panels.used[s])

        def dve_mods(dve, dst, bias, n):
            for p in range(6 * D // 512):
                dve.wait_ge(to_dve.full, to_dve.next_full())
                bank = to_dve.take()
                dve.tensor_tensor(dst[:, 4 * p:4 * p + 4, :],
                                  bank[:, 0:4 * n].rearrange("p (m n) -> p m n", n=n),
                                  bias[:, 4 * p:4 * p + 4].rearrange("p (m n) -> p m n", n=1).broadcast_to([P, 4, n]),
                                  ALU.add).then_inc(to_dve.free, 1)
            dve.wait_ge(to_dve.free, to_dve.own_reads())

        x_tok = hidden[:, :, :].rearrange("p a b -> p (a b)").rearrange("p (t d) -> p t d", d=D)
        rows = part(0, 3, P)
        w_alpha = sb("w_alpha", [16, 256])

        def sp_first_loads(sp):
            ada = a["ada_w"][0]
            for p in range(12):
                panels.load(sp, ada[:, p * 512:(p + 1) * 512])
            w = a["w_in"][0]
            for c0, c1 in IN_PANELS:
                panels.load(sp, w[:, c0:c1])
            panels.load(sp, a["s5_glu_w"][0])
            for p in range(2):
                panels.load(sp, a["w_out"][0][:, p * 512:(p + 1) * 512])
            for p in range(12):
                panels.load(sp, a["w_mod_2"][0][:, p * 512:(p + 1) * 512])

        IN_PANELS = [(1536, 1552), (0, 512), (512, 1024), (1024, 1536), (1552, 2064)]

        def act_first_loads(act):
            act.dma_start(const[:, :], a["const"]).then_inc(const_loaded.sem, 16)
            act.dma_start(x_tok, a["x"][0].rearrange("(t p) d -> p t d", p=P)).then_inc(x_loaded.sem, 16)
            for tile_no, group in enumerate(VECTOR_TILES):
                at = 0
                for name, n in group:
                    act.dma_start(rows[at:at + n, tile_no, :], flat(name).rearrange("(r c) -> r c", c=P))\
                       .then_inc(rows_loaded.sem, 16)
                    at += n
            act.dma_start(w_alpha[:, :], a["w_alpha"][0]).then_inc(gla_loaded.sem, 16)

        N_ROWS = sum(len(g) for g in VECTOR_TILES)

        def flat(name):
            v = a[name]
            if len(v.shape) == 1:
                return v
            names = " ".join(f"d{i}" for i in range(len(v.shape)))
            return v.rearrange(f"{names} -> ({names})")

        silus = sb("silus", [P, 24])
        c_first = silus[:, 0:8].rearrange("p (k n) -> p k n", n=1)
        c_second = silus[:, 8:24].rearrange("p (n k) -> p k n", n=2)

        def pe_turn_inputs(pe, mm):
            pe.wait_ge(const_loaded.sem, const_loaded.next(pe, 16))
            pe.wait_ge(rows_loaded.sem, rows_loaded.next(pe, 16 * N_ROWS))
            pe.wait_ge(to_dve.free, to_dve.room())
            bank = to_dve.fill()
            for i, group in enumerate(VECTOR_TILES):
                n = sum(r for _, r in group)
                ins = mm.transpose(bank[:, i * P:i * P + n], rows[0:n, i, :], ident[0:n, 0:n])
                if i == 2:
                    ins.then_inc(to_dve.full, 1)
            pe.wait_ge(x_loaded.sem, x_loaded.next(pe, 16))
            for m in range(DT):
                pe.wait_ge(to_dve.free, to_dve.room())
                bank = to_dve.fill()
                for t in range(TT):
                    ins = mm.transpose(bank[:, t * P:(t + 1) * P], x_tok[:, t, m * P:(m + 1) * P], ident)
                    if t == TT - 1:
                        ins.then_inc(to_dve.full, 1)

        def dve_turn_inputs(dve, step):
            dve.memset(eps_col[:, :], EPS).then_inc(dve_done, 1)
            dve.wait_ge(dve_done, step.next())
            dve.wait_ge(to_dve.full, to_dve.next_full())
            bank = to_dve.take()
            for i, group in enumerate(VECTOR_TILES):
                n = sum(r for _, r in group)
                c = dve.tensor_copy(cols[:, i, 0:n], bank[:, i * P:i * P + n])
                if i < 2:
                    c.then_inc(dve_done, 1)
                    dve.wait_ge(dve_done, step.next())
                else:
                    c.then_inc(to_dve.free, 1)
            dve.wait_ge(to_dve.free, to_dve.own_reads())
            dve.sem_inc(cols_ready.sem, 1)
            for m in range(DT):
                dve.wait_ge(to_dve.full, to_dve.next_full())
                bank = to_dve.take()
                dve.tensor_copy(resid[:, m, :], bank[:, :]).then_inc(to_dve.free, 1)
            dve.wait_ge(to_dve.free, to_dve.own_reads())
            dve.sem_inc(resid_ready.sem, 1)

        def act_silus(act, step):
            act.wait_ge(cols_ready.sem, cols_ready.next(act))
            act.activation(silus[:, 0:24], cols[:, 0, 96:120], ACT.Silu).then_inc(act_done, 1)
            act.wait_ge(act_done, step.next())
            act.sem_inc(silu_ready.sem, 1)

        A1, G1, A2, G2 = (small[:, i * 8:(i + 1) * 8] for i in range(4))

        def dve_first_factors(dve, step):
            dve_mods(dve, mods, col("ada_b"), 1)
            for i, (factor, gain, m) in enumerate([(A1, "mix_pre_g", 8), (A2, "ffn_pre_g", 32)]):
                dve.scalar_tensor_tensor(factor, mods[:, m:m + 8, 0], 1.0, col(gain), ALU.add, ALU.mult)\
                    .then_inc(dve_done, 1)
                dve.wait_ge(dve_done, step.next())
            for factor, gain, m in [(G1, "mix_post_g", 16), (G2, "ffn_post_g", 40)]:
                dve.tensor_tensor(factor, mods[:, m:m + 8, 0], col(gain), ALU.mult).then_inc(dve_done, 1)
                dve.wait_ge(dve_done, step.next())
            dve.sem_inc(mods_ready.sem, 1)

        n_sq, n_std = part(0, DT, T), part(4096, T)
        q, kk, v_tok = part(0, 2, T), part(1024, 2, T), part(2048, TT, 512)
        og, u_t, alr = part(4096, 4, T), part(6144, 4, T), part(8192, T)

        def act_project(act, step):
            for m in range(4):
                act.wait_ge(to_act.full, to_act.next_full())
                bank = to_act.take()
                act.activation((q if m < 2 else kk)[:, m % 2, :], bank[:, :], ACT.Copy).then_inc(to_act.free, 1)
            act.wait_ge(to_act.free, to_act.own_reads())
            act.sem_inc(gla_act.sem, 1)

        def act_project_v(act):
            for m in range(4):
                act.wait_ge(to_act.full, to_act.next_full())
                bank = to_act.take()
                act.activation(v_tok[:, m, :], bank[:, :], ACT.Copy).then_inc(to_act.free, 1)

        def act_project_rest(act, step):
            for m in range(4):
                act.wait_ge(to_act.full, to_act.next_full())
                bank = to_act.take()
                act.activation(og[:, m, :], bank[:, :], ACT.Silu).then_inc(to_act.free, 1)
            for m in range(4):
                act.wait_ge(to_act.full, to_act.next_full())
                bank = to_act.take()
                act.activation(u_t[:, m, :], bank[:, :], ACT.Copy).then_inc(to_act.free, 1)
            act.wait_ge(to_act.free, to_act.own_reads())
            act.sem_inc(gla_act.sem, 1)

        bsum, work, kinv = part(8704, 2, T), part(9728, 2, T), part(10752, 2, T)
        kte, states = part(11776, TT, 256), part(12800, NCHUNK, 2, P)
        probs = [part(14848, TT, P), part(15360, TT, P)]
        o_sb, o_sq = part(15872, T), part(8704, T)
        decays = sb("decays", [P, 2, NCHUNK])
        o_std = alr

        def pe_gla(pe, mm):
            pe.wait_ge(normed.sem, normed.next(pe, DT))
            pe_linear(pe, mm, to_dve, hidden, T, DT, 16)
            pe_linear(pe, mm, to_act, hidden, T, DT, 512)
            pe.wait_ge(gla_loaded.sem, gla_loaded.next(pe, 16))
            pe.wait_ge(alr_ready.sem, alr_ready.next(pe))
            for m in range(2):
                pe.wait_ge(to_dve.free, to_dve.room())
                bank = to_dve.fill()
                mm(bank[:, :], w_alpha[:, m * P:(m + 1) * P], alr[0:16, :]).then_inc(to_dve.full, 1)
            pe_linear_tokens(pe, mm, to_act, hidden, TT, DT, 512)
            pe_linear(pe, mm, to_act, hidden, T, DT, 512)
            pe_linear(pe, mm, to_act, hidden, T, DT, 512)
            pe.wait_ge(kte_ready.sem, kte_ready.next(pe))
            for m in range(2):
                pe.wait_ge(to_dve.free, to_dve.room())
                bank = to_dve.fill()
                for t in range(TT):
                    ins = mm.transpose(bank[:, t * P:(t + 1) * P], work[:, m, t * P:(t + 1) * P], ident)
                    if t == TT - 1:
                        ins.then_inc(to_dve.full, 1)
            pe.wait_ge(to_dve.free, to_dve.all_sent())
            pe.wait_ge(to_act.free, to_act.all_sent())
            for n in range(NCHUNK - 1):
                h = slice(64 * (n % 2), 64 * (n % 2) + 64)
                pe.wait_ge(to_dve.free, to_dve.room())
                bank = to_dve.fill()
                for pr in range(2):
                    ins = mm(bank[:, pr * 256:(pr + 1) * 256], kte[h, n // 2, pr * P:(pr + 1) * P],
                             v_tok[h, n // 2, pr * 256:(pr + 1) * 256])
                    if pr:
                        ins.then_inc(to_dve.full, 1)
            for h in range(GLA_HEADS):
                pr, half = h // 2, slice(64 * (h % 2), 64 * (h % 2) + 64)
                pe.wait_ge(to_dve.free, to_dve.room())
                bank = to_dve.fill()
                for t in range(TT):
                    tok = slice(t * P, (t + 1) * P)
                    ins = mm(bank[:, tok], kinv[half, pr, tok], q[half, pr, tok])
                    if t == TT - 1:
                        ins.then_inc(to_dve.full, 1)
            for h in range(GLA_HEADS):
                pr, half = h // 2, slice(64 * (h % 2), 64 * (h % 2) + 64)
                pe.wait_ge(probs_ready.sem, probs_ready.next(pe))
                if h == 0:
                    pe.wait_ge(state_ready.sem, state_ready.next(pe))
                pe.wait_ge(to_act.free, to_act.room())
                bank = to_act.fill()
                for t in range(TT):
                    mm(bank[:, t * P:(t + 1) * P], v_tok[:, t, h * P:(h + 1) * P], probs[h % 2][:, t, :],
                       t == 0, False)
                for n in range(1, NCHUNK):
                    ins = mm(bank[:, n * 64:(n + 1) * 64], states[half, n, pr, :],
                             q[half, pr, n * 64:(n + 1) * 64], False, n == NCHUNK - 1)
                    if n == NCHUNK - 1:
                        ins.then_inc(to_act.full, 1)
                pe.wait_ge(osq_ready.sem, osq_ready.next(pe))
                pe.wait_ge(to_act.free, to_act.room())
                bank = to_act.fill()
                mm(bank[:, :], ones, o_sq).then_inc(to_act.full, 1)

        def dve_gla(dve, step):
            dve.wait_ge(to_dve.full, to_dve.next_full())
            bank = to_dve.take()
            dve.tensor_copy(alr[0:16, :], bank[0:16, :]).then_inc(to_dve.free, 1)
            dve.wait_ge(to_dve.free, to_dve.own_reads())
            dve.sem_inc(alr_ready.sem, 1)
            for m in range(2):
                dve.wait_ge(to_dve.full, to_dve.next_full())
                bank = to_dve.take()
                dve.tensor_scalar(bsum[:, m, :], bank[:, :], col("b_alpha", m, 1), None, ALU.add)\
                   .then_inc(to_dve.free, 1)
            dve.wait_ge(to_dve.free, to_dve.own_reads())
            dve.sem_inc(gla_dve.sem, 1)
            dve.wait_ge(gla_act.sem, gla_act.next(dve, 2))
            for m in range(2):
                dve.scalar_tensor_tensor(bsum[:, m, :], bsum[:, m, :], 0.0, work[:, m, :], ALU.min, ALU.subtract)\
                    .then_inc(dve_done, 1)
                dve.wait_ge(dve_done, step.next())
                dve.tensor_tensor_scan(kinv[:, m, :], con("chunk_keep"), bsum[:, m, :], 0.0, ALU.mult, ALU.add)\
                    .then_inc(dve_done, 1)
                dve.wait_ge(dve_done, step.next())
            dve.tensor_copy(bsum, kinv).then_inc(dve_done, 1)
            dve.wait_ge(dve_done, step.next())
            c = bsum.rearrange("p m (n c) -> p (m n) c", c=CHUNK)
            dve.tensor_tensor(work.rearrange("p m (n c) -> p (m n) c", c=CHUNK),
                              c[:, :, CHUNK - 1:CHUNK].broadcast_to([P, 2 * NCHUNK, CHUNK]), c, ALU.subtract)\
                .then_inc(dve_done, 1)
            dve.wait_ge(dve_done, step.next())
            dve.sem_inc(gla_dve.sem, 1)
            dve.wait_ge(gla_act.sem, gla_act.next(dve))
            dve.tensor_copy(decays.rearrange("p m n -> p (m n)"), c[:, :, CHUNK - 1]).then_inc(dve_done, 1)
            dve.wait_ge(dve_done, step.next())
            dve.scalar_tensor_tensor(q, q, DK ** -0.5, bsum, ALU.mult, ALU.mult).then_inc(dve_done, 1)
            dve.wait_ge(dve_done, step.next())
            dve.tensor_tensor(kinv, kk, kinv, ALU.mult).then_inc(dve_done, 1)
            dve.wait_ge(dve_done, step.next())
            dve.tensor_tensor(work, kk, work, ALU.mult).then_inc(dve_done, 1)
            dve.wait_ge(dve_done, step.next())
            dve.sem_inc(kte_ready.sem, 1)
            for m in range(2):
                dve.wait_ge(to_dve.full, to_dve.next_full())
                bank = to_dve.take()
                dve.tensor_copy(kte[:, :, m * P:(m + 1) * P], bank[:, :].rearrange("p (t c) -> p t c", c=P))\
                   .then_inc(to_dve.free, 1)
            dve.memset(states[:, 0, :, :], 0.0).then_inc(dve_done, 1)
            dve.wait_ge(dve_done, step.next())
            for n in range(NCHUNK - 1):
                dve.wait_ge(to_dve.full, to_dve.next_full())
                bank = to_dve.take()
                for pr in range(2):
                    for i in range(2):
                        half = slice(64 * i, 64 * i + 64)
                        ins = dve.scalar_tensor_tensor(states[half, n + 1, pr, :], states[half, n, pr, :],
                                                       decays[half, pr, n:n + 1],
                                                       bank[half, pr * 256 + i * P:pr * 256 + (i + 1) * P],
                                                       ALU.mult, ALU.add)
                        if pr == 1 and i == 1:
                            ins.then_inc(to_dve.free, 1)
                            dve.wait_ge(to_dve.free, to_dve.own_reads())
                        else:
                            ins.then_inc(dve_done, 1)
                            dve.wait_ge(dve_done, step.next())
            dve.sem_inc(state_ready.sem, 1)
            for h in range(GLA_HEADS):
                dve.wait_ge(to_dve.full, to_dve.next_full())
                bank = to_dve.take()
                if h >= 2:
                    dve.wait_ge(o_ready.sem, o_ready.next(dve))
                dve.tensor_tensor(probs[h % 2], bank[:, :].rearrange("p (t c) -> p t c", c=P),
                                  con("gla_mask").rearrange("p (t c) -> p t c", t=1).broadcast_to([P, TT, P]),
                                  ALU.mult).then_inc(to_dve.free, 1)
                dve.wait_ge(to_dve.free, to_dve.own_reads())
                dve.sem_inc(probs_ready.sem, 1)
                if h >= 1:
                    dve_gla_out(dve, step, h - 1)
            dve_gla_out(dve, step, GLA_HEADS - 1)

        def dve_gla_out(dve, step, h):
            dve.wait_ge(ostd_ready.sem, ostd_ready.next(dve))
            dve.reciprocal(o_std, o_std).then_inc(dve_done, 1)
            dve.wait_ge(dve_done, step.next())
            dve.scalar_tensor_tensor(o_sb, o_sb, col("gla_norm_g"), o_std, ALU.mult, ALU.mult).then_inc(dve_done, 1)
            dve.wait_ge(dve_done, step.next())
            if h == 0:
                dve.wait_ge(gla_act.sem, gla_act.next(dve))
            dve.tensor_tensor(hidden[:, h, :], o_sb, og[:, h, :], ALU.mult).then_inc(dve_done, 1)
            dve.wait_ge(dve_done, step.next())
            dve.sem_inc(gla_out.sem, 1)

        def act_gla(act, step):
            act_project(act, step)
            act.wait_ge(gla_dve.sem, gla_dve.next(act))
            act.activation(work, bsum, ACT.Abs).then_inc(act_done, 1)
            act.wait_ge(act_done, step.next())
            act.activation(work, work, ACT.Exp, scale=-1.0).then_inc(act_done, 1)
            act.wait_ge(act_done, step.next())
            act.activation(work, work, ACT.Ln, bias=1.0).then_inc(act_done, 1)
            act.wait_ge(act_done, step.next())
            act.sem_inc(gla_act.sem, 1)
            act_project_v(act)
            act.wait_ge(gla_dve.sem, gla_dve.next(act))
            act.activation(kinv, bsum, ACT.Exp, scale=-1.0 / TAU).then_inc(act_done, 1)
            act.wait_ge(act_done, step.next())
            act.activation(bsum, bsum, ACT.Exp, scale=1.0 / TAU).then_inc(act_done, 1)
            act.wait_ge(act_done, step.next())
            act.activation(work, work, ACT.Exp, scale=1.0 / TAU).then_inc(act_done, 1)
            act.wait_ge(act_done, step.next())
            act.sem_inc(gla_act.sem, 1)
            act_project_rest(act, step)
            for h in range(GLA_HEADS):
                act.wait_ge(to_act.full, to_act.next_full())
                bank = to_act.take()
                if h >= 1:
                    act.wait_ge(gla_out.sem, gla_out.next(act))
                act.activation(o_sq, bank[:, :], ACT.Square).then_inc(act_done, 1)
                act.wait_ge(act_done, step.next())
                act.activation(o_sb, bank[:, :], ACT.Copy).then_inc(to_act.free, 1)
                act.wait_ge(to_act.free, to_act.own_reads())
                act.sem_inc(osq_ready.sem, 1)
                act.sem_inc(o_ready.sem, 1)
                act.wait_ge(to_act.full, to_act.next_full())
                bank = to_act.take()
                act.activation(o_std, bank[:, :], ACT.Sqrt, scale=1.0 / DV, bias=eps_col[:, 0:1]).then_inc(to_act.free, 1)
                act.wait_ge(to_act.free, to_act.own_reads())
                act.sem_inc(ostd_ready.sem, 1)

        S5_DT, S5_MAG, S5_TH = 0, 1, 2
        S5_C, S5_S, S5_T = 4, 13, 22
        b_pad = [part(i * 2048, S5_PAIRS, P) for i in range(2)]
        b_nat = [part(4096 + i * 256, S5_PAIRS, 16) for i in range(2)]
        c_nat = [part(4608 + i * 512, 4, P) for i in range(2)]
        b_bar = [part(5632 + i * 256, S5_PAIRS, 16) for i in range(2)]
        s5_b = [part(8192 + i * 2048, S5_PAIRS, P) for i in range(2)]
        s5_c = [part(12288 + i * 2048, S5_PAIRS, P) for i in range(2)]
        s5_tab = [[part((2 * b + i) * 512, T) for i in range(2)] for b in range(2)]
        w1, w2, z_re, z_im = (part(2048 + i * 512, T) for i in range(4))
        x_out = [[part(4096 + (2 * b + i) * 512, T) for i in range(2)] for b in range(2)]
        gate_tmp = part(0, 4, T)
        pool_tmp = hidden[:, 7, :].rearrange("p (a b) -> p a b", a=2)

        def pool_s5_loads(pool):
            pool.wait_ge(gla_out.sem, gla_out.next(pool, GLA_HEADS))
            for half in range(2):
                rows64 = slice(64 * half, 64 * half + 64)
                for i, name in enumerate(("s5_b_re", "s5_b_im")):
                    pool.dma_start(b_nat[i][rows64, :, :],
                                 a[name][0].rearrange("(g two) p h -> two p g h", two=2)[half])\
                      .then_inc(s5_loaded.sem, 16)
                pool.dma_start(s5c[rows64, S5_DT, :],
                             a["s5_log_dt"].rearrange("a (g two) -> two a g", two=2)[half].broadcast_to([64, S5_PAIRS]),
                             allow_slow_non_contiguous=True)\
                  .then_inc(s5_loaded.sem, 16)
                for i, name in enumerate(("s5_c_re", "s5_c_im")):
                    pool.dma_start(c_nat[i][:, :, 64 * half:64 * half + 64],
                                 a[name][0].rearrange("(q g) h p -> (g h) q p", q=4)).then_inc(s5_loaded.sem, 16)

        def act_s5_setup(act, step):
            act.wait_ge(s5_loaded.sem, s5_loaded.next(act, 16 * 10))
            v = lambda i: s5c[:, i, :]
            act.activation(v(S5_DT), v(S5_DT), ACT.Exp).then_inc(act_done, 1)
            act.wait_ge(act_done, step.next())
            act.sem_inc(s5_cols.sem, 1)
            act.wait_ge(s5_dve.sem, s5_dve.next(act))
            act.activation(v(S5_MAG), v(S5_MAG), ACT.Exp).then_inc(act_done, 1)
            act.wait_ge(act_done, step.next())
            act.activation(v(S5_S), v(S5_T), ACT.Sin).then_inc(act_done, 1)
            act.wait_ge(act_done, step.next())
            act.activation(v(S5_C), v(S5_T + 1), ACT.Sin).then_inc(act_done, 1)
            act.wait_ge(act_done, step.next())
            act.sem_inc(s5_cols.sem, 1)
            for i in range(2):
                for q4 in range(4):
                    act.wait_ge(to_act.full, to_act.next_full())
                    bank = to_act.take()
                    act.activation(s5_b[i][:, 4 * q4:4 * q4 + 4, :], bank[:, :].rearrange("p (m c) -> p m c", c=P),
                                   ACT.Copy).then_inc(to_act.free, 1)
            act.wait_ge(to_act.free, to_act.own_reads())
            act.sem_inc(s5_blocks.sem, 1)

        def dve_s5_setup(dve, step):
            v = lambda i: s5c[:, i, :]
            tt = lambda o, x, y, op: dve.tensor_tensor(o, x, y, op)
            ts = lambda o, x, s1, o1, s2=None, o2=None: (
                dve.tensor_scalar(o, x, s1, s2, o1, o2) if o2 is not None else dve.tensor_scalar(o, x, s1, None, o1))
            for i in range(2):
                dve.memset(b_pad[i], 0.0).then_inc(dve_done, 1)
                dve.wait_ge(dve_done, step.next())
                dve.memset(s5_c[i], 0.0).then_inc(dve_done, 1)
                dve.wait_ge(dve_done, step.next())
            for q4 in range(4):
                dve.tensor_scalar(s5_dd[:, q4, :], ident, col("s5_d", q4, 1), None, ALU.mult).then_inc(dve_done, 1)
                dve.wait_ge(dve_done, step.next())
            lr, li = col("s5_lambda_re"), col("s5_lambda_im")
            dve.wait_ge(s5_cols.sem, s5_cols.next(dve))
            tt(v(S5_TH), li, v(S5_DT), ALU.mult).then_inc(dve_done, 1)
            dve.wait_ge(dve_done, step.next())
            tt(v(S5_MAG), lr, v(S5_DT), ALU.mult).then_inc(dve_done, 1)
            dve.wait_ge(dve_done, step.next())
            MAGIC, C1 = 12582912.0, 6.28125
            C2, EDGE = 2 * np.pi - C1, 3.1415925
            for k in range(2):
                r, n = v(S5_T + k), v(S5_T + 2)
                ts(n, v(S5_TH), 1 / (2 * np.pi), ALU.mult, 0.25 * k, ALU.add).then_inc(dve_done, 1)
                dve.wait_ge(dve_done, step.next())
                ts(n, n, MAGIC, ALU.add).then_inc(dve_done, 1)
                dve.wait_ge(dve_done, step.next())
                ts(n, n, MAGIC, ALU.subtract).then_inc(dve_done, 1)
                dve.wait_ge(dve_done, step.next())
                dve.scalar_tensor_tensor(r, n, -C1, v(S5_TH), ALU.mult, ALU.add).then_inc(dve_done, 1)
                dve.wait_ge(dve_done, step.next())
                dve.scalar_tensor_tensor(r, n, -C2, r, ALU.mult, ALU.add).then_inc(dve_done, 1)
                dve.wait_ge(dve_done, step.next())
                ts(r, r, k * np.pi / 2, ALU.add, EDGE, ALU.min).then_inc(dve_done, 1)
                dve.wait_ge(dve_done, step.next())
                ts(r, r, -EDGE, ALU.max).then_inc(dve_done, 1)
                dve.wait_ge(dve_done, step.next())
            dve.sem_inc(s5_dve.sem, 1)
            dve.wait_ge(s5_cols.sem, s5_cols.next(dve))
            t0, t1, t2, t3 = (v(S5_T + i) for i in range(4))
            for level in range(9):
                c, s = v(S5_C + level), v(S5_S + level)
                if level:
                    pc, ps = v(S5_C + level - 1), v(S5_S + level - 1)
                    tt(t0, pc, pc, ALU.mult).then_inc(dve_done, 1)
                    dve.wait_ge(dve_done, step.next())
                    tt(t1, ps, ps, ALU.mult).then_inc(dve_done, 1)
                    dve.wait_ge(dve_done, step.next())
                    tt(c, t0, t1, ALU.subtract).then_inc(dve_done, 1)
                    dve.wait_ge(dve_done, step.next())
                    tt(s, pc, ps, ALU.mult).then_inc(dve_done, 1)
                    dve.wait_ge(dve_done, step.next())
                    ts(s, s, 2.0, ALU.mult).then_inc(dve_done, 1)
                    dve.wait_ge(dve_done, step.next())
                tt(t0, c, c, ALU.mult).then_inc(dve_done, 1)
                dve.wait_ge(dve_done, step.next())
                tt(t1, s, s, ALU.mult).then_inc(dve_done, 1)
                dve.wait_ge(dve_done, step.next())
                tt(t0, t0, t1, ALU.add).then_inc(dve_done, 1)
                dve.wait_ge(dve_done, step.next())
                ts(t0, t0, -0.5, ALU.mult, 1.5, ALU.add).then_inc(dve_done, 1)
                dve.wait_ge(dve_done, step.next())
                tt(c, c, t0, ALU.mult).then_inc(dve_done, 1)
                dve.wait_ge(dve_done, step.next())
                tt(s, s, t0, ALU.mult).then_inc(dve_done, 1)
                dve.wait_ge(dve_done, step.next())
            dve.sem_inc(s5_table.sem, 1)
            are, aim, den = t0, t1, t2
            tt(are, v(S5_MAG), v(S5_C), ALU.mult).then_inc(dve_done, 1)
            dve.wait_ge(dve_done, step.next())
            ts(are, are, -1.0, ALU.add).then_inc(dve_done, 1)
            dve.wait_ge(dve_done, step.next())
            tt(aim, v(S5_MAG), v(S5_S), ALU.mult).then_inc(dve_done, 1)
            dve.wait_ge(dve_done, step.next())
            tt(den, lr, lr, ALU.mult).then_inc(dve_done, 1)
            dve.wait_ge(dve_done, step.next())
            tt(t3, li, li, ALU.mult).then_inc(dve_done, 1)
            dve.wait_ge(dve_done, step.next())
            tt(den, den, t3, ALU.add).then_inc(dve_done, 1)
            dve.wait_ge(dve_done, step.next())
            dve.reciprocal(den, den).then_inc(dve_done, 1)
            dve.wait_ge(dve_done, step.next())
            fre, fim, t6 = v(S5_T + 4), v(S5_T + 5), v(S5_T + 6)
            tt(fre, are, lr, ALU.mult).then_inc(dve_done, 1)
            dve.wait_ge(dve_done, step.next())
            tt(t6, aim, li, ALU.mult).then_inc(dve_done, 1)
            dve.wait_ge(dve_done, step.next())
            tt(fre, fre, t6, ALU.add).then_inc(dve_done, 1)
            dve.wait_ge(dve_done, step.next())
            tt(fre, fre, den, ALU.mult).then_inc(dve_done, 1)
            dve.wait_ge(dve_done, step.next())
            tt(fim, aim, lr, ALU.mult).then_inc(dve_done, 1)
            dve.wait_ge(dve_done, step.next())
            tt(t6, are, li, ALU.mult).then_inc(dve_done, 1)
            dve.wait_ge(dve_done, step.next())
            tt(fim, fim, t6, ALU.subtract).then_inc(dve_done, 1)
            dve.wait_ge(dve_done, step.next())
            tt(fim, fim, den, ALU.mult).then_inc(dve_done, 1)
            dve.wait_ge(dve_done, step.next())
            wide = lambda x: x.rearrange("p (g h) -> p g h", h=1).broadcast_to([P, S5_PAIRS, 16])
            tmp = part(12288 - 256, S5_PAIRS, 16)
            for o, f1, f2, op in ((0, fre, fim, ALU.subtract), (1, fim, fre, ALU.add)):
                tt(b_bar[o], b_nat[0], wide(f1), ALU.mult).then_inc(dve_done, 1)
                dve.wait_ge(dve_done, step.next())
                tt(tmp, b_nat[1], wide(f2), ALU.mult).then_inc(dve_done, 1)
                dve.wait_ge(dve_done, step.next())
                tt(b_bar[o], b_bar[o], tmp, op).then_inc(dve_done, 1)
                dve.wait_ge(dve_done, step.next())
            for i in range(2):
                for m in range(4):
                    for par in range(2):
                        half, c0 = slice(64 * par, 64 * par + 64), 32 * m + 16 * par
                        dve.tensor_copy(b_pad[i][half, m::4, c0:c0 + 16], b_bar[i][half, m::4, :])\
                            .then_inc(dve_done, 1)
                        dve.wait_ge(dve_done, step.next())
            dve.sem_inc(s5_dve.sem, 1)
            for i in range(2):
                dve.wait_ge(to_dve.full, to_dve.next_full())
                bank = to_dve.take()
                b4 = bank[:, :].rearrange("p (q c) -> p q c", c=P)
                for m in range(4):
                    for par in range(2):
                        half, c0 = slice(64 * par, 64 * par + 64), 32 * m + 16 * par
                        ins = dve.tensor_scalar(s5_c[i][half, m::4, c0:c0 + 16], b4[half, :, c0:c0 + 16],
                                                -1.0 if i else 1.0, None, ALU.mult)
                        if m == 3 and par == 1:
                            ins.then_inc(to_dve.free, 1)
                        else:
                            ins.then_inc(dve_done, 1)
                            dve.wait_ge(dve_done, step.next())
            dve.wait_ge(to_dve.free, to_dve.own_reads())
            dve.sem_inc(s5_blocks.sem, 1)

        def pe_s5(pe, mm):
            pe.wait_ge(s5_loaded.sem, s5_loaded.next(pe, 16 * 10))
            for i in range(2):
                pe.wait_ge(to_dve.free, to_dve.room())
                bank = to_dve.fill()
                for q4 in range(4):
                    ins = mm.transpose(bank[:, q4 * P:(q4 + 1) * P], c_nat[i][:, q4, :], ident)
                    if q4 == 3:
                        ins.then_inc(to_dve.full, 1)
            pe.wait_ge(s5_dve.sem, s5_dve.next(pe, 2))
            for i in range(2):
                for q4 in range(4):
                    pe.wait_ge(to_act.free, to_act.room())
                    bank = to_act.fill()
                    for m in range(4):
                        ins = mm.transpose(bank[:, m * P:(m + 1) * P], b_pad[i][:, 4 * q4 + m, :], ident)
                        if m == 3:
                            ins.then_inc(to_act.full, 1)
            pe.wait_ge(s5_blocks.sem, s5_blocks.next(pe, 2))
            held = None

            def outputs(p):
                nonlocal held
                q4 = p // 4
                if p % 4 == 0:
                    pe.wait_ge(to_act.free, to_act.room())
                    held = to_act.fill()
                    mm(held[:, :], s5_dd[:, q4, :], u_t[:, q4, :], True, False)
                pe.wait_ge(s5_x.sem, s5_x.next(pe))
                for i in range(2):
                    ins = mm(held[:, :], s5_c[i][:, p, :], x_out[p % 2][i], False, p % 4 == 3 and i == 1)
                    if p % 4 == 3 and i == 1:
                        ins.then_inc(to_act.full, 1)
                mm.done(s5_y.sem)

            for p in range(S5_PAIRS):
                for i in range(2):
                    pe.wait_ge(to_dve.free, to_dve.room())
                    bank = to_dve.fill()
                    mm(bank[:, :], s5_b[i][:, p, :], u_t[:, p // 4, :]).then_inc(to_dve.full, 1)
                if p:
                    outputs(p - 1)
            outputs(S5_PAIRS - 1)
            pe.wait_ge(s5_gelu.sem, s5_gelu.next(pe, 4))
            pe_linear(pe, mm, to_act, hidden[:, 4:8, :], T, 4, 512)

        def pool_s5(pool, step):
            pool.wait_ge(s5_table.sem, s5_table.next(pool))
            for p in range(S5_PAIRS):
                c, s = s5_tab[p % 2]
                if p == 0:
                    pool.wait_ge(s5_blocks.sem, s5_blocks.next(pool, 2))
                if p >= 2:
                    pool.wait_ge(s5_table_used.sem, s5_table_used.next(pool))
                pool.memset(c[:, 0:1], 1.0).then_inc(pool_done, 1)
                pool.wait_ge(pool_done, step.next())
                pool.memset(s[:, 0:1], 0.0).then_inc(pool_done, 1)
                pool.wait_ge(pool_done, step.next())
                for level in range(9):
                    n = 1 << level
                    cl, sl = (s5c[:, i + level, p:p + 1].broadcast_to([P, n]) for i in (S5_C, S5_S))
                    t0, t1 = pool_tmp[:, 0, 0:n], pool_tmp[:, 1, 0:n]
                    pool.tensor_tensor(t0, c[:, 0:n], cl, ALU.mult).then_inc(pool_done, 1)
                    pool.wait_ge(pool_done, step.next())
                    pool.tensor_tensor(t1, s[:, 0:n], sl, ALU.mult).then_inc(pool_done, 1)
                    pool.wait_ge(pool_done, step.next())
                    pool.tensor_tensor(c[:, n:2 * n], t0, t1, ALU.subtract).then_inc(pool_done, 1)
                    pool.wait_ge(pool_done, step.next())
                    pool.tensor_tensor(t0, c[:, 0:n], sl, ALU.mult).then_inc(pool_done, 1)
                    pool.wait_ge(pool_done, step.next())
                    pool.tensor_tensor(t1, s[:, 0:n], cl, ALU.mult).then_inc(pool_done, 1)
                    pool.wait_ge(pool_done, step.next())
                    pool.tensor_tensor(s[:, n:2 * n], t0, t1, ALU.add).then_inc(pool_done, 1)
                    pool.wait_ge(pool_done, step.next())
                pool.sem_inc(s5_tab_ready.sem, 1)

        def dve_s5(dve, step):
            tt = lambda o, x, y, op: dve.tensor_tensor(o, x, y, op)
            for p in range(S5_PAIRS):
                c, s = s5_tab[p % 2]
                dve.wait_ge(s5_tab_ready.sem, s5_tab_ready.next(dve))
                mag = s5c[:, S5_MAG, p:p + 1].broadcast_to([P, T])
                dve.wait_ge(to_dve.full, to_dve.next_full())
                b_re = to_dve.take()[:, :]
                dve.wait_ge(to_dve.full, to_dve.next_full())
                b_im = to_dve.take()[:, :]
                tt(w1, b_re, c, ALU.mult).then_inc(dve_done, 1)
                dve.wait_ge(dve_done, step.next())
                tt(w2, b_im, s, ALU.mult).then_inc(dve_done, 1)
                dve.wait_ge(dve_done, step.next())
                tt(w1, w1, w2, ALU.add).then_inc(dve_done, 1)
                dve.wait_ge(dve_done, step.next())
                dve.tensor_tensor_scan(z_re, mag, w1, 0.0, ALU.mult, ALU.add).then_inc(dve_done, 1)
                dve.wait_ge(dve_done, step.next())
                dve.tensor_tensor(w1, b_re, s, ALU.mult).then_inc(to_dve.free, 1)
                dve.tensor_tensor(w2, b_im, c, ALU.mult).then_inc(to_dve.free, 1)
                dve.wait_ge(to_dve.free, to_dve.own_reads())
                tt(w2, w2, w1, ALU.subtract).then_inc(dve_done, 1)
                dve.wait_ge(dve_done, step.next())
                dve.tensor_tensor_scan(z_im, mag, w2, 0.0, ALU.mult, ALU.add).then_inc(dve_done, 1)
                dve.wait_ge(dve_done, step.next())
                x_re, x_im = x_out[p % 2]
                if p >= 2:
                    dve.wait_ge(s5_y.sem, s5_y.next(dve))
                tt(w1, z_re, c, ALU.mult).then_inc(dve_done, 1)
                dve.wait_ge(dve_done, step.next())
                tt(w2, z_im, s, ALU.mult).then_inc(dve_done, 1)
                dve.wait_ge(dve_done, step.next())
                tt(x_re, w1, w2, ALU.subtract).then_inc(dve_done, 1)
                dve.wait_ge(dve_done, step.next())
                tt(w1, z_re, s, ALU.mult).then_inc(dve_done, 1)
                dve.wait_ge(dve_done, step.next())
                tt(w2, z_im, c, ALU.mult).then_inc(dve_done, 1)
                dve.wait_ge(dve_done, step.next())
                tt(x_im, w1, w2, ALU.add).then_inc(dve_done, 1)
                dve.wait_ge(dve_done, step.next())
                dve.sem_inc(s5_x.sem, 1)
                dve.sem_inc(s5_table_used.sem, 1)
            dve.wait_ge(s5_gate.sem, s5_gate.next(dve))
            dve.tensor_tensor(hidden[:, 4:8, :], hidden[:, 4:8, :], gate_tmp, ALU.mult).then_inc(dve_done, 1)
            dve.wait_ge(dve_done, step.next())
            dve.sem_inc(s5_out.sem, 1)

        def act_s5(act, step):
            for q4 in range(4):
                act.wait_ge(to_act.full, to_act.next_full())
                bank = to_act.take()
                act.activation(hidden[:, 4 + q4, :], bank[:, :], ACT.Gelu_apprx_tanh).then_inc(to_act.free, 1)
                act.wait_ge(to_act.free, to_act.own_reads())
                act.sem_inc(s5_gelu.sem, 1)
            for m in range(4):
                act.wait_ge(to_act.full, to_act.next_full())
                bank = to_act.take()
                act.activation(gate_tmp[:, m, :], bank[:, :], ACT.Sigmoid, bias=col("s5_glu_b", m, 1)).then_inc(to_act.free, 1)
            act.wait_ge(to_act.free, to_act.own_reads())
            act.sem_inc(s5_gate.sem, 1)

        mix = part(0, DT, T)
        m_sq, m_std = part(4096, DT, T), part(8192, T)

        def pe_project_out(pe, mm):
            pe.wait_ge(s5_out.sem, s5_out.next(pe))
            pe.wait_ge(gla_out.sem, gla_out.next(pe, GLA_HEADS))
            pe_linear(pe, mm, to_act, hidden, T, DT, 512)
            pe_linear(pe, mm, to_act, hidden, T, DT, 512)

        def act_copy_tiles(act, dst, n_tiles, n=T):
            for m in range(n_tiles):
                act.wait_ge(to_act.full, to_act.next_full())
                bank = to_act.take()
                act.activation(dst[:, m, :], bank[:, 0:n], ACT.Copy).then_inc(to_act.free, 1)
            act.wait_ge(to_act.free, to_act.own_reads())

        def dve_add_normed(dve, step, branch, std, gains):
            dve.wait_ge(std_ready.sem, std_ready.next(dve))
            dve.reciprocal(std, std).then_inc(dve_done, 1)
            dve.wait_ge(dve_done, step.next())
            for k in range(DT):
                dve.scalar_tensor_tensor(branch[:, k, :], branch[:, k, :], gains[:, k:k + 1], std, ALU.mult, ALU.mult)\
                    .then_inc(dve_done, 1)
                dve.wait_ge(dve_done, step.next())
                dve.tensor_tensor(resid[:, k, :], resid[:, k, :], branch[:, k, :], ALU.add).then_inc(dve_done, 1)
                dve.wait_ge(dve_done, step.next())
            dve.sem_inc(resid_ready.sem, 1)
        n2_sq, n2_std = part(0, DT, T), part(4096, T)

        hn_tok = part(0, TT, D)
        xg = part(4096, DT, S)
        gb, ub, sg = part(5120, DT, S), part(6144, DT, S), part(7168, DT, S)
        sel, selg = part(8192, TT, S), part(8704, TT, S)
        selgt = part(9216, T)
        y_sb = part(9728, D)
        bgu = part(10752, NE, 16)
        POS = NE + 1
        posm, gate = part(11264, POS, TT), part(11400, POS, TT)
        bdown = part(12288, D)
        router_w = part(13312, DT, NE)
        router_b = part(13568, NE)
        r_at = [13600]

        def r_part(*shape):
            v = part(r_at[0], *shape)
            r_at[0] += int(np.prod(shape))
            return v

        logits, cur, hot, cand, chosen, expo, im64 = (r_part(TT, NE) for _ in range(7))
        row_max, row_min, top, total = (r_part(TT) for _ in range(4))
        counts_f, extra_n, extra_c, x_e, x_b, x_t = (r_part(NE) for _ in range(6))
        cmp_t = r_part(16, NE)
        gate_t = part(15360 + 256, T)
        assert r_at[0] <= 15616, r_at
        bgu_rows = part(5120, 2 * DFF)
        extra_e = sb("extra_expert", [1, 16], I32)
        extra_b = sb("extra_block", [1, 16], I32)

        router_loaded = signal("router_loaded")
        router_dve = signal("router_dve")
        router_act = signal("router_act")
        router_table = signal("router_table")
        moe_sel = signal("moe_sel")
        moe_selg = signal("moe_selg")
        moe_gm = signal("moe_gm")
        moe_sig = signal("moe_sig")
        moe_act = signal("moe_act")
        moe_start = signal("moe_start")
        moe_done = signal("moe_done")
        moe_a = Banks(psum[0:5], sem("moe_act_full"), sem("moe_act_free"))
        moe_d = Banks(psum[5:8], sem("moe_dve_full"), sem("moe_dve_free"))
        turn = sem("extra_turn")
        extra_w = sem("extra_weights")

        def pool_moe_loads(pool):
            pool.wait_ge(resid_ready.sem, resid_ready.next(pool, 2))
            pool.dma_start(router_w, a["router_w"][0].rearrange("(k p) e -> p k e", p=P)).then_inc(router_loaded.sem, 16)
            pool.dma_start(router_b, a["router_b"].broadcast_to([P, NE])).then_inc(router_loaded.sem, 16)
            pool.dma_start(bdown[0:NE, :], a["exp_b_down"][0]).then_inc(router_loaded.sem, 16)
            pool.dma_start(bgu_rows[0:NE, :], a["exp_b_gu"][0]).then_inc(router_loaded.sem, 16)

        def pe_route(pe, mm):
            pe.wait_ge(router_loaded.sem, router_loaded.next(pe, 64))
            pe.wait_ge(normed.sem, normed.next(pe, DT))
            pe.wait_ge(to_dve.free, to_dve.room())
            bank = to_dve.fill()
            for t in range(TT):
                for k in range(DT):
                    ins = mm(bank[:, t * NE:(t + 1) * NE], hidden[:, k, t * P:(t + 1) * P],
                             router_w[:, k, :], k == 0, k == DT - 1)
                    if t == TT - 1 and k == DT - 1:
                        ins.then_inc(to_dve.full, 1)
            for t in range(TT):
                for g in range(2):
                    pe.wait_ge(to_act.free, to_act.room())
                    bank = to_act.fill()
                    for m in range(4):
                        ins = mm.transpose(bank[:, m * P:(m + 1) * P], hidden[:, 4 * g + m, t * P:(t + 1) * P], ident)
                        if m == 3:
                            ins.then_inc(to_act.full, 1)
            pe.wait_ge(to_act.free, to_act.room())
            bank = to_act.fill()
            for f in range(16):
                ins = mm.transpose(bank[:, f * NE:(f + 1) * NE], bgu_rows[0:NE, f * P:(f + 1) * P], ident[0:NE, 0:NE])
                if f == 15:
                    ins.then_inc(to_act.full, 1)
            pe.wait_ge(router_dve.sem, router_dve.next(pe, 2))
            pe.wait_ge(to_dve.free, to_dve.room())
            bank = to_dve.fill()
            for t in range(TT):
                for s in range(t + 1):
                    mm(bank[:, t * NE:(t + 1) * NE], con("upper") if s == t else ones, chosen[:, s, :], s == 0, s == t)
            for s in range(TT):
                ins = mm(bank[:, P:P + NE], ones, chosen[:, s, :], s == 0, s == TT - 1)
                if s == TT - 1:
                    ins.then_inc(to_dve.full, 1)
            pe.wait_ge(router_dve.sem, router_dve.next(pe))
            pe.wait_ge(to_dve.free, to_dve.room())
            bank = to_dve.fill()
            for t in range(TT):
                ins = mm.transpose(bank[0:NE, t * P:(t + 1) * P], cand[:, t, :], ident)
                if t == TT - 1:
                    ins.then_inc(to_dve.full, 1)
            pe.wait_ge(to_dve.free, to_dve.all_sent())
            pe.wait_ge(to_act.free, to_act.all_sent())
            for m in range(DT):
                pe.wait_ge(to_dve.free, to_dve.room())
                bank = to_dve.fill()
                mm(bank[:, :], bdown[0:NE, m * P:(m + 1) * P], gate_t[0:NE, :]).then_inc(to_dve.full, 1)
            pe.wait_ge(to_dve.free, to_dve.all_sent())

        def act_route(act, step):
            for t in range(TT):
                for g in range(2):
                    act.wait_ge(to_act.full, to_act.next_full())
                    bank = to_act.take()
                    act.activation(hn_tok[:, t, g * 512:(g + 1) * 512], bank[:, :], ACT.Copy).then_inc(to_act.free, 1)
            act.wait_ge(to_act.full, to_act.next_full())
            bank = to_act.take()
            act.activation(bgu.rearrange("p e f -> p f e"), bank[:, :].rearrange("p (f e) -> p f e", e=NE),
                           ACT.Copy).then_inc(to_act.free, 1)
            act.wait_ge(to_act.free, to_act.own_reads())
            act.sem_inc(router_act.sem, 1)
            act.wait_ge(router_dve.sem, router_dve.next(act))
            act.activation(expo, expo, ACT.Exp).then_inc(act_done, 1)
            act.wait_ge(act_done, step.next())
            act.sem_inc(router_act.sem, 1)
            act.sem_inc(moe_a.free, len(moe_a.banks))

        def wide_e(x):
            return x.rearrange("p (t e) -> p t e", e=1).broadcast_to([P, TT, NE])

        def dve_route(dve, step):
            tt = lambda o, x, y, op: dve.tensor_tensor(o, x, y, op)
            ts = lambda o, x, s1, o1: dve.tensor_scalar(o, x, s1, None, o1)
            dve.wait_ge(router_loaded.sem, router_loaded.next(dve, 64))
            iota_e = con("iota", NE).rearrange("p (t e) -> p t e", t=1).broadcast_to([P, TT, NE])
            dve.wait_ge(to_dve.full, to_dve.next_full())
            bank = to_dve.take()
            dve.tensor_tensor(logits, bank[:, 0:P].rearrange("p (t e) -> p t e", e=NE),
                              router_b.rearrange("p (t e) -> p t e", t=1).broadcast_to([P, TT, NE]), ALU.add)\
               .then_inc(to_dve.free, 1)
            dve.wait_ge(to_dve.free, to_dve.own_reads())
            ts(im64, iota_e, -64.0, ALU.add).then_inc(dve_done, 1)
            dve.wait_ge(dve_done, step.next())
            dve.tensor_copy(cur, logits).then_inc(dve_done, 1)
            dve.wait_ge(dve_done, step.next())
            for i in range(TOPK):
                dve.tensor_reduce(row_max, cur, AX_X, ALU.max).then_inc(dve_done, 1)
                dve.wait_ge(dve_done, step.next())
                if i == 0:
                    dve.tensor_copy(top, row_max).then_inc(dve_done, 1)
                    dve.wait_ge(dve_done, step.next())
                    tt(expo, logits, wide_e(top), ALU.subtract).then_inc(dve_done, 1)
                    dve.wait_ge(dve_done, step.next())
                    dve.sem_inc(router_dve.sem, 1)
                tt(hot, cur, wide_e(row_max), ALU.is_equal).then_inc(dve_done, 1)
                dve.wait_ge(dve_done, step.next())
                tt(hot, hot, im64, ALU.mult).then_inc(dve_done, 1)
                dve.wait_ge(dve_done, step.next())
                dve.tensor_reduce(row_min, hot, AX_X, ALU.min).then_inc(dve_done, 1)
                dve.wait_ge(dve_done, step.next())
                tt(hot, im64, wide_e(row_min), ALU.is_equal).then_inc(dve_done, 1)
                dve.wait_ge(dve_done, step.next())
                if i == 0:
                    dve.tensor_copy(chosen, hot).then_inc(dve_done, 1)
                    dve.wait_ge(dve_done, step.next())
                else:
                    tt(chosen, chosen, hot, ALU.add).then_inc(dve_done, 1)
                    dve.wait_ge(dve_done, step.next())
                dve.scalar_tensor_tensor(cur, hot, NEG, cur, ALU.mult, ALU.add).then_inc(dve_done, 1)
                dve.wait_ge(dve_done, step.next())
            dve.sem_inc(router_dve.sem, 1)
            dve.wait_ge(router_act.sem, router_act.next(dve, 2))
            tt(cand, expo, chosen, ALU.mult).then_inc(dve_done, 1)
            dve.wait_ge(dve_done, step.next())
            dve.tensor_reduce(total, cand, AX_X, ALU.add).then_inc(dve_done, 1)
            dve.wait_ge(dve_done, step.next())
            dve.reciprocal(total, total).then_inc(dve_done, 1)
            dve.wait_ge(dve_done, step.next())
            tt(cand, cand, wide_e(total), ALU.mult).then_inc(dve_done, 1)
            dve.wait_ge(dve_done, step.next())
            dve.sem_inc(router_dve.sem, 1)
            dve.tensor_copy(gate[:, 0:NE, :].rearrange("p e t -> p t e"), cand).then_inc(dve_done, 1)
            dve.wait_ge(dve_done, step.next())
            dve.memset(gate[:, NE:POS, :], 0.0).then_inc(dve_done, 1)
            dve.wait_ge(dve_done, step.next())
            dve.wait_ge(to_dve.full, to_dve.next_full())
            bank = to_dve.take()
            tt(hot, bank[:, 0:P].rearrange("p (t e) -> p t e", e=NE), chosen, ALU.mult).then_inc(dve_done, 1)
            dve.wait_ge(dve_done, step.next())
            dve.tensor_copy(counts_f[0:1, :], bank[0:1, P:P + NE]).then_inc(to_dve.free, 1)
            dve.wait_ge(to_dve.free, to_dve.own_reads())
            ts(posm[:, 0:NE, :].rearrange("p e t -> p t e"), hot, -1.0, ALU.add).then_inc(dve_done, 1)
            dve.wait_ge(dve_done, step.next())
            dve.memset(posm[:, NE:POS, :], -1.0).then_inc(dve_done, 1)
            dve.wait_ge(dve_done, step.next())
            dve.wait_ge(to_dve.full, to_dve.next_full())
            bank = to_dve.take()
            dve.tensor_copy(gate_t[0:NE, :], bank[0:NE, :]).then_inc(to_dve.free, 1)
            dve.wait_ge(to_dve.free, to_dve.own_reads())
            for m in range(DT):
                dve.wait_ge(to_dve.full, to_dve.next_full())
                bank = to_dve.take()
                dve.tensor_copy(hidden[:, m, :], bank[:, :]).then_inc(to_dve.free, 1)
            dve.wait_ge(to_dve.free, to_dve.own_reads())
            n1, c1 = extra_n[0:1, :], extra_c[0:1, :]
            ts(n1, counts_f[0:1, :], float(S), ALU.is_gt).then_inc(dve_done, 1)
            dve.wait_ge(dve_done, step.next())
            for b in range(2, XBLOCKS):
                dve.tensor_scalar(x_t[0:1, :], counts_f[0:1, :], float(b * S), None, ALU.is_gt)\
                    .then_inc(dve_done, 1)
                dve.wait_ge(dve_done, step.next())
                tt(n1, n1, x_t[0:1, :], ALU.add).then_inc(dve_done, 1)
                dve.wait_ge(dve_done, step.next())
            dve.tensor_tensor_scan(c1, ones[0:1, 0:NE], n1, 0.0, ALU.mult, ALU.add).then_inc(dve_done, 1)
            dve.wait_ge(dve_done, step.next())
            cj = c1.rearrange("p (j e) -> p j e", j=1).broadcast_to([1, 16, NE])
            jj = con("iota", 16)[0:1, :].rearrange("p (j e) -> p j e", e=1).broadcast_to([1, 16, NE])
            ct = cmp_t[0:1, :, :]
            xe, xb, xt = x_e[0:1, 0:16], x_b[0:1, 0:16], x_t[0:1, 0:16]
            tt(ct, cj, jj, ALU.is_le)\
                .then_inc(dve_done, 1)
            dve.wait_ge(dve_done, step.next())
            dve.tensor_reduce(xe, ct, AX_X, ALU.add).then_inc(dve_done, 1)
            dve.wait_ge(dve_done, step.next())
            tt(ct, ct, n1.rearrange("p (j e) -> p j e", j=1).broadcast_to([1, 16, NE]), ALU.mult)\
                .then_inc(dve_done, 1)
            dve.wait_ge(dve_done, step.next())
            dve.tensor_reduce(xb, ct, AX_X, ALU.add).then_inc(dve_done, 1)
            dve.wait_ge(dve_done, step.next())
            tt(xb, con("iota", 16)[0:1, :], xb, ALU.subtract).then_inc(dve_done, 1)
            dve.wait_ge(dve_done, step.next())
            ts(xb, xb, 1.0, ALU.add).then_inc(dve_done, 1)
            dve.wait_ge(dve_done, step.next())
            ts(xt, xe, float(NE), ALU.is_lt).then_inc(dve_done, 1)
            dve.wait_ge(dve_done, step.next())
            tt(xb, xb, xt, ALU.mult).then_inc(dve_done, 1)
            dve.wait_ge(dve_done, step.next())
            tt(xe, xe, xt, ALU.mult).then_inc(dve_done, 1)
            dve.wait_ge(dve_done, step.next())
            dve.tensor_copy(extra_e[:, :], xe).then_inc(dve_done, 1)
            dve.wait_ge(dve_done, step.next())
            dve.tensor_copy(extra_b[:, :], xb).then_inc(dve_done, 1)
            dve.wait_ge(dve_done, step.next())
            dve.memset(y_sb, 0.0).then_inc(dve_done, 1)
            dve.wait_ge(dve_done, step.next())
            dve.memset(selgt, 0.0).then_inc(dve_done, 1)
            dve.wait_ge(dve_done, step.next())
            dve.sem_inc(moe_d.free, len(moe_d.banks))
            for _ in range(1):
                dve_select(dve, step, 0)
            dve.sem_inc(moe_start.sem, 1)
            dve.sem_inc(moe_sel.sem, 1)

        iota_slots = con("iota").rearrange("p (t s) -> p t s", t=1).broadcast_to([P, TT, S])

        def slots_of(x):
            return x.rearrange("p t -> p t").rearrange("p (t s) -> p t s", s=1).broadcast_to([P, TT, S])

        def expert_column(x, e):
            v = x[:, bass.ds(e, 1), :]
            return v.rearrange("p e t -> p (e t)")

        def dve_select(dve, step, e):
            dve.tensor_tensor(sel, iota_slots, slots_of(expert_column(posm, e)), ALU.is_equal).then_inc(dve_done, 1)
            dve.wait_ge(dve_done, step.next())

        def pe_gather(pe, mm, banks):
            for g in range(2):
                pe.wait_ge(banks.free, banks.room())
                bank = banks.fill()
                for m in range(4):
                    for t in range(TT):
                        last = m == 3 and t == TT - 1
                        ins = mm(bank[:, m * S:(m + 1) * S], hn_tok[:, t, (4 * g + m) * P:(4 * g + m + 1) * P],
                                 sel[:, t, :], t == 0, t == TT - 1)
                        if last:
                            ins.then_inc(banks.full, 1)

        def pe_up(pe, mm, banks, n_panels=4):
            for _ in range(n_panels):
                s, w = panels.use(DT, 512)
                pe.wait_ge(panels.loaded[s], panels.arrived(s))
                pe.wait_ge(banks.free, banks.room())
                bank = banks.fill()
                for f in range(4):
                    for k in range(DT):
                        ins = mm(bank[:, f * S:(f + 1) * S], w[:, k, f * P:(f + 1) * P],
                                 xg[:, k, :], k == 0, k == DT - 1)
                        if f == 3 and k == DT - 1:
                            ins.then_inc(banks.full, 1)
                mm.done(panels.used[s])

        def pe_moe(pe, mm):
            pe.wait_ge(moe_start.sem, moe_start.next(pe))
            pe.wait_ge(moe_sel.sem, moe_sel.next(pe))
            pe_gather(pe, mm, moe_a)
            counts = [moe_a.sent, moe_d.sent, moe_sel.count(pe), moe_selg.count(pe), moe_act.count(pe), *panels.arrivals]
            turns = [5, 12, 1, 1, 1] + [16] * SLOTS
            with pe.Fori(0, NE) as e:
                for c, n in zip(counts, turns):
                    c.enter(e, n)
                pe.wait_ge(moe_a.free, moe_a.all_sent())
                pe_up(pe, mm, moe_d)
                pe.wait_ge(moe_sel.sem, moe_sel.next(pe))
                pe_gather(pe, mm, moe_a)
                for m in range(DT):
                    pe.wait_ge(moe_d.free, moe_d.room())
                    bank = moe_d.fill()
                    mm(bank[:, :], y_sb[:, m * P:(m + 1) * P], selgt).then_inc(moe_d.full, 1)
                pe.wait_ge(moe_selg.sem, moe_selg.next(pe))
                pe.wait_ge(moe_a.free, moe_a.room())
                bank = moe_a.fill()
                for t in range(TT):
                    ins = mm.transpose(bank[:, t * P:(t + 1) * P], selg[:, t, :], ident)
                    if t == TT - 1:
                        ins.then_inc(moe_a.full, 1)
                pe.wait_ge(moe_act.sem, moe_act.next(pe))
                for half in range(2):
                    s, w = panels.use(DT, 512)
                    pe.wait_ge(panels.loaded[s], panels.arrived(s))
                    pe.wait_ge(moe_a.free, moe_a.room())
                    bank = moe_a.fill()
                    for k in range(DT):
                        ins = mm(bank[:, :], ub[:, k, :], w[:, k, :], k == 0, k == DT - 1)
                        if k == DT - 1:
                            ins.then_inc(moe_a.full, 1)
                    mm.done(panels.used[s])
                mm.settle()
                for c in counts:
                    c.leave(NE)
            pe.wait_ge(moe_a.free, moe_a.all_sent())
            for m in range(DT):
                pe.wait_ge(moe_d.free, moe_d.room())
                bank = moe_d.fill()
                mm(bank[:, :], y_sb[:, m * P:(m + 1) * P], selgt).then_inc(moe_d.full, 1)
            pe.wait_ge(moe_d.free, moe_d.all_sent())

        def sp_moe(sp):
            with sp.Fori(0, NE) as e:
                for c in panels.loads:
                    c.enter(e, 1)
                for p in range(4):
                    panels.load(sp, expert_dram(a["exp_w_gu"], e)[:, p * 512:(p + 1) * 512])
                for p in range(2):
                    panels.load(sp, expert_dram(a["exp_w_down"], e)[:, p * 512:(p + 1) * 512])
                for c in panels.loads:
                    c.leave(NE)

        def expert_dram(w, e):
            return w[0, bass.ds(e, 1), :, :].rearrange("e r c -> (e r) c")

        def act_moe(act, step):
            counts = [step.count, moe_a.read, moe_gm.count(act)]
            for g in range(2):
                act.wait_ge(moe_a.full, moe_a.next_full())
                bank = moe_a.take()
                act.activation(xg[:, 4 * g:4 * g + 4, :], bank[:, :].rearrange("p (m s) -> p m s", s=S), ACT.Copy)\
                   .then_inc(moe_a.free, 1)
            with act.Fori(0, NE) as e:
                for c, n in zip(counts, [1, 5, 1]):
                    c.enter(e, n)
                act.wait_ge(moe_gm.sem, moe_gm.next(act))
                act.activation(sg, gb, ACT.Sigmoid, scale=ALPHA).then_inc(act_done, 1)
                act.wait_ge(act_done, step.next())
                act.sem_inc(moe_sig.sem, 1)
                for g in range(2):
                    act.wait_ge(moe_a.full, moe_a.next_full())
                    bank = moe_a.take()
                    act.activation(xg[:, 4 * g:4 * g + 4, :], bank[:, :].rearrange("p (m s) -> p m s", s=S), ACT.Copy)\
                       .then_inc(moe_a.free, 1)
                act.wait_ge(moe_a.full, moe_a.next_full())
                bank = moe_a.take()
                act.activation(selgt, bank[:, :], ACT.Copy).then_inc(moe_a.free, 1)
                for half in range(2):
                    act.wait_ge(moe_a.full, moe_a.next_full())
                    bank = moe_a.take()
                    act.activation(y_sb[:, half * 512:(half + 1) * 512], bank[:, :], ACT.Copy).then_inc(moe_a.free, 1)
                for c in counts:
                    c.leave(NE)
            act.wait_ge(moe_a.free, moe_a.own_reads())

        def bias_of(e, first):
            v = bgu[:, bass.ds(e, 1), first:first + 4].rearrange("p e f -> p (e f)")
            return v.rearrange("p (f s) -> p f s", s=1).broadcast_to([P, 4, S])

        def dve_moe(dve, step):
            counts = [step.count, moe_d.read, moe_sig.count(dve)]
            with dve.Fori(0, NE) as e:
                for c, n in zip(counts, [7, 12, 1]):
                    c.enter(e, n)
                for g in range(2):
                    dve.wait_ge(moe_d.full, moe_d.next_full())
                    bank = moe_d.take()
                    dve.tensor_tensor(gb[:, 4 * g:4 * g + 4, :], bank[:, :].rearrange("p (f s) -> p f s", s=S),
                                      bias_of(e, 4 * g), ALU.add).then_inc(moe_d.free, 1)
                dve.wait_ge(moe_d.free, moe_d.own_reads())
                dve.tensor_scalar(gb, gb, LIMIT, None, ALU.min).then_inc(dve_done, 1)
                dve.wait_ge(dve_done, step.next())
                dve.sem_inc(moe_gm.sem, 1)
                dve_select(dve, step, e + 1)
                dve.sem_inc(moe_sel.sem, 1)
                dve.tensor_tensor(selg, iota_slots, slots_of(expert_column(posm, e)), ALU.is_equal)\
                    .then_inc(dve_done, 1)
                dve.wait_ge(dve_done, step.next())
                dve.tensor_tensor(selg, selg, slots_of(expert_column(gate, e)), ALU.mult).then_inc(dve_done, 1)
                dve.wait_ge(dve_done, step.next())
                dve.sem_inc(moe_selg.sem, 1)
                for g in range(2):
                    dve.wait_ge(moe_d.full, moe_d.next_full())
                    bank = moe_d.take()
                    dve.tensor_tensor(ub[:, 4 * g:4 * g + 4, :], bank[:, :].rearrange("p (f s) -> p f s", s=S),
                                      bias_of(e, 8 + 4 * g), ALU.add).then_inc(moe_d.free, 1)
                dve.wait_ge(moe_d.free, moe_d.own_reads())
                dve.tensor_scalar(ub, ub, LIMIT, -LIMIT, ALU.min, ALU.max).then_inc(dve_done, 1)
                dve.wait_ge(dve_done, step.next())
                dve.scalar_tensor_tensor(ub, ub, 1.0, gb, ALU.add, ALU.mult).then_inc(dve_done, 1)
                dve.wait_ge(dve_done, step.next())
                dve.wait_ge(moe_sig.sem, moe_sig.next(dve))
                dve.tensor_tensor(ub, ub, sg, ALU.mult).then_inc(dve_done, 1)
                dve.wait_ge(dve_done, step.next())
                dve.sem_inc(moe_act.sem, 1)
                dve_give_out(dve, moe_d)
                for c in counts:
                    c.leave(NE)
            dve_give_out(dve, moe_d)
            dve.wait_ge(moe_d.free, moe_d.own_reads())

        def dve_give_out(dve, banks):
            for m in range(DT):
                dve.wait_ge(banks.full, banks.next_full())
                bank = banks.take()
                dve.tensor_tensor(hidden[:, m, :], hidden[:, m, :], bank[:, :], ALU.add).then_inc(banks.free, 1)

        STAGES, LOADS = 11, 16 * SLOTS

        def extra_blocks(eng, taken, skipped=None):
            with eng.Fori(0, 16) as j:
                block_no = eng.value_load(extra_b[0:1, bass.ds(j, 1)], min_val=0, max_val=XBLOCKS - 1)
                with eng.If(block_no > 0):
                    e = eng.value_load(extra_e[0:1, bass.ds(j, 1)], min_val=0, max_val=NE - 1)
                    taken(j, e, block_no)
                if skipped is not None:
                    with eng.Else():
                        skipped(j)
                eng.end_ifs()

        def stage(j, s):
            return j * STAGES + s + 1

        def sp_extra(sp):
            sp.wait_ge(moe_done.sem, moe_done.next(sp, 3))

            def taken(j, e, b):
                sp.wait_ge(turn, stage(j, 0))
                for i in range(SLOTS):
                    w = expert_dram(a["exp_w_gu"] if i < 4 else a["exp_w_down"], e)
                    src = w[:, (i % 4) * 512:(i % 4 + 1) * 512].rearrange("(k p) c -> p k c", p=P)
                    sp.dma_start(slots[i][:, :].rearrange("p (k c) -> p k c", k=DT), src).then_inc(extra_w, 16)

            def skipped(j):
                sp.wait_ge(turn, stage(j, 0))
                sp.sem_inc(extra_w, LOADS)

            extra_blocks(sp, taken, skipped)

        def dve_extra(dve, step):
            dve.sem_inc(moe_done.sem, 1)
            dve.wait_ge(moe_done.sem, moe_done.next(dve, 3))
            dve.sem_inc(turn, 1)

            def taken(j, e, b):
                dve.wait_ge(turn, stage(j, 0))
                pos = total
                chain = TurnOrder(j, 9)
                dve.tensor_scalar(pos, expert_column(posm, e), con("block_start")[:, bass.ds(b, 1)], None, ALU.subtract)\
                    .then_inc(extra_dve, 1)
                dve.wait_ge(extra_dve, chain.next())
                dve.tensor_tensor(sel, iota_slots, slots_of(pos), ALU.is_equal).then_inc(extra_dve, 1)
                dve.wait_ge(extra_dve, chain.next())
                dve.tensor_tensor(selg, sel, slots_of(expert_column(gate, e)), ALU.mult).then_inc(extra_dve, 1)
                dve.wait_ge(extra_dve, chain.next())
                dve.sem_inc(turn, 1)
                dve.wait_ge(turn, stage(j, 4))
                for g in range(2):
                    dve.tensor_tensor(gb[:, 4 * g:4 * g + 4, :], psum[3 + g][:, :].rearrange("p (f s) -> p f s", s=S),
                                      bias_of(e, 4 * g), ALU.add)
                    ins = dve.tensor_tensor(ub[:, 4 * g:4 * g + 4, :], psum[5 + g][:, :].rearrange("p (f s) -> p f s", s=S),
                                            bias_of(e, 8 + 4 * g), ALU.add)
                ins.then_inc(extra_dve, 1)
                dve.wait_ge(extra_dve, chain.next())
                dve.tensor_scalar(gb, gb, LIMIT, None, ALU.min).then_inc(extra_dve, 1)
                dve.wait_ge(extra_dve, chain.next())
                dve.tensor_scalar(ub, ub, LIMIT, -LIMIT, ALU.min, ALU.max).then_inc(extra_dve, 1)
                dve.wait_ge(extra_dve, chain.next())
                dve.scalar_tensor_tensor(ub, ub, 1.0, gb, ALU.add, ALU.mult).then_inc(extra_dve, 1)
                dve.wait_ge(extra_dve, chain.next())
                dve.sem_inc(turn, 1)
                dve.wait_ge(turn, stage(j, 6))
                dve.tensor_tensor(ub, ub, sg, ALU.mult).then_inc(extra_dve, 1)
                dve.wait_ge(extra_dve, chain.next())
                dve.sem_inc(turn, 1)
                dve.wait_ge(turn, stage(j, 10))
                for m in range(DT):
                    ins = dve.tensor_tensor(hidden[:, m, :], hidden[:, m, :], psum[m][:, :], ALU.add)
                ins.then_inc(extra_dve, 1)
                dve.wait_ge(extra_dve, chain.next())
                chain.end()
                dve.sem_inc(turn, 1)

            def skipped(j):
                dve.sem_inc(extra_dve, 9)
                dve.sem_inc(turn, STAGES)

            extra_blocks(dve, taken, skipped)
            dve.wait_ge(turn, 16 * STAGES + 1)

        def pe_extra(pe, mm):
            pe.sem_inc(moe_done.sem, 1)
            pe.wait_ge(moe_done.sem, moe_done.next(pe, 3))

            def taken(j, e, b):
                pe.wait_ge(turn, stage(j, 1))
                for g in range(2):
                    for m in range(4):
                        for t in range(TT):
                            mm(psum[g][:, m * S:(m + 1) * S], hn_tok[:, t, (4 * g + m) * P:(4 * g + m + 1) * P],
                               sel[:, t, :], t == 0, t == TT - 1)
                for t in range(TT):
                    ins = mm.transpose(psum[2][:, t * P:(t + 1) * P], selg[:, t, :], ident)
                    if t == TT - 1:
                        ins.then_inc(turn, 1)
                pe.wait_ge(turn, stage(j, 3))
                pe.wait_ge(extra_w, j * LOADS + LOADS)
                for i in range(4):
                    w = slots[i][:, :].rearrange("p (k c) -> p k c", k=DT)
                    for f in range(4):
                        for k in range(DT):
                            last = i == 3 and f == 3 and k == DT - 1
                            ins = mm(psum[3 + i][:, f * S:(f + 1) * S], w[:, k, f * P:(f + 1) * P],
                                     xg[:, k, :], k == 0, k == DT - 1)
                            if last:
                                ins.then_inc(turn, 1)
                pe.wait_ge(turn, stage(j, 7))
                for i in range(2):
                    w = slots[4 + i][:, :].rearrange("p (k c) -> p k c", k=DT)
                    for k in range(DT):
                        ins = mm(psum[i][:, :], ub[:, k, :], w[:, k, :], k == 0, k == DT - 1)
                        if i == 1 and k == DT - 1:
                            ins.then_inc(turn, 1)
                pe.wait_ge(turn, stage(j, 9))
                for m in range(DT):
                    ins = mm(psum[m][:, :], y_sb[:, m * P:(m + 1) * P], selgt)
                    if m == DT - 1:
                        ins.then_inc(turn, 1)

            extra_blocks(pe, taken)

        def act_extra(act, step):
            act.sem_inc(moe_done.sem, 1)
            act.wait_ge(moe_done.sem, moe_done.next(act, 3))

            def taken(j, e, b):
                chain = TurnOrder(j, 3)
                act.wait_ge(turn, stage(j, 2))
                for g in range(2):
                    act.activation(xg[:, 4 * g:4 * g + 4, :], psum[g][:, :].rearrange("p (m s) -> p m s", s=S), ACT.Copy)
                act.activation(selgt, psum[2][:, :], ACT.Copy).then_inc(extra_act, 1)
                act.wait_ge(extra_act, chain.next())
                act.sem_inc(turn, 1)
                act.wait_ge(turn, stage(j, 5))
                act.activation(sg, gb, ACT.Sigmoid, scale=ALPHA).then_inc(extra_act, 1)
                act.wait_ge(extra_act, chain.next())
                act.sem_inc(turn, 1)
                act.wait_ge(turn, stage(j, 8))
                act.activation(y_sb[:, 0:512], psum[0][:, :], ACT.Copy)
                act.activation(y_sb[:, 512:1024], psum[1][:, :], ACT.Copy).then_inc(extra_act, 1)
                act.wait_ge(extra_act, chain.next())
                chain.end()
                act.sem_inc(turn, 1)

            def skipped(j):
                act.sem_inc(extra_act, 3)

            extra_blocks(act, taken, skipped)

        extra_dve, extra_act = sem("extra_dve_order"), sem("extra_act_order")

        panels2 = Panels(slots[0:4], [sem(f"panel2_{i}_loaded") for i in range(4)],
                         [sem(f"panel2_{i}_used") for i in range(4)])
        freed = [slots[i][:, :] for i in (4, 5)]
        xs_tok, y_tok = (v.rearrange("p (t d) -> p t d", d=D) for v in freed)
        row_vecs = sb("row_vectors", [P, 88])
        dt_bias, a_log, ssm_d, sink = row_vecs[:, 0:32], row_vecs[:, 32:64], row_vecs[:, 64:80], row_vecs[:, 80:88]
        qk_gain = sb("qk_gain", [P, 2])
        rows2_loaded = signal("rows2_loaded")
        ctx_loaded = signal("ctx_loaded")
        rope_loaded = signal("rope_loaded")
        A1X, A1C, A2X = (small[:, 32 + 8 * i:40 + 8 * i] for i in range(3))

        hc = part(0, DT, CTX)
        ctx_tok = part(2048, CT, D)
        ctx_t = part(4096, DT, CTX)
        c_sq, c_std = part(6144, DT, CTX), part(8192, CTX)
        x_sq, x_std = part(8704, DT, T), part(12800, T)

        def sp_second_loads(sp):
            sp.wait_ge(turn, 16 * STAGES + 1)
            sp.dma_start(ctx_tok, a["ctx_2"][0].rearrange("(t p) d -> p t d", p=P)).then_inc(ctx_loaded.sem, 16)
            w = a["w_in_2"][0]
            load = lambda src: panels2.load(sp, src)
            load(w[:, 3328:3360])
            for p in range(3):
                load(w[:, 1792 + p * 512:1792 + (p + 1) * 512])
            for p in range(2):
                load(w[:, 768 + p * 512:768 + (p + 1) * 512])
            for c0 in (0, 3360):
                load(w[:, c0:c0 + 512])
                load(w[:, c0 + 512:c0 + 768])
            for half in range(2):
                c = slice(half * 512, (half + 1) * 512)
                for i, name in enumerate(("w_oa_2", "w_ob_2", "w_oc_2")):
                    g0 = 4128 + i * D + half * 512
                    load(w[:, g0:g0 + 512])
                    load(a[name][0][:, c])
            for half in range(2):
                load(a["w_out_2"][0][:, half * 512:(half + 1) * 512])
            for c0, c1 in FFN_PANELS:
                load(a["ffn_w_gate_2"][0][:, c0:c1])
                load(a["ffn_w_up_2"][0][:, c0:c1])
            for half in range(2):
                for r0, r1 in DOWN_ROWS:
                    load(a["ffn_w_down_2"][0][r0 * P:r1 * P, half * 512:(half + 1) * 512])

        FFN_PANELS = [(c, min(c + 512, DFF2)) for c in range(0, DFF2, 512)]
        DOWN_ROWS = [(r, min(r + 8, FT2)) for r in range(0, FT2, 8)]

        def pool_row_loads(pool):
            for dst, name in ((dt_bias, "ssm_dt_bias_2"), (a_log, "ssm_A_log_2"), (ssm_d, "ssm_D_2"), (sink, "a_sink_2")):
                v = flat(name)
                pool.dma_start(dst, v.rearrange("(a n) -> a n", a=1).broadcast_to([P, v.shape[0]]))\
                    .then_inc(rows2_loaded.sem, 16)
            for i, name in enumerate(QK_NORMS):
                for half in range(2):
                    pool.dma_start(qk_gain[64 * half:64 * half + 64, i:i + 1], flat(name).rearrange("(p n) -> p n", n=1),
                                   allow_slow_non_contiguous=True).then_inc(rows2_loaded.sem, 16)

        def pe_second_norms(pe, mm):
            pe.wait_ge(ctx_loaded.sem, ctx_loaded.next(pe, 16))
            for m in range(DT):
                pe.wait_ge(to_dve.free, to_dve.room())
                bank = to_dve.fill()
                for t in range(CT):
                    ins = mm.transpose(bank[:, t * P:(t + 1) * P], ctx_tok[:, t, m * P:(m + 1) * P], ident)
                    if t == CT - 1:
                        ins.then_inc(to_dve.full, 1)
            pe_norm(pe, mm, c_sq, CTX, DT)
            pe_norm(pe, mm, x_sq, T, DT)

        def dve_second_norms(dve, step):
            for m in range(DT):
                dve.wait_ge(to_dve.full, to_dve.next_full())
                bank = to_dve.take()
                dve.tensor_copy(ctx_t[:, m, :], bank[:, 0:CTX]).then_inc(to_dve.free, 1)
            dve.wait_ge(to_dve.free, to_dve.own_reads())
            for factor, gain, m, which in ((A1X, "norm1_2", 8, 0), (A1C, "norm1_2", 8, 1), (A2X, "norm2_2", 32, 0)):
                dve.scalar_tensor_tensor(factor, mods2[:, m:m + 8, which], 1.0, col(gain), ALU.add, ALU.mult)\
                    .then_inc(dve_done, 1)
                dve.wait_ge(dve_done, step.next())
            dve.sem_inc(resid_ready.sem, 1)
            dve_norm(dve, step, ctx_t, hc, c_std, DT, A1C)
            dve_norm(dve, step, resid, hidden, x_std, DT, A1X)

        def act_second_norms(act, step):
            act.wait_ge(resid_ready.sem, resid_ready.next(act, 2))
            act_norm(act, step, ctx_t, c_sq, c_std, CTX, DT, D, [mods2[:, k, 1:2] for k in range(DT)], hc)
            act_norm(act, step, resid[:, :, :], x_sq, x_std, T, DT, D, [mods2[:, k, 0:1] for k in range(DT)], hidden)

        NC, NH = TT + CT, SSM_HEADS
        ctx_xs = part(2048, CT, D)
        b_t, c_t = part(4096, 2, T), part(5120, 2, T)
        b_tok, b_ctx = part(6144, TT, 256), part(7168, CT, 256)
        h_state = [part(7680 + i * 1024, NH, SSM_P) for i in range(2)]
        s_at = [9728]

        def s_part(*shape):
            v = part(s_at[0], *shape)
            s_at[0] += int(np.prod(shape))
            return v

        d_t, d_ta, acs, e_acs, w_end, e_tot = (s_part(2, NC * NH) for _ in range(6))
        SSM_TMP = 10880
        assert s_at[0] <= SSM_TMP
        conv_x = part(SSM_TMP, 4, T)
        conv_ctx = part(SSM_TMP + 2048, 4, CTX)
        conv = [part(SSM_TMP + 3072 + i * T, T) for i in range(2)]
        decay = [part(SSM_TMP + i * 1024, 8, P) for i in range(2)]
        cb = part(SSM_TMP + 2048, 2, P)
        xdt, xw = part(SSM_TMP + 2304, D), part(SSM_TMP + 3328, D)
        y_part = part(SSM_TMP + 4352, T)

        dt_z = signal("dt_z")
        dt_act = signal("dt_act")
        dt_dve = signal("dt_dve")
        conv_ready = signal("conv_ready")
        conv_silu = signal("conv_silu")
        xs_ready = signal("xs_ready")
        ssm_x = signal("ssm_x")
        ssm_seg = signal("ssm_seg")
        ssm_exp = signal("ssm_exp")
        ssm_probs = signal("ssm_probs")
        ssm_h = signal("ssm_h")
        ssm_d_ready = signal("ssm_d_ready")
        z_ready = signal("z_ready")
        z_used = signal("z_used")
        y_ready = signal("y_ready")
        y_sq = signal("y_sq")
        y_normed = signal("y_normed")
        ys_ready = signal("ys_ready")

        def by_dir(x):
            return x.rearrange("p d (c h) -> p d c h", h=NH)

        def pe_dt(pe, mm):
            pe.wait_ge(normed.sem, normed.next(pe, 2 * DT))
            s, w = panels2.use(DT, 32)
            pe.wait_ge(panels2.loaded[s], panels2.arrived(s))
            pe.wait_ge(to_dve.free, to_dve.room())
            bank = to_dve.fill()
            for c in range(NC):
                src, t = (hidden, c) if c < TT else (hc, c - TT)
                for k in range(DT):
                    ins = mm(bank[:, c * 32:(c + 1) * 32], src[:, k, t * P:(t + 1) * P],
                             w[:, k, :], k == 0, k == DT - 1)
                    if c == NC - 1 and k == DT - 1:
                        ins.then_inc(to_dve.full, 1)
            mm.done(panels2.used[s])

        def pe_dt_sums(pe, mm):
            pe.wait_ge(dt_dve.sem, dt_dve.next(pe))
            pe.wait_ge(to_dve.free, to_dve.room())
            bank = to_dve.fill()
            n = NC * NH
            mm(bank[:, 0:n], con("upper"), d_ta[:, 0, :])
            mm(bank[:, n:2 * n], con("lower"), d_ta[:, 1, :])
            mm(bank[:, 2 * n:4 * n], ones, d_ta.rearrange("p d n -> p (d n)")).then_inc(to_dve.full, 1)

        def dve_dt(dve, step):
            dve.wait_ge(rows2_loaded.sem, rows2_loaded.next(dve, 16 * 8))
            dve.wait_ge(to_dve.full, to_dve.next_full())
            bank = to_dve.take()
            out4 = by_dir(d_t)
            for d in range(2):
                ins = dve.tensor_tensor(out4[:, d, :, :], bank[:, 0:32 * NC].rearrange("p (c x) -> p c x", x=32)[:, :, d * NH:(d + 1) * NH],
                                        dt_bias[:, d * NH:(d + 1) * NH].rearrange("p (c h) -> p c h", c=1).broadcast_to([P, NC, NH]),
                                        ALU.add)
                if d:
                    ins.then_inc(to_dve.free, 1)
                else:
                    ins.then_inc(dve_done, 1)
                    dve.wait_ge(dve_done, step.next())
            dve.wait_ge(to_dve.free, to_dve.own_reads())
            dve.sem_inc(dt_z.sem, 1)
            dve.wait_ge(dt_act.sem, dt_act.next(dve))
            dve.scalar_tensor_tensor(d_t, d_t, 0.0, acs, ALU.max, ALU.add).then_inc(dve_done, 1)
            dve.wait_ge(dve_done, step.next())
            for d in range(2):
                dve.scalar_tensor_tensor(by_dir(d_ta)[:, d, :, :], by_dir(d_t)[:, d, :, :], -1.0,
                                         a_log[:, d * NH:(d + 1) * NH].rearrange("p (c h) -> p c h", c=1).broadcast_to([P, NC, NH]),
                                         ALU.mult, ALU.mult).then_inc(dve_done, 1)
                dve.wait_ge(dve_done, step.next())
            dve.sem_inc(dt_dve.sem, 1)

        def dve_dt_sums(dve, step):
            n = NC * NH
            dve.wait_ge(to_dve.full, to_dve.next_full())
            bank = to_dve.take()
            flat2 = lambda x: x.rearrange("p d n -> p (d n)")
            dve.tensor_copy(flat2(acs), bank[:, 0:2 * n]).then_inc(dve_done, 1)
            dve.wait_ge(dve_done, step.next())
            dve.tensor_copy(flat2(e_tot), bank[:, 2 * n:4 * n]).then_inc(to_dve.free, 1)
            dve.wait_ge(to_dve.free, to_dve.own_reads())
            dve.tensor_tensor(w_end, e_tot, acs, ALU.subtract).then_inc(dve_done, 1)
            dve.wait_ge(dve_done, step.next())
            dve.sem_inc(dt_z.sem, 1)
            dve.wait_ge(dt_act.sem, dt_act.next(dve))
            dve.tensor_tensor(w_end, w_end, d_t, ALU.mult).then_inc(dve_done, 1)
            dve.wait_ge(dve_done, step.next())

        def act_dt(act, step):
            act.wait_ge(dt_z.sem, dt_z.next(act))
            act.activation(acs, d_t, ACT.Abs).then_inc(act_done, 1)
            act.wait_ge(act_done, step.next())
            act.activation(acs, acs, ACT.Exp, scale=-1.0).then_inc(act_done, 1)
            act.wait_ge(act_done, step.next())
            act.activation(acs, acs, ACT.Ln, bias=1.0).then_inc(act_done, 1)
            act.wait_ge(act_done, step.next())
            act.activation(a_log, a_log, ACT.Exp).then_inc(act_done, 1)
            act.wait_ge(act_done, step.next())
            act.sem_inc(dt_act.sem, 1)

        def act_dt_sums(act, step):
            act.wait_ge(dt_z.sem, dt_z.next(act))
            act.activation(e_acs, acs, ACT.Exp).then_inc(act_done, 1)
            act.wait_ge(act_done, step.next())
            act.activation(w_end, w_end, ACT.Exp).then_inc(act_done, 1)
            act.wait_ge(act_done, step.next())
            act.activation(e_tot, e_tot, ACT.Exp).then_inc(act_done, 1)
            act.wait_ge(act_done, step.next())
            act.sem_inc(dt_act.sem, 1)

        def conv_tiles(panel):
            tiles = []
            for m in range(4):
                j = 4 * panel + m
                tiles.append(((conv_x[:, m, :] if panel < 2 else (b_t if m < 2 else c_t)[:, m % 2, :]), T, j))
                if j < 10:
                    tiles.append((conv_ctx[:, m, :], CTX, j))
            return tiles

        def pe_xbc(pe, mm):
            for panel in range(3):
                s, w = panels2.use(DT, 512)
                pe.wait_ge(panels2.loaded[s], panels2.arrived(s))
                for _, n, j in conv_tiles(panel):
                    src = hidden if n == T else hc
                    m = j % 4
                    pe.wait_ge(to_dve.free, to_dve.room())
                    bank = to_dve.fill()
                    for k in range(DT):
                        ins = mm(bank[:, 0:n], w[:, k, m * P:(m + 1) * P], src[:, k, :], k == 0, k == DT - 1)
                        if k == DT - 1:
                            ins.then_inc(to_dve.full, 1)
                mm.done(panels2.used[s])
                if panel == 0:
                    pe_dt_sums(pe, mm)
                for dst, n, j in conv_tiles(panel):
                    pe.wait_ge(conv_silu.sem, conv_silu.next(pe))
                    if j >= 10:
                        continue
                    pe.wait_ge(to_act.free, to_act.room())
                    bank = to_act.fill()
                    for t in range(n // P):
                        ins = mm.transpose(bank[:, t * P:(t + 1) * P], dst[:, t * P:(t + 1) * P], ident)
                        if t == n // P - 1:
                            ins.then_inc(to_act.full, 1)
            pe.wait_ge(to_act.free, to_act.all_sent())

        def dve_conv(dve, step, bank, dst, n, w, bias):
            dve.tensor_scalar(dst[:, 0:n], bank[:, 0:n], w[1], bias, ALU.mult, ALU.add).then_inc(dve_done, 1)
            dve.wait_ge(dve_done, step.next())
            dve.scalar_tensor_tensor(dst[:, 1:n], bank[:, 0:n - 1], w[0], dst[:, 1:n], ALU.mult, ALU.add)\
                .then_inc(dve_done, 1)
            dve.wait_ge(dve_done, step.next())
            dve.scalar_tensor_tensor(dst[:, 0:n - 1], bank[:, 1:n], w[2], dst[:, 0:n - 1], ALU.mult, ALU.add)\
               .then_inc(to_dve.free, 1)
            dve.wait_ge(to_dve.free, to_dve.own_reads())
            dve.sem_inc(conv_ready.sem, 1)

        def dve_xbc(dve, step):
            n_done = 0
            for panel in range(3):
                for _, n, j in conv_tiles(panel):
                    dve.wait_ge(to_dve.full, to_dve.next_full())
                    bank = to_dve.take()
                    if n_done >= 2:
                        dve.wait_ge(conv_silu.sem, conv_silu.next(dve))
                    dve_conv(dve, step, bank, conv[n_done % 2], n,
                             [col("ssm_conv_w_2", 12 * i + j, 1) for i in range(3)], col("ssm_conv_b_2", j, 1))
                    n_done += 1
                if panel == 0:
                    dve_dt_sums(dve, step)
            dve.wait_ge(conv_silu.sem, conv_silu.next(dve, 2))

        def act_xbc(act, step):
            n_done = 0
            for panel in range(3):
                for dst, n, j in conv_tiles(panel):
                    act.wait_ge(conv_ready.sem, conv_ready.next(act))
                    act.activation(dst, conv[n_done % 2][:, 0:n], ACT.Silu).then_inc(act_done, 1)
                    act.wait_ge(act_done, step.next())
                    act.sem_inc(conv_silu.sem, 1)
                    n_done += 1
                if panel == 0:
                    act_dt_sums(act, step)
                for _, n, j in conv_tiles(panel):
                    if j >= 10:
                        continue
                    act.wait_ge(to_act.full, to_act.next_full())
                    bank = to_act.take()
                    if j < 8:
                        dst = (xs_tok if n == T else ctx_xs)[:, :, j * P:(j + 1) * P]
                    else:
                        dst = (b_tok if n == T else b_ctx)[:, :, (j - 8) * P:(j - 7) * P]
                    act.activation(dst, bank[:, 0:n].rearrange("p (t c) -> p t c", c=P), ACT.Copy).then_inc(to_act.free, 1)
            act.wait_ge(to_act.free, to_act.own_reads())
            act.sem_inc(xs_ready.sem, 1)

        def ssm_units():
            for d in range(2):
                for c in (range(NC - CT, NC) if d == 0 else range(NC - 1, NC - CT - 1, -1)):
                    yield d, c
                for c in (range(TT) if d == 0 else range(TT - 1, -1, -1)):
                    yield d, c

        def head_cols(x, d, c, g=None):
            h0, n = (0, NH) if g is None else (8 * g, 8)
            return x[:, d, c * NH + h0:c * NH + h0 + n]

        def over(x, n):
            return x.rearrange("p (h n) -> p h n", n=1).broadcast_to([P, x.shape[1], n])

        def pe_ssm(pe, mm):
            for d, c in ssm_units():
                tri = con("upper") if d == 0 else con("lower")
                own = c < TT
                if own:
                    chunk = slice(c * P, (c + 1) * P)
                    pe.wait_ge(to_dve.free, to_dve.room())
                    bank = to_dve.fill()
                    for g in range(2):
                        ins = mm(bank[:, g * P:(g + 1) * P], b_t[:, g, chunk], c_t[:, g, chunk])
                        if g:
                            ins.then_inc(to_dve.full, 1)
                    for q4 in range(4):
                        pe.wait_ge(to_dve.free, to_dve.room())
                        bank = to_dve.fill()
                        for i in range(4):
                            h = 4 * q4 + i
                            ins = mm(bank[:, i * P:(i + 1) * P], head_cols(d_ta, d, c)[:, h:h + 1].broadcast_to([P, P]),
                                     tri)
                            if i == 3:
                                ins.then_inc(to_dve.full, 1)
                    pe.wait_ge(ssm_h.sem, ssm_h.next(pe))
                    for g in range(2):
                        pe.wait_ge(to_dve.free, to_dve.room())
                        bank = to_dve.fill()
                        mm(bank[:, :], c_t[:, g, chunk],
                           h_state[d][:, 8 * g:8 * g + 8, :].rearrange("p h x -> p (h x)")).then_inc(to_dve.full, 1)
                pe.wait_ge(ssm_x.sem, ssm_x.next(pe))
                for g in range(2):
                    pe.wait_ge(to_dve.free, to_dve.room())
                    bank = to_dve.fill()
                    bt = (b_tok[:, c, :] if own else b_ctx[:, c - TT, :])[:, g * P:(g + 1) * P]
                    mm(bank[:, :], bt, xw[:, g * 512:(g + 1) * 512]).then_inc(to_dve.full, 1)
                if own:
                    for g in range(2):
                        pe.wait_ge(ssm_probs.sem, ssm_probs.next(pe))
                        pe.wait_ge(to_dve.free, to_dve.room())
                        bank = to_dve.fill()
                        for i in range(8):
                            ins = mm(bank[:, i * 64:(i + 1) * 64], decay[g][:, i, :],
                                     xdt[:, (8 * g + i) * 64:(8 * g + i + 1) * 64])
                            if i == 7:
                                ins.then_inc(to_dve.full, 1)

        def dve_ssm(dve, step):
            tt = lambda o, x, y, op: dve.tensor_tensor(o, x, y, op)
            dve.wait_ge(xs_ready.sem, xs_ready.next(dve))
            heads = lambda x: x.rearrange("p (h x) -> p h x", x=SSM_P)
            for i in range(2):
                dve.memset(h_state[i], 0.0).then_inc(dve_done, 1)
                dve.wait_ge(dve_done, step.next())
            for d, c in ssm_units():
                own = c < TT
                xs = heads(xs_tok[:, c, :] if own else ctx_xs[:, c - TT, :])
                tt(heads(xw), xs, over(head_cols(w_end, d, c), SSM_P), ALU.mult).then_inc(dve_done, 1)
                dve.wait_ge(dve_done, step.next())
                if own:
                    tt(heads(xdt), xs, over(head_cols(d_t, d, c), SSM_P), ALU.mult).then_inc(dve_done, 1)
                    dve.wait_ge(dve_done, step.next())
                dve.sem_inc(ssm_x.sem, 1)
                y_g = lambda g: y_tok[:, c, g * 512:(g + 1) * 512].rearrange("p (h x) -> p h x", x=SSM_P)
                if own:
                    dve.wait_ge(to_dve.full, to_dve.next_full())
                    bank = to_dve.take()
                    dve.tensor_tensor(cb, bank[:, 0:256].rearrange("p (g i) -> p g i", g=2),
                                      con("upper" if d == 0 else "lower").rearrange("p (g i) -> p g i", g=1).broadcast_to([P, 2, P]),
                                      ALU.mult).then_inc(to_dve.free, 1)
                    for g in range(2):
                        for i in range(2):
                            dve.wait_ge(to_dve.full, to_dve.next_full())
                            bank = to_dve.take()
                            dve.tensor_tensor(decay[g][:, 4 * i:4 * i + 4, :], over(head_cols(acs, d, c, g)[:, 4 * i:4 * i + 4], P),
                                              bank[:, :].rearrange("p (h i) -> p h i", i=P), ALU.subtract).then_inc(to_dve.free, 1)
                        dve.wait_ge(to_dve.free, to_dve.own_reads())
                        dve.tensor_scalar(decay[g], decay[g], 0.0, None, ALU.max).then_inc(dve_done, 1)
                        dve.wait_ge(dve_done, step.next())
                        dve.sem_inc(ssm_seg.sem, 1)
                    if c == (0 if d == 0 else TT - 1):
                        dve.sem_inc(ssm_h.sem, 1)
                    for g in range(2):
                        dve.wait_ge(to_dve.full, to_dve.next_full())
                        bank = to_dve.take()
                        dst = y_g(g) if d == 0 else y_part.rearrange("p (h x) -> p h x", x=SSM_P)
                        dve.tensor_tensor(dst, bank[:, :].rearrange("p (h x) -> p h x", x=SSM_P),
                                          over(head_cols(e_acs, d, c, g), SSM_P), ALU.mult).then_inc(to_dve.free, 1)
                        dve.wait_ge(to_dve.free, to_dve.own_reads())
                        if d == 1:
                            tt(y_g(g), y_g(g), dst, ALU.add).then_inc(dve_done, 1)
                            dve.wait_ge(dve_done, step.next())
                for g in range(2):
                    h = h_state[d][:, 8 * g:8 * g + 8, :]
                    tt(h, h, over(head_cols(e_tot, d, c, g), SSM_P), ALU.mult).then_inc(dve_done, 1)
                    dve.wait_ge(dve_done, step.next())
                    dve.wait_ge(to_dve.full, to_dve.next_full())
                    bank = to_dve.take()
                    dve.tensor_tensor(h, h, bank[:, :].rearrange("p (h x) -> p h x", x=SSM_P), ALU.add).then_inc(to_dve.free, 1)
                    dve.wait_ge(to_dve.free, to_dve.own_reads())
                if own:
                    if c != (TT - 1 if d == 0 else 0):
                        dve.sem_inc(ssm_h.sem, 1)
                    for g in range(2):
                        dve.wait_ge(to_dve.full, to_dve.next_full())
                        bank = to_dve.take()
                        dve.tensor_tensor(y_g(g), y_g(g), bank[:, :].rearrange("p (h x) -> p h x", x=SSM_P), ALU.add)\
                           .then_inc(to_dve.free, 1)
                    dve.wait_ge(to_dve.free, to_dve.own_reads())
            for t in range(TT):
                tt(heads(xs_tok[:, t, :]), heads(xs_tok[:, t, :]), over(ssm_d, SSM_P), ALU.mult)\
                    .then_inc(dve_done, 1)
                dve.wait_ge(dve_done, step.next())
                tt(y_tok[:, t, :], y_tok[:, t, :], xs_tok[:, t, :], ALU.add).then_inc(dve_done, 1)
                dve.wait_ge(dve_done, step.next())
            for half in range(2):
                for t in range(TT):
                    dve.wait_ge(z_ready.sem, z_ready.next(dve))
                    cc = slice(half * 512, (half + 1) * 512)
                    tt(y_tok[:, t, cc], y_tok[:, t, cc], z_buf[t % 2], ALU.mult).then_inc(dve_done, 1)
                    dve.wait_ge(dve_done, step.next())
                    dve.sem_inc(z_used.sem, 1)
            dve.wait_ge(y_sq.sem, y_sq.next(dve))
            dve.reciprocal(y_rms, y_rms).then_inc(dve_done, 1)
            dve.wait_ge(dve_done, step.next())
            for t in range(TT):
                dve.tensor_scalar(y_tok[:, t, :], y_tok[:, t, :], y_rms[:, t:t + 1], None, ALU.mult)\
                    .then_inc(dve_done, 1)
                dve.wait_ge(dve_done, step.next())
            dve.sem_inc(y_normed.sem, 1)

        z_buf = [part(SSM_TMP + i * T, T) for i in range(2)]
        y_sqr = part(SSM_TMP + 1024, D)
        y_rms = part(SSM_TMP + 2048, TT)
        ys_t = freed[0].rearrange("p (m t) -> p m t", t=T)

        def pool_ssm(pool, step):
            for d, c in ssm_units():
                if c < TT:
                    for g in range(2):
                        pool.wait_ge(ssm_exp.sem, ssm_exp.next(pool))
                        pool.tensor_tensor(decay[g], decay[g], cb[:, g:g + 1, :].broadcast_to([P, 8, P]), ALU.mult)\
                            .then_inc(pool_done, 1)
                        pool.wait_ge(pool_done, step.next())
                        pool.sem_inc(ssm_probs.sem, 1)

        def act_ssm(act, step):
            for d, c in ssm_units():
                if c < TT:
                    for g in range(2):
                        act.wait_ge(ssm_seg.sem, ssm_seg.next(act))
                        act.activation(decay[g], decay[g], ACT.Exp, scale=-1.0).then_inc(act_done, 1)
                        act.wait_ge(act_done, step.next())
                        act.sem_inc(ssm_exp.sem, 1)
            for half in range(2):
                for t in range(TT):
                    act.wait_ge(to_act.full, to_act.next_full())
                    bank = to_act.take()
                    n = half * TT + t
                    if n >= 2:
                        act.wait_ge(z_used.sem, z_used.next(act))
                    act.activation(z_buf[t % 2], bank[:, :], ACT.Silu).then_inc(to_act.free, 1)
                    act.wait_ge(to_act.free, to_act.own_reads())
                    act.sem_inc(z_ready.sem, 1)
            act.wait_ge(z_used.sem, z_used.next(act, 2))
            for t in range(TT):
                act.activation(y_sqr, y_tok[:, t, :], ACT.Square, accum_out=y_rms[:, t:t + 1]).then_inc(act_done, 1)
                act.wait_ge(act_done, step.next())
            act.activation(y_rms, y_rms, ACT.Sqrt, scale=1.0 / D, bias=eps_col[:, 0:1]).then_inc(act_done, 1)
            act.wait_ge(act_done, step.next())
            act.sem_inc(y_sq.sem, 1)
            for m in range(DT):
                act.wait_ge(to_act.full, to_act.next_full())
                bank = to_act.take()
                act.activation(ys_t[:, m, :], bank[:, :], ACT.Copy, scale=col("ssm_norm_2", m, 1)).then_inc(to_act.free, 1)
            act.wait_ge(to_act.free, to_act.own_reads())
            act.sem_inc(ys_ready.sem, 1)

        def pe_ssm_out(pe, mm):
            for half in range(2):
                s, w = panels2.use(DT, 512)
                pe.wait_ge(panels2.loaded[s], panels2.arrived(s))
                for t in range(TT):
                    pe.wait_ge(to_act.free, to_act.room())
                    bank = to_act.fill()
                    for k in range(DT):
                        ins = mm(bank[:, :], hidden[:, k, t * P:(t + 1) * P], w[:, k, :], k == 0, k == DT - 1)
                        if k == DT - 1:
                            ins.then_inc(to_act.full, 1)
                mm.done(panels2.used[s])
            pe.wait_ge(y_normed.sem, y_normed.next(pe))
            for m in range(DT):
                pe.wait_ge(to_act.free, to_act.room())
                bank = to_act.fill()
                for t in range(TT):
                    ins = mm.transpose(bank[:, t * P:(t + 1) * P], y_tok[:, t, m * P:(m + 1) * P], ident)
                    if t == TT - 1:
                        ins.then_inc(to_act.full, 1)

        def pool_rope_load(pool):
            pool.wait_ge(ys_ready.sem, ys_ready.next(pool))
            pool.dma_start(rope.rearrange("p a t -> p (a t)"), a["rope"]).then_inc(rope_loaded.sem, 16)

        q_t, k_t, k_sw = part(2048, 4, T), part(4096, T), part(4608, T)
        kc_t, kc_sw = part(5120, CTX), part(5376, CTX)
        v_all = part(5632, TT + CT, P)
        rope = part(6400, 2, T)
        p_sb = [part(7424 + i * 768, 768) for i in range(2)]
        pt_sb = [part(8960 + i * 768, 768) for i in range(2)]
        att_tok = part(10496, T)
        rot = part(11008, T)
        att_small = part(11520, 64)
        neg_max, row_sum, row_inv, tmp_max = (att_small[:, i * 8:(i + 1) * 8] for i in range(4))
        ya_t, yc_t = part(11648, 4, T), part(13696, 4, T)
        nrm_sq, nrm_std = part(7424, T), part(8192, T)
        att_pairs = [psum_all[:, 0:2, :].rearrange("p a b -> p (a b)"), psum_all[:, 2:4, :].rearrange("p a b -> p (a b)")]
        pt_banks, y_bank, turn_bank = psum[4:6], psum[6], psum[7]

        kv_ready = signal("kv_ready")
        head_sq = signal("head_sq")
        head_std = signal("head_std")
        head_norm = signal("head_norm")
        roped = signal("roped")
        att_in = signal("att_in")
        s_full = signal("scores_full")
        max_ready = signal("max_ready")
        p_ready = signal("p_ready")
        pt_full = signal("pt_full")
        pt_act = signal("pt_act")
        pt_dve = signal("pt_dve")
        y_full = signal("y_full")
        sink_in = signal("sink_in")
        sink_exp = signal("sink_exp")
        att_scaled = signal("att_scaled")
        att_turned = signal("att_turned")
        att_out = signal("att_out")
        att_done = signal("att_done")

        def att_units(kind):
            for n in range(TT):
                lo, hi = (max(0, n - 1), min(TT, n + 2)) if kind == 0 else (0, TT)
                for h in range(ATT_HEADS):
                    yield n, h, lo, (hi - lo) * P, list(range(lo, hi)) + list(range(TT, TT + CT))

        def pe_att_in(pe, mm, kind):
            if kind == 0:
                pe.wait_ge(ys_ready.sem, ys_ready.next(pe))
                pe.wait_ge(rope_loaded.sem, rope_loaded.next(pe, 16))
            s, w = panels2.use(DT, 512)
            pe.wait_ge(panels2.loaded[s], panels2.arrived(s))
            for m in range(4):
                pe.wait_ge(to_act.free, to_act.room())
                bank = to_act.fill()
                for k in range(DT):
                    ins = mm(bank[:, :], w[:, k, m * P:(m + 1) * P], hidden[:, k, :], k == 0, k == DT - 1)
                    if k == DT - 1:
                        ins.then_inc(to_act.full, 1)
            mm.done(panels2.used[s])
            s, w = panels2.use(DT, 256)
            pe.wait_ge(panels2.loaded[s], panels2.arrived(s))
            for src, n in ((hidden, T), (hc, CTX)):
                pe.wait_ge(to_act.free, to_act.room())
                bank = to_act.fill()
                for k in range(DT):
                    ins = mm(bank[:, 0:n], w[:, k, 0:P], src[:, k, :], k == 0, k == DT - 1)
                    if k == DT - 1:
                        ins.then_inc(to_act.full, 1)
            for src, n in ((hidden, TT), (hc, CT)):
                pe.wait_ge(to_act.free, to_act.room())
                bank = to_act.fill()
                for t in range(n):
                    for k in range(DT):
                        ins = mm(bank[:, t * P:(t + 1) * P], src[:, k, t * P:(t + 1) * P],
                                 w[:, k, P:2 * P], k == 0, k == DT - 1)
                        if k == DT - 1 and t == n - 1:
                            ins.then_inc(to_act.full, 1)
            mm.done(panels2.used[s])
            pe.wait_ge(kv_ready.sem, kv_ready.next(pe))
            if kind == 1:
                for v, n in HEADS_NORMED:
                    pe.wait_ge(head_sq.sem, head_sq.next(pe))
                    pe.wait_ge(to_act.free, to_act.room())
                    bank = to_act.fill()
                    mm(bank[:, 0:n], con("head_sum"), nrm_sq[:, 0:n]).then_inc(to_act.full, 1)
                pe.wait_ge(head_norm.sem, head_norm.next(pe, len(HEADS_NORMED)))
            for v in (*[q_t[:, m, :] for m in range(4)], k_t):
                pe.wait_ge(to_dve.free, to_dve.room())
                bank = to_dve.fill()
                mm(bank[:, :], con("rotate"), v).then_inc(to_dve.full, 1)
            pe.wait_ge(roped.sem, roped.next(pe))
            for v, n in ((k_t, T), (kc_t, CTX)):
                pe.wait_ge(to_act.free, to_act.room())
                bank = to_act.fill()
                mm(bank[:, 0:n], con("swap"), v).then_inc(to_act.full, 1)
            pe.wait_ge(to_act.free, to_act.all_sent())
            pe.wait_ge(to_dve.free, to_dve.all_sent())

        HEADS_NORMED = [(q_t[:, m, :], T) for m in range(4)] + [(k_t, T), (kc_t, CTX)]

        def act_att_in(act, step, kind):
            if kind == 1:
                act.wait_ge(att_done.sem, att_done.next(act))
            for dst, n in (*[(q_t[:, m, :], T) for m in range(4)], (k_t, T), (kc_t, CTX),
                           (v_all[:, 0:TT, :].rearrange("p t c -> p (t c)"), T),
                           (v_all[:, TT:TT + CT, :].rearrange("p t c -> p (t c)"), CTX)):
                act.wait_ge(to_act.full, to_act.next_full())
                bank = to_act.take()
                act.activation(dst, bank[:, 0:n], ACT.Copy).then_inc(to_act.free, 1)
            act.wait_ge(to_act.free, to_act.own_reads())
            act.sem_inc(kv_ready.sem, 1)
            if kind == 1:
                for i, (v, n) in enumerate(HEADS_NORMED):
                    act.activation(nrm_sq[:, 0:n], v, ACT.Square).then_inc(act_done, 1)
                    act.wait_ge(act_done, step.next())
                    act.sem_inc(head_sq.sem, 1)
                    act.wait_ge(to_act.full, to_act.next_full())
                    bank = to_act.take()
                    if i:
                        act.wait_ge(head_norm.sem, head_norm.next(act))
                    act.activation(nrm_std[:, 0:n], bank[:, 0:n], ACT.Sqrt, scale=1.0 / HD, bias=eps_col[:, 0:1]).then_inc(to_act.free, 1)
                    act.wait_ge(to_act.free, to_act.own_reads())
                    act.sem_inc(head_std.sem, 1)
            for dst, n in ((k_sw, T), (kc_sw, CTX)):
                act.wait_ge(to_act.full, to_act.next_full())
                bank = to_act.take()
                act.activation(dst, bank[:, 0:n], ACT.Copy).then_inc(to_act.free, 1)
            act.wait_ge(to_act.free, to_act.own_reads())
            act.sem_inc(att_in.sem, 1)

        def dve_att_in(dve, step, kind):
            dve.wait_ge(kv_ready.sem, kv_ready.next(dve))
            if kind == 0:
                dve.wait_ge(rope_loaded.sem, rope_loaded.next(dve, 16))
            if kind == 1:
                for i, (v, n) in enumerate(HEADS_NORMED):
                    dve.wait_ge(head_std.sem, head_std.next(dve))
                    dve.reciprocal(nrm_std[:, 0:n], nrm_std[:, 0:n]).then_inc(dve_done, 1)
                    dve.wait_ge(dve_done, step.next())
                    gain = qk_gain[:, 0:1] if i < 4 else qk_gain[:, 1:2]
                    dve.scalar_tensor_tensor(v, v, gain, nrm_std[:, 0:n], ALU.mult, ALU.mult).then_inc(dve_done, 1)
                    dve.wait_ge(dve_done, step.next())
                    dve.sem_inc(head_norm.sem, 1)
            for v in (*[q_t[:, m, :] for m in range(4)], k_t):
                dve.wait_ge(to_dve.full, to_dve.next_full())
                bank = to_dve.take()
                dve.tensor_tensor(rot, bank[:, :], rope[:, 1, :], ALU.mult).then_inc(to_dve.free, 1)
                dve.wait_ge(to_dve.free, to_dve.own_reads())
                dve.tensor_tensor(v, v, rope[:, 0, :], ALU.mult).then_inc(dve_done, 1)
                dve.wait_ge(dve_done, step.next())
                dve.tensor_tensor(v, v, rot, ALU.add).then_inc(dve_done, 1)
                dve.wait_ge(dve_done, step.next())
            dve.sem_inc(roped.sem, 1)

        def split_tiles(tiles):
            k = (len(tiles) + 1) // 2
            return tiles[:k], tiles[k:]

        def pe_att(pe, mm, kind):
            units_ = list(att_units(kind))
            U = len(units_)
            base = kind * U

            def scores(u):
                n, h, lo, w, tiles = units_[u]
                half, j = slice(64 * (h % 2), 64 * (h % 2) + 64), h // 4
                keys, ckeys = (k_t, kc_t) if h % 2 == j else (k_sw, kc_sw)
                pair = att_pairs[u % 2]
                if base + u >= 2:
                    pe.wait_ge(p_ready.sem, base + u - 1)
                qb = q_t[half, h // 2, n * P:(n + 1) * P]
                mm(pair[:, 512 - w:512], qb, keys[half, lo * P:lo * P + w])
                mm(pair[:, 512:768], qb, ckeys[half, :]).then_inc(s_full.sem, 1)

            def turns(u):
                pe.wait_ge(p_ready.sem, base + u + 1)
                if base + u >= 1:
                    pe.wait_ge(pt_act.sem, base + u)
                    pe.wait_ge(pt_dve.sem, base + u)
                tiles = units_[u][4]
                at = 0
                for b, part_tiles in enumerate(split_tiles(tiles)):
                    for i in range(len(part_tiles)):
                        last = i == len(part_tiles) - 1
                        ins = mm.transpose(pt_banks[b][:, i * P:(i + 1) * P], p_sb[u % 2][:, at * P:(at + 1) * P],
                                           ident)
                        if last:
                            ins.then_inc(pt_full.sem, 1)
                        at += 1

            def values(u):
                n, h, lo, w, tiles = units_[u]
                pe.wait_ge(pt_act.sem, base + u + 1)
                pe.wait_ge(pt_dve.sem, base + u + 1)
                if h == 0 and kind * TT + n >= 1:
                    pe.wait_ge(att_scaled.sem, kind * TT + n)
                j = h // 4
                for i, t in enumerate(tiles):
                    ins = mm(y_bank[:, h * HD:(h + 1) * HD], pt_sb[u % 2][:, i * P:(i + 1) * P],
                             v_all[:, t, j * HD:(j + 1) * HD], i == 0, i == len(tiles) - 1)
                    if h == ATT_HEADS - 1 and i == len(tiles) - 1:
                        ins.then_inc(y_full.sem, 1)

            def turn_out(n):
                pe.wait_ge(att_scaled.sem, kind * TT + n + 1)
                if kind * TT + n >= 1:
                    pe.wait_ge(att_turned.sem, kind * TT + n)
                for m in range(4):
                    ins = mm.transpose(turn_bank[:, m * P:(m + 1) * P], att_tok[:, m * P:(m + 1) * P], ident)
                    if m == 3:
                        ins.then_inc(att_out.sem, 1)

            pe.wait_ge(att_in.sem, att_in.next(pe))
            for i in range(U + 2):
                if i < U:
                    scores(i)
                if i >= 2:
                    values(i - 2)
                if 1 <= i <= U:
                    turns(i - 1)
                if i >= 4 and (i - 4) % ATT_HEADS == ATT_HEADS - 1:
                    turn_out((i - 4) // ATT_HEADS)
            turn_out(TT - 1)

        def dve_att(dve, step, kind):
            units_ = list(att_units(kind))
            U = len(units_)
            scale = HD ** -0.5

            def maximum(u):
                n, h, lo, w, tiles = units_[u]
                pair = att_pairs[u % 2]
                dve.wait_ge(s_full.sem, s_full.next(dve))
                if kind == 0:
                    if n > 0:
                        dve.tensor_tensor(pair[:, 512 - w:640 - w], pair[:, 512 - w:640 - w], con("prev_mask"), ALU.add)\
                            .then_inc(dve_done, 1)
                        dve.wait_ge(dve_done, step.next())
                    if n < TT - 1:
                        dve.tensor_tensor(pair[:, 384:512], pair[:, 384:512], con("next_mask"), ALU.add)\
                            .then_inc(dve_done, 1)
                        dve.wait_ge(dve_done, step.next())
                dve.tensor_reduce(tmp_max[:, 0:1], pair[:, 512 - w:768], AX_X, ALU.max).then_inc(dve_done, 1)
                dve.wait_ge(dve_done, step.next())
                if kind == 0:
                    dve.scalar_tensor_tensor(tmp_max[:, 0:1], tmp_max[:, 0:1], scale, sink[:, h:h + 1], ALU.mult, ALU.max)\
                        .then_inc(dve_done, 1)
                    dve.wait_ge(dve_done, step.next())
                dve.tensor_scalar(neg_max[:, h:h + 1], tmp_max[:, 0:1], -1.0 if kind == 0 else -scale, None, ALU.mult)\
                    .then_inc(dve_done, 1)
                dve.wait_ge(dve_done, step.next())
                dve.sem_inc(max_ready.sem, 1)

            def copy(u):
                tiles = units_[u][4]
                first, second = split_tiles(tiles)
                dve.wait_ge(pt_full.sem, pt_full.next(dve, 2))
                k, m = len(first), len(second)
                dve.tensor_copy(pt_sb[u % 2][:, k * P:(k + m) * P], pt_banks[1][:, 0:m * P]).then_inc(dve_done, 1)
                dve.wait_ge(dve_done, step.next())
                dve.sem_inc(pt_dve.sem, 1)

            def block_out(n):
                dve.wait_ge(y_full.sem, y_full.next(dve))
                if kind == 0:
                    dve.tensor_tensor(row_inv, neg_max, sink, ALU.add).then_inc(dve_done, 1)
                    dve.wait_ge(dve_done, step.next())
                    dve.sem_inc(sink_in.sem, 1)
                    dve.wait_ge(sink_exp.sem, sink_exp.next(dve))
                    dve.tensor_tensor(row_sum, row_sum, row_inv, ALU.add).then_inc(dve_done, 1)
                    dve.wait_ge(dve_done, step.next())
                dve.reciprocal(row_inv, row_sum).then_inc(dve_done, 1)
                dve.wait_ge(dve_done, step.next())
                if kind * TT + n >= 1:
                    dve.wait_ge(att_turned.sem, att_turned.next(dve))
                dve.tensor_tensor(att_tok.rearrange("p (h x) -> p h x", x=HD),
                                  y_bank[:, :].rearrange("p (h x) -> p h x", x=HD), over(row_inv, HD), ALU.mult)\
                    .then_inc(dve_done, 1)
                dve.wait_ge(dve_done, step.next())
                dve.sem_inc(att_scaled.sem, 1)

            for i in range(U + 2):
                if i < U and i % ATT_HEADS != 0:
                    maximum(i)
                if 1 <= i <= U:
                    copy(i - 1)
                if i >= ATT_HEADS and i % ATT_HEADS == 0:
                    block_out(i // ATT_HEADS - 1)
                if i < U and i % ATT_HEADS == 0:
                    maximum(i)

        def act_att(act, step, kind):
            units_ = list(att_units(kind))
            U = len(units_)
            y_dst = ya_t if kind == 0 else yc_t

            def exps(u):
                n, h, lo, w, tiles = units_[u]
                act.wait_ge(max_ready.sem, max_ready.next(act))
                if kind * U + u >= 2:
                    pt_full_wait(act, kind * U + u - 1)
                act.activation(p_sb[u % 2][:, 0:w + CTX], att_pairs[u % 2][:, 512 - w:768], ACT.Exp,
                               bias=neg_max[:, h:h + 1], scale=HD ** -0.5, accum_out=row_sum[:, h:h + 1])\
                    .then_inc(act_done, 1)
                act.wait_ge(act_done, step.next())
                act.sem_inc(p_ready.sem, 1)

            def copy(u):
                first, _ = split_tiles(units_[u][4])
                pt_full_wait(act, kind * U + u + 1)
                act.activation(pt_sb[u % 2][:, 0:len(first) * P], pt_banks[0][:, 0:len(first) * P], ACT.Copy)\
                    .then_inc(act_done, 1)
                act.wait_ge(act_done, step.next())
                act.sem_inc(pt_act.sem, 1)

            def block_out(n):
                act.wait_ge(att_out.sem, att_out.next(act))
                act.activation(y_dst[:, :, n * P:(n + 1) * P], turn_bank[:, :].rearrange("p (m t) -> p m t", t=P), ACT.Copy)\
                    .then_inc(act_done, 1)
                act.wait_ge(act_done, step.next())
                act.sem_inc(att_turned.sem, 1)

            def sink_term():
                if kind == 0:
                    act.wait_ge(sink_in.sem, sink_in.next(act))
                    act.activation(row_inv, row_inv, ACT.Exp).then_inc(act_done, 1)
                    act.wait_ge(act_done, step.next())
                    act.sem_inc(sink_exp.sem, 1)

            for i in range(U + 2):
                if i < U and i % ATT_HEADS != 0:
                    exps(i)
                if 1 <= i <= U:
                    copy(i - 1)
                if i >= ATT_HEADS and i % ATT_HEADS == 0:
                    sink_term()
                if i < U and i % ATT_HEADS == 0:
                    exps(i)
                if i >= 4 and (i - 4) % ATT_HEADS == ATT_HEADS - 1:
                    block_out((i - 4) // ATT_HEADS)
            block_out(TT - 1)
            act.sem_inc(att_done.sem, 1)

        def pt_full_wait(act, units_turned):
            act.wait_ge(pt_full.sem, 2 * units_turned)

        g_buf = [part(2048 + i * 2048, 4, T) for i in range(2)]
        merged = freed[1].rearrange("p (m t) -> p m t", t=T)
        m_tmp = part(6400, T)
        gate_ready = signal("gate_ready")
        gate_used = signal("gate_used")
        merged_ready = signal("merged_ready")

        def branches():
            return ((ya_t, 4), (ys_t, DT), (yc_t, 4))

        def pe_merge(pe, mm):
            pe.wait_ge(att_done.sem, att_done.next(pe, 2))
            for half in range(2):
                for y, k_tiles in branches():
                    for src, kt, banks in ((hidden, DT, to_act), (y, k_tiles, to_dve)):
                        s, w = panels2.use(kt, 512)
                        pe.wait_ge(panels2.loaded[s], panels2.arrived(s))
                        for m in range(4):
                            pe.wait_ge(banks.free, banks.room())
                            bank = banks.fill()
                            for k in range(kt):
                                ins = mm(bank[:, :], w[:, k, m * P:(m + 1) * P], src[:, k, :], k == 0, k == kt - 1)
                                if k == kt - 1:
                                    ins.then_inc(banks.full, 1)
                        mm.done(panels2.used[s])
            mm.settle()
            pe.wait_ge(merged_ready.sem, merged_ready.next(pe))
            for half in range(2):
                pe_linear2(pe, mm, to_dve, merged, DT, 512)

        def pe_linear2(pe, mm, banks, x, k_tiles, width):
            s, w = panels2.use(k_tiles, width)
            pe.wait_ge(panels2.loaded[s], panels2.arrived(s))
            for m in range(width // P):
                pe.wait_ge(banks.free, banks.room())
                bank = banks.fill()
                for k in range(k_tiles):
                    ins = mm(bank[:, :], w[:, k, m * P:(m + 1) * P], x[:, k, :], k == 0, k == k_tiles - 1)
                    if k == k_tiles - 1:
                        ins.then_inc(banks.full, 1)
            mm.done(panels2.used[s])

        def act_merge(act, step):
            for i in range(6):
                if i >= 2:
                    act.wait_ge(gate_used.sem, gate_used.next(act))
                for m in range(4):
                    act.wait_ge(to_act.full, to_act.next_full())
                    bank = to_act.take()
                    act.activation(g_buf[i % 2][:, m, :], bank[:, :], ACT.Sigmoid).then_inc(to_act.free, 1)
                act.wait_ge(to_act.free, to_act.own_reads())
                act.sem_inc(gate_ready.sem, 1)

        def dve_merge(dve, step):
            for i in range(6):
                half, branch = i // 3, i % 3
                dve.wait_ge(gate_ready.sem, gate_ready.next(dve))
                for m in range(4):
                    dve.wait_ge(to_dve.full, to_dve.next_full())
                    bank = to_dve.take()
                    dst = merged[:, 4 * half + m, :] if branch == 0 else m_tmp
                    dve.tensor_tensor(dst, g_buf[i % 2][:, m, :], bank[:, :], ALU.mult).then_inc(to_dve.free, 1)
                    dve.wait_ge(to_dve.free, to_dve.own_reads())
                    if branch:
                        dve.tensor_tensor(merged[:, 4 * half + m, :], merged[:, 4 * half + m, :], m_tmp, ALU.add)\
                            .then_inc(dve_done, 1)
                        dve.wait_ge(dve_done, step.next())
                dve.sem_inc(gate_used.sem, 1)
            dve.sem_inc(merged_ready.sem, 1)
            dve_gated_residual(dve, 16)
            dve.sem_inc(resid_ready.sem, 1)

        def dve_gated_residual(dve, first):
            for m in range(DT):
                dve.wait_ge(to_dve.full, to_dve.next_full())
                bank = to_dve.take()
                dve.scalar_tensor_tensor(resid[:, m, :], bank[:, :], mods2[:, first + m, 0:1], resid[:, m, :],
                                         ALU.mult, ALU.add).then_inc(to_dve.free, 1)
            dve.wait_ge(to_dve.free, to_dve.own_reads())

        f_sq, f_std = part(0, DT, T), part(4096, T)
        act_t = part(4608, FT2, T)
        f_conv = part(0, 2, 4 * T)
        ffn_gate = signal("ffn_gate")

        def conv_buf(i):
            return f_conv[:, (i // 4) % 2, (i % 4) * T:(i % 4 + 1) * T]

        def pe_ffn(pe, mm):
            pe_norm(pe, mm, f_sq, T, DT)
            pe.wait_ge(normed.sem, normed.next(pe, DT))
            for c0, c1 in FFN_PANELS:
                for _ in range(2):
                    pe_linear2(pe, mm, to_dve, hidden, DT, c1 - c0)
            mm.settle()
            pe.wait_ge(to_dve.free, to_dve.all_sent())
            for half in range(2):
                banks = []
                for _ in range(4):
                    pe.wait_ge(to_dve.free, to_dve.room())
                    banks.append(to_dve.fill())
                for r0, r1 in DOWN_ROWS:
                    s, w = panels2.use(r1 - r0, 512)
                    pe.wait_ge(panels2.loaded[s], panels2.arrived(s))
                    for m in range(4):
                        for k in range(r0, r1):
                            ins = mm(banks[m][:, :], w[:, k - r0, m * P:(m + 1) * P],
                                     act_t[:, k, :], k == 0, k == FT2 - 1)
                            if k == FT2 - 1:
                                ins.then_inc(to_dve.full, 1)
                    mm.done(panels2.used[s])
                mm.settle()

        def act_ffn(act, step):
            act.wait_ge(resid_ready.sem, resid_ready.next(act))
            act_norm(act, step, resid[:, :, :], f_sq, f_std, T, DT, D, [mods2[:, 24 + k, 0:1] for k in range(DT)], hidden)
            for f in range(FT2):
                act.wait_ge(conv_ready.sem, conv_ready.next(act))
                act.activation(conv_buf(f), conv_buf(f), ACT.Silu).then_inc(act_done, 1)
                act.wait_ge(act_done, step.next())
                act.sem_inc(ffn_gate.sem, 1)

        def dve_ffn(dve, step):
            dve_norm(dve, step, resid, hidden, f_std, DT, A2X)
            for c0, c1 in FFN_PANELS:
                tiles = range(c0 // P, c1 // P)
                for f in tiles:
                    dve.wait_ge(to_dve.full, to_dve.next_full())
                    bank = to_dve.take()
                    dve_conv(dve, step, bank, conv_buf(f), T, [col("ffn_conv_w_2", FT2 * i + f, 1) for i in range(3)],
                             col("ffn_conv_b_2", f, 1))
                for f in tiles:
                    dve.wait_ge(to_dve.full, to_dve.next_full())
                    bank = to_dve.take()
                    dve.wait_ge(ffn_gate.sem, ffn_gate.next(dve))
                    dve.tensor_tensor(act_t[:, f, :], conv_buf(f), bank[:, :], ALU.mult).then_inc(to_dve.free, 1)
            dve.wait_ge(to_dve.free, to_dve.own_reads())
            dve_gated_residual(dve, 40)
            dve.sem_inc(resid_ready.sem, 1)

        o_sq2, o_std2 = part(0, DT, T), part(4096, T)
        out_tok = part(4608, TT, D)
        final_ready = signal("final_ready")
        out_ready = signal("out_ready")
        out_stored = signal("out_stored")

        def pe_out(pe, mm):
            pe_norm(pe, mm, o_sq2, T, DT)
            pe.wait_ge(final_ready.sem, final_ready.next(pe))
            for t in range(TT):
                for g in range(2):
                    pe.wait_ge(to_act.free, to_act.room())
                    bank = to_act.fill()
                    for m in range(4):
                        ins = mm.transpose(bank[:, m * P:(m + 1) * P], hidden[:, 4 * g + m, t * P:(t + 1) * P], ident)
                        if m == 3:
                            ins.then_inc(to_act.full, 1)

        def act_out(act, step):
            act.wait_ge(resid_ready.sem, resid_ready.next(act))
            act_norm(act, step, resid[:, :, :], o_sq2, o_std2, T, DT, D)
            for t in range(TT):
                for g in range(2):
                    act.wait_ge(to_act.full, to_act.next_full())
                    bank = to_act.take()
                    act.activation(out_tok[:, t, g * 512:(g + 1) * 512], bank[:, :], ACT.Copy).then_inc(to_act.free, 1)
                act.wait_ge(to_act.free, to_act.own_reads())
                act.sem_inc(out_ready.sem, 1)

        def dve_out(dve, step):
            dve.wait_ge(std_ready.sem, std_ready.next(dve))
            dve.reciprocal(o_std2, o_std2).then_inc(dve_done, 1)
            dve.wait_ge(dve_done, step.next())
            for k in range(DT):
                dve.scalar_tensor_tensor(hidden[:, k, :], resid[:, k, :], col("final_norm_2", k, 1), o_std2, ALU.mult, ALU.mult)\
                    .then_inc(dve_done, 1)
                dve.wait_ge(dve_done, step.next())
            dve.sem_inc(final_ready.sem, 1)

        def sp_out(sp):
            for t in range(TT):
                sp.wait_ge(out_ready.sem, out_ready.next(sp))
                sp.dma_start(out[0, t * P:(t + 1) * P, :], out_tok[:, t, :]).then_inc(out_stored.sem, 16)
            sp.wait_ge(out_stored.sem, out_stored.next(sp, 16 * TT))

        block = ctx.enter_context(nc.Block())

        @block.sync
        def _(sp):
            sp_first_loads(sp)
            sp_moe(sp)
            sp_extra(sp)
            sp_second_loads(sp)
            sp_out(sp)

        @block.gpsimd
        def _(pool):
            step = Order()
            pool_row_loads(pool)
            pool_s5_loads(pool)
            pool_s5(pool, step)
            pool_moe_loads(pool)
            pool_ssm(pool, step)
            pool_rope_load(pool)

        @block.tensor
        def _(pe):
            mm = Matmuls(pe)
            pe_turn_inputs(pe, mm)
            pe.wait_ge(silu_ready.sem, silu_ready.next(pe))
            pe_mods(pe, mm, c_first, 1)
            pe_norm(pe, mm, n_sq, T, DT)
            pe_gla(pe, mm)
            pe_s5(pe, mm)
            pe_project_out(pe, mm)
            pe_norm(pe, mm, m_sq, T, DT)
            pe_mods(pe, mm, c_second, 2)
            pe_norm(pe, mm, n2_sq, T, DT)
            pe_route(pe, mm)
            pe_moe(pe, mm)
            pe_extra(pe, mm)
            pe_norm(pe, mm, m_sq, T, DT)
            pe_second_norms(pe, mm)
            pe_dt(pe, mm)
            pe_xbc(pe, mm)
            pe_ssm(pe, mm)
            pe_ssm_out(pe, mm)
            for kind in range(2):
                pe_att_in(pe, mm, kind)
                pe_att(pe, mm, kind)
            pe_merge(pe, mm)
            pe_ffn(pe, mm)
            pe_out(pe, mm)
            mm.settle()

        @block.scalar
        def _(act):
            step = Order()
            act.sem_inc(to_act.free, len(to_act.banks))
            act_first_loads(act)
            act_silus(act, step)
            act.wait_ge(resid_ready.sem, resid_ready.next(act))
            act_norm(act, step, resid[:, :, :], n_sq, n_std, T, DT, D,
                     [mods[:, k, :] for k in range(DT)], hidden)
            act_gla(act, step)
            act_s5_setup(act, step)
            act_s5(act, step)
            act_copy_tiles(act, mix, DT)
            act_norm(act, step, mix, m_sq, m_std, T, DT, D)
            act.wait_ge(resid_ready.sem, resid_ready.next(act))
            act_norm(act, step, resid[:, :, :], n2_sq, n2_std, T, DT, D,
                     [mods[:, 24 + k, :] for k in range(DT)], hidden)
            act_route(act, step)
            act_moe(act, step)
            act_extra(act, step)
            act.wait_ge(turn, 16 * STAGES + 1)
            act_norm(act, step, hidden[:, :, :], m_sq, m_std, T, DT, D)
            act_second_norms(act, step)
            act_dt(act, step)
            act_xbc(act, step)
            act_ssm(act, step)
            for kind in range(2):
                act_att_in(act, step, kind)
                act_att(act, step, kind)
            act_merge(act, step)
            act_ffn(act, step)
            act_out(act, step)

        @block.vector
        def _(dve):
            step = Order()
            dve.sem_inc(to_dve.free, len(to_dve.banks))
            dve_turn_inputs(dve, step)
            dve_first_factors(dve, step)
            dve_norm(dve, step, resid, hidden, n_std, DT, A1)
            dve_gla(dve, step)
            dve_s5_setup(dve, step)
            dve_s5(dve, step)
            dve_add_normed(dve, step, mix, m_std, G1)
            dve_mods(dve, mods2, col("b_mod_2"), 2)
            dve_norm(dve, step, resid, hidden, n2_std, DT, A2)
            dve_route(dve, step)
            dve_moe(dve, step)
            dve_extra(dve, step)
            dve_add_normed(dve, step, hidden, m_std, G2)
            dve_second_norms(dve, step)
            dve_dt(dve, step)
            dve_xbc(dve, step)
            dve_ssm(dve, step)
            for kind in range(2):
                dve_att_in(dve, step, kind)
                dve_att(dve, step, kind)
            dve_merge(dve, step)
            dve_ffn(dve, step)
            dve_out(dve, step)


INPUTS = ["x", "c", "ada_w", "ada_b", "mix_pre_g", "mix_post_g", "ffn_pre_g", "ffn_post_g", "w_in", "w_alpha",
          "b_alpha", "gla_norm_g", "s5_lambda_re", "s5_lambda_im", "s5_log_dt", "s5_b_re", "s5_b_im", "s5_c_re",
          "s5_c_im", "s5_d", "s5_glu_w", "s5_glu_b", "w_out", "router_w", "router_b", "exp_w_gu", "exp_b_gu",
          "exp_w_down", "exp_b_down", "c_2", "ctx_2", "c_ctx_2", "w_mod_2", "b_mod_2", "norm1_2", "norm2_2",
          "w_in_2", "a_sink_2", "ssm_conv_w_2", "ssm_conv_b_2", "ssm_A_log_2", "ssm_dt_bias_2", "ssm_D_2",
          "ssm_norm_2", "c_q_norm_2", "c_k_norm_2", "w_oa_2", "w_ob_2", "w_oc_2", "w_out_2", "ffn_w_up_2",
          "ffn_w_gate_2", "ffn_conv_w_2", "ffn_conv_b_2", "ffn_w_down_2", "final_norm_2"]


def kernel(**inputs):
    from concourse import bacc
    from concourse.bass_utils import run_bass_kernel_spmd

    nc = bacc.Bacc("TRN2", target_bir_lowering=False, num_devices=1)
    table, where, rope = constants()
    arrays, a = {}, {}
    for name, v in [*((n, inputs[n]) for n in INPUTS), ("const", table), ("rope", rope)]:
        v = np.ascontiguousarray(v)
        arrays[f"in_{name}"] = v
        a[name] = nc.dram_tensor(f"in_{name}", v.shape, mybir.dt.from_np(v.dtype), kind="ExternalInput").ap()
    out = nc.dram_tensor("out", (1, T, D), F32, kind="ExternalOutput").ap()
    build(nc, a, table, where, out)
    r = run_bass_kernel_spmd(nc, [arrays], core_ids=[0])
    return r.results[0]["out"]
```

```python
from contextlib import ExitStack

import numpy as np

import concourse.bass as bass
from concourse import mybir

F32 = mybir.dt.float32
I32 = mybir.dt.int32
F32R = mybir.dt.float32r
ALU = mybir.AluOpType
ACT = mybir.ActivationFunctionType
AX_X = mybir.AxisListType.X

P = 128
T = 512
TT = T // P
D = 1024
DT = D // P
EPS = 1e-6

GLA_HEADS, DK, DV, CHUNK = 4, 64, 128, 64
NCHUNK = T // CHUNK
TAU = 16.0
S5_PAIRS = 16
NE, TOPK, DFF = 32, 4, 1024
S = 128
XBLOCKS = T // S
ALPHA, LIMIT = 1.702, 7.0
NEG = -1.0e30

CTX = 256
CT = CTX // P
HD = 64
ATT_HEADS, SSM_HEADS, SSM_P = 8, 16, 64
DFF2 = 2816
FT2 = DFF2 // P

SLOTS = 6
MOE_SLOTS = 4
PANEL = DT * 512


class Count:

    def __init__(self):
        self.n, self.turn, self.index = 0, 0, None

    def add(self, k=1):
        self.n += k
        return self.value()

    def value(self, less=0):
        if self.index is None:
            return self.n - less
        return self.index * self.turn + (self.n - less)

    def enter(self, index, turn):
        self.index, self.turn, self.start = index, turn, self.n

    def leave(self, turns):
        assert self.n - self.start == self.turn, (self.n - self.start, self.turn)
        self.n, self.index = self.start + self.turn * turns, None


class Signal:

    def __init__(self, sem):
        self.sem, self.seen = sem, {}

    def count(self, eng):
        return self.seen.setdefault(eng.engine, Count())

    def next(self, eng, k=1):
        return self.count(eng).add(k)


class Order:

    def __init__(self):
        self.count = Count()

    def next(self, k=1):
        return self.count.add(k)


class TurnOrder:

    def __init__(self, j, n):
        self.j, self.n, self.at = j, n, 0

    def next(self):
        self.at += 1
        return self.j * self.n + self.at

    def end(self):
        assert self.at == self.n, (self.at, self.n)


class Banks:

    def __init__(self, banks, full, free):
        self.banks, self.full, self.free = banks, full, free
        self.sent, self.read = Count(), Count()
        self.at_write = self.at_read = 0

    def room(self):
        return self.sent.value(less=-1)

    def fill(self):
        self.sent.add()
        self.at_write += 1
        return self.banks[(self.at_write - 1) % len(self.banks)]

    def next_full(self):
        return self.read.value(less=-1)

    def take(self):
        self.read.add()
        self.at_read += 1
        return self.banks[(self.at_read - 1) % len(self.banks)]

    def all_sent(self, but=0):
        return self.sent.value(less=but - len(self.banks))

    def own_reads(self):
        return self.read.value(less=-len(self.banks))


class Panels:

    def __init__(self, slots, loaded, used):
        self.slots, self.loaded, self.used = slots, loaded, used
        self.loads = [Count() for _ in slots]
        self.arrivals = [Count() for _ in slots]
        self.at_load = self.at_use = 0

    def load(self, sp, src):
        s = self.at_load % len(self.slots)
        self.at_load += 1
        c = self.loads[s]
        if c.index is not None or c.n > 0:
            sp.wait_ge(self.used[s], c.value())
        c.add()
        rows, cols = src.shape
        k = rows // P
        dst = self.slots[s][:, 0:k * cols].rearrange("p (k c) -> p k c", k=k)
        sp.dma_start(dst, src.rearrange("(k p) c -> p k c", p=P)).then_inc(self.loaded[s], 16)

    def use(self, k, cols):
        s = self.at_use % len(self.slots)
        self.at_use += 1
        return s, self.slots[s][:, 0:k * cols].rearrange("p (k c) -> p k c", k=k)

    def arrived(self, s):
        return self.arrivals[s].add(16)


class Matmuls:

    def __init__(self, pe):
        self.pe, self.owed = pe, None

    def __call__(self, out, lhsT, rhs, start=True, stop=True):
        if stop:
            self.settle()
        ins = self.pe.matmul(out, lhsT, rhs, start=start, stop=stop)
        if self.owed is not None:
            ins.then_inc(self.owed, 1)
            self.owed = None
        return ins

    def transpose(self, out, in_, ident):
        self.settle()
        return self.pe.transpose(out, in_, ident)

    def done(self, sem):
        self.settle()
        self.owed = sem

    def settle(self):
        if self.owed is not None:
            self.pe.drain().then_inc(self.owed, 1)
            self.owed = None


def constants():
    a, b = np.arange(P)[:, None], np.arange(P)[None, :]
    parts = {}
    parts["ident"] = a == b
    parts["ones"] = np.ones((P, P))
    parts["upper"] = a <= b
    parts["lower"] = a >= b
    parts["gla_mask"] = (a <= b) & (a // CHUNK == b // CHUNK)
    parts["rotate"] = np.where((a == b + 1) & (b % 2 == 0), -1.0, 0.0) + ((a == b - 1) & (b % 2 == 1))
    parts["swap"] = a == (b + HD) % P
    parts["head_sum"] = a // HD == b // HD
    parts["prev_mask"] = np.where(a <= b, 0.0, NEG)
    parts["next_mask"] = np.where(b <= a, 0.0, NEG)
    parts["chunk_keep"] = np.broadcast_to((np.arange(T) % CHUNK != 0)[None, :], (P, T))
    parts["iota"] = np.broadcast_to(b, (P, P))
    parts["block_start"] = np.broadcast_to(S * np.arange(XBLOCKS)[None, :], (P, XBLOCKS))
    rows = T // 64
    inv = 10000.0 ** (-np.arange(HD // 4, dtype=np.float32) / (HD // 4))
    t_row = np.repeat(np.arange(rows), 64).astype(np.float32)
    t_col = np.tile(np.arange(64), rows).astype(np.float32)
    ang = np.concatenate([t_row[:, None] * inv, t_col[:, None] * inv], axis=-1).astype(np.float32)
    per_feature = np.tile(np.repeat(ang.T, 2, axis=0), (2, 1))
    rope = np.concatenate([np.cos(per_feature), np.sin(per_feature)], axis=1).astype(np.float32)
    where, at = {}, 0
    for name, v in parts.items():
        where[name] = (at, v.shape[1])
        at += v.shape[1]
    table = np.concatenate([np.asarray(v, np.float32) for v in parts.values()], axis=1)
    return np.ascontiguousarray(table), where, np.ascontiguousarray(rope)


VECTOR_TILES = [
    [("ada_b", 48), ("b_mod_2", 48), ("c", 8), ("c_2", 8), ("c_ctx_2", 8)],
    [("mix_pre_g", 8), ("mix_post_g", 8), ("ffn_pre_g", 8), ("ffn_post_g", 8), ("norm1_2", 8),
     ("norm2_2", 8), ("ssm_norm_2", 8), ("final_norm_2", 8), ("ssm_conv_w_2", 36), ("ssm_conv_b_2", 12), ("s5_d", 4)],
    [("ffn_conv_w_2", 66), ("ffn_conv_b_2", 22), ("s5_glu_b", 4), ("b_alpha", 2), ("gla_norm_g", 1),
     ("s5_lambda_re", 16), ("s5_lambda_im", 16)],
]
QK_NORMS = ["c_q_norm_2", "c_k_norm_2"]


def build(nc, a, table, where, out):
    ctx = ExitStack()
    with ctx:
        def sb(name, shape, dt=F32):
            return ctx.enter_context(nc.sbuf_tensor(name, shape, dt))

        def sem(name):
            return ctx.enter_context(nc.semaphore(name))

        def signal(name):
            return Signal(sem(name))

        resid = sb("resid", [P, DT, T])
        hidden = sb("hidden", [P, DT, T])
        slots = [sb(f"panel{i}", [P, PANEL]) for i in range(MOE_SLOTS)]
        with ExitStack() as over:
            hn_hi = over.enter_context(nc.sbuf_tensor("tokens_high", [P, TT, D], F32R))
            hn_lo = over.enter_context(nc.sbuf_tensor("tokens_low", [P, TT, D], F32R))
        slots += [sb(f"panel{i}", [P, PANEL]) for i in range(MOE_SLOTS, SLOTS)]
        const = sb("const", [P, table.shape[1]])
        cols = sb("cols", [P, 3, P])
        mods = sb("mods", [P, 48, 1])
        mods2 = sb("mods2", [P, 48, 2])
        small = sb("small", [P, 96])
        SCRATCH = 16384
        with ExitStack() as over:
            sel2 = over.enter_context(nc.sbuf_tensor("slots_of_two", [P, TT, 2 * S], F32R))
        s5c = sb("s5_columns", [P, 32, S5_PAIRS])
        s5_dd = sb("s5_d_diagonals", [P, 4, P])
        eps_col = sb("eps_col", [P, 1])
        SELGT_AT, Y_AT, Y_LO_AT = 9216, 9728, 14592
        with ExitStack() as over:
            over.enter_context(nc.sbuf_tensor("under_experts", [P, SELGT_AT], F32))
            tokens_r = over.enter_context(nc.sbuf_tensor("tokens_r", [P, T], F32R))
            y_hi = over.enter_context(nc.sbuf_tensor("y_high", [P, D], F32R))
            over.enter_context(nc.sbuf_tensor("under_y_low", [P, Y_LO_AT - Y_AT - D], F32))
            y_lo = over.enter_context(nc.sbuf_tensor("y_low", [P, D], F32R))
        scratch = sb("scratch", [P, SCRATCH])

        def part(at, *shape):
            n = int(np.prod(shape))
            assert at + n <= SCRATCH, (at, shape)
            v = scratch[:, at:at + n]
            if len(shape) == 2:
                v = v.rearrange("p (a b) -> p a b", b=shape[1])
            if len(shape) == 3:
                v = v.rearrange("p (a b c) -> p a b c", b=shape[1], c=shape[2])
            return v

        def con(name, width=None):
            at, n = where[name]
            return const[:, at:at + (width or n)]

        column_at = {}
        for tile_no, rows in enumerate(VECTOR_TILES):
            at = 0
            for name, n in rows:
                column_at[name] = (tile_no, at, n)
                at += n

        def col(name, first=0, n=None):
            tile_no, at, k = column_at[name]
            n = k - first if n is None else n
            return cols[:, tile_no, at + first:at + first + n]

        ident = con("ident")
        ones = con("ones")

        psum_all = ctx.enter_context(nc.psum_tensor("psum_all", [P, 8, 512], F32))
        psum = [psum_all[:, i, :] for i in range(8)]
        to_act = Banks(psum[0:4], sem("act_banks_full"), sem("act_banks_free"))
        to_dve = Banks(psum[4:8], sem("dve_banks_full"), sem("dve_banks_free"))
        panels = Panels(slots, [sem(f"panel{i}_loaded") for i in range(SLOTS)],
                        [sem(f"panel{i}_used") for i in range(SLOTS)])

        act_done = sem("act_done")
        dve_done = sem("dve_done")
        pool_done = sem("pool_done")
        x_loaded = signal("x_loaded")
        const_loaded = signal("const_loaded")
        rows_loaded = signal("rows_loaded")
        s5_loaded = signal("s5_loaded")
        gla_loaded = signal("gla_loaded")
        cols_ready = signal("cols_ready")
        silu_ready = signal("silu_ready")
        mod_row = signal("mod_row")
        mod_cols = signal("mod_cols")
        sq_ready = signal("sq_ready")
        std_ready = signal("std_ready")
        scaled = signal("scaled")
        normed = signal("normed")
        resid_ready = signal("resid_ready")
        resid_tile = signal("resid_tile")
        alr_ready = signal("alr_ready")
        gla_act = signal("gla_act")
        gla_dve = signal("gla_dve")
        kte_ready = signal("kte_ready")
        state_ready = signal("state_ready")
        probs_ready = signal("probs_ready")
        o_ready = signal("o_ready")
        osq_ready = signal("osq_ready")
        ostd_ready = signal("ostd_ready")
        gla_out = signal("gla_out")
        s5_cols = signal("s5_cols")
        s5_dve = signal("s5_dve")
        s5_steps = signal("s5_steps")
        s5_blocks = signal("s5_blocks")
        s5_table = signal("s5_table")
        s5_tab_ready = signal("s5_tab_ready")
        s5_table_used = signal("s5_table_used")
        s5_x = signal("s5_x")
        s5_y = signal("s5_y")
        s5_gelu = signal("s5_gelu")
        s5_gate = signal("s5_gate")
        s5_out = signal("s5_out")


        def act_norm(act, step, src, sq, std, n, kt, dim, shifts=None, dst=None, after=None, copied=False):
            for k in range(kt):
                if after is not None:
                    act.wait_ge(after.sem, after.next(act))
                if copied:
                    act.wait_ge(to_act.full, to_act.next_full())
                    bank = to_act.take()
                    act.activation(src[:, k, :], bank[:, 0:n], ACT.Copy).then_inc(to_act.free, 1)
                    act.wait_ge(to_act.free, to_act.own_reads())
                act.activation(sq[:, k, :], src[:, k, :], ACT.Square).then_inc(sq_ready.sem, 1)
            act.wait_ge(to_act.full, to_act.next_full())
            bank = to_act.take()
            act.activation(std, bank[:, 0:n], ACT.Sqrt, scale=1.0 / dim, bias=eps_col[:, 0:1]).then_inc(to_act.free, 1)
            act.wait_ge(to_act.free, to_act.own_reads())
            act.sem_inc(std_ready.sem, 1)
            if shifts is not None:
                for k in range(kt):
                    act.wait_ge(scaled.sem, scaled.next(act))
                    act.activation(dst[:, k, :], dst[:, k, :], ACT.Identity, bias=shifts[k]).then_inc(normed.sem, 1)

        def pe_norm(pe, mm, sq, n, kt):
            pe.wait_ge(to_act.free, to_act.room())
            bank = to_act.fill()
            for k in range(kt):
                pe.wait_ge(sq_ready.sem, sq_ready.next(pe))
                ins = mm(bank[:, 0:n], ones, sq[:, k, :], k == 0, k == kt - 1)
                if k == kt - 1:
                    ins.then_inc(to_act.full, 1)

        def dve_norm(dve, step, src, dst, std, kt, factors):
            dve.wait_ge(std_ready.sem, std_ready.next(dve))
            dve.reciprocal(std, std).then_inc(dve_done, 1)
            dve.wait_ge(dve_done, step.next())
            for k in range(kt):
                dve.scalar_tensor_tensor(dst[:, k, :], src[:, k, :], factors[:, k:k + 1], std,
                                         ALU.mult, ALU.mult).then_inc(scaled.sem, 1)

        def pe_linear(pe, mm, banks, x, n, k_tiles, width, col_tiles=None):
            s, w = panels.use(k_tiles, width)
            pe.wait_ge(panels.loaded[s], panels.arrived(s))
            for m in range(-(-width // P)):
                pe.wait_ge(banks.free, banks.room())
                bank = banks.fill()
                c = min(P, width - m * P)
                for k in range(k_tiles):
                    ins = mm(bank[0:c, 0:n], w[:, k, m * P:m * P + c], x[:, k, 0:n], k == 0, k == k_tiles - 1)
                    if k == k_tiles - 1:
                        ins.then_inc(banks.full, 1)
            mm.done(panels.used[s])

        def pe_linear_tokens(pe, mm, banks, x, tok_tiles, k_tiles, width):
            s, w = panels.use(k_tiles, width)
            pe.wait_ge(panels.loaded[s], panels.arrived(s))
            for t in range(tok_tiles):
                pe.wait_ge(banks.free, banks.room())
                bank = banks.fill()
                for k in range(k_tiles):
                    ins = mm(bank[:, 0:width], x[:, k, t * P:(t + 1) * P], w[:, k, :], k == 0, k == k_tiles - 1)
                    if k == k_tiles - 1:
                        ins.then_inc(banks.full, 1)
            mm.done(panels.used[s])

        def pe_mod_row(pe, mm, banks, vectors, n):
            s, w = panels.use(DT, 512)
            pe.wait_ge(panels.loaded[s], panels.arrived(s))
            pe.wait_ge(banks.free, banks.room())
            bank = banks.fill()
            for k in range(DT):
                ins = mm(bank[0:n, :], vectors[:, k, :], w[:, k, :], k == 0, k == DT - 1)
                if k == DT - 1:
                    ins.then_inc(banks.full, 1)
            mm.done(panels.used[s])

        def pe_mod_turn(pe, mm, banks, row, n):
            pe.wait_ge(mod_row.sem, mod_row.next(pe))
            pe.wait_ge(banks.free, banks.room())
            bank = banks.fill()
            for m in range(4):
                ins = mm.transpose(bank[:, m * n:(m + 1) * n], row[0:n, m * P:(m + 1) * P], ident[0:n, 0:n])
                if m == 3:
                    ins.then_inc(banks.full, 1)

        def act_mod_row(act, banks, row, n):
            act.wait_ge(banks.full, banks.next_full())
            bank = banks.take()
            act.activation(row[0:n, :], bank[0:n, :], ACT.Copy).then_inc(banks.free, 1)
            act.wait_ge(banks.free, banks.own_reads())
            act.sem_inc(mod_row.sem, 1)

        def act_mod_turn(act, banks, dst, p, n):
            act.wait_ge(banks.full, banks.next_full())
            bank = banks.take()
            act.activation(dst[:, 4 * p:4 * p + 4, :], bank[:, 0:4 * n].rearrange("p (m n) -> p m n", n=n),
                           ACT.Copy).then_inc(banks.free, 1)

        def dve_mod_bias(dve, step, dst, bias, n):
            dve.wait_ge(mod_cols.sem, mod_cols.next(dve))
            dve.tensor_tensor(dst[:, :, :], dst[:, :, :],
                              bias.rearrange("p (m n) -> p m n", n=1).broadcast_to([P, 48, n]),
                              ALU.add).then_inc(dve_done, 1)
            dve.wait_ge(dve_done, step.next())

        MOD_PANELS = 6 * D // 512

        mod_rows = [part(8192 + i * 512, 512) for i in range(2)]

        def pe_first_mods(pe, mm):
            for p in range(MOD_PANELS):
                pe_mod_row(pe, mm, to_act, c_first, 1)
                if p:
                    pe_mod_turn(pe, mm, to_act, mod_rows[(p - 1) % 2], 1)
            pe_mod_turn(pe, mm, to_act, mod_rows[(MOD_PANELS - 1) % 2], 1)

        def act_first_mods(act):
            for p in range(MOD_PANELS):
                act_mod_row(act, to_act, mod_rows[p % 2], 1)
                if p:
                    act_mod_turn(act, to_act, mods, p - 1, 1)
            act_mod_turn(act, to_act, mods, MOD_PANELS - 1, 1)
            act.wait_ge(to_act.free, to_act.own_reads())
            act.sem_inc(mod_cols.sem, 1)

        x_tok = hidden[:, :, :].rearrange("p a b -> p (a b)").rearrange("p (t d) -> p t d", d=D)
        rows = part(0, 3, P)
        w_alpha = sb("w_alpha", [16, 256])

        def sp_first_loads(sp):
            ada = a["ada_w"][0]
            for p in range(MOD_PANELS):
                if p == 1:
                    sp.wait_ge(rows_loaded.sem, rows_loaded.next(sp, 16 * N_ROWS))
                panels.load(sp, ada[:, p * 512:(p + 1) * 512])
            w = a["w_in"][0]
            for c0, c1 in IN_PANELS:
                panels.load(sp, w[:, c0:c1])
            for p in range(MOD_PANELS):
                panels.load(sp, a["w_mod_2"][0][:, p * 512:(p + 1) * 512])
            panels.load(sp, a["s5_glu_w"][0])
            for p in range(2):
                panels.load(sp, a["w_out"][0][:, p * 512:(p + 1) * 512])

        IN_PANELS = [(1536, 1552), (0, 512), (512, 1024), (1024, 1536), (1552, 2064)]

        def act_first_loads(act):
            act.dma_start(const[:, :], a["const"]).then_inc(const_loaded.sem, 16)
            for tile_no, group in enumerate(VECTOR_TILES):
                at = 0
                for name, n in group:
                    act.dma_start(rows[at:at + n, tile_no, :], flat(name).rearrange("(r c) -> r c", c=P))\
                       .then_inc(rows_loaded.sem, 16)
                    at += n
            act.dma_start(x_tok, a["x"][0].rearrange("(t p) d -> p t d", p=P)).then_inc(x_loaded.sem, 16)
            act.dma_start(w_alpha[:, :], a["w_alpha"][0]).then_inc(gla_loaded.sem, 16)

        N_ROWS = sum(len(g) for g in VECTOR_TILES)

        def flat(name):
            v = a[name]
            if len(v.shape) == 1:
                return v
            names = " ".join(f"d{i}" for i in range(len(v.shape)))
            return v.rearrange(f"{names} -> ({names})")

        silus = sb("silus", [P, 24])
        c_first = silus[:, 0:8].rearrange("p (k n) -> p k n", n=1)
        c_second = silus[:, 8:24].rearrange("p (n k) -> p k n", n=2)

        def pe_turn_inputs(pe, mm):
            pe.wait_ge(const_loaded.sem, const_loaded.next(pe, 16))
            pe.wait_ge(rows_loaded.sem, rows_loaded.next(pe, 16 * N_ROWS))
            pe.wait_ge(to_dve.free, to_dve.room())
            bank = to_dve.fill()
            for i, group in enumerate(VECTOR_TILES):
                n = sum(r for _, r in group)
                ins = mm.transpose(bank[:, i * P:i * P + n], rows[0:n, i, :], ident[0:n, 0:n])
                if i == 2:
                    ins.then_inc(to_dve.full, 1)
            pe.wait_ge(x_loaded.sem, x_loaded.next(pe, 16))
            for m in range(DT):
                pe.wait_ge(to_dve.free, to_dve.room())
                bank = to_dve.fill()
                for t in range(TT):
                    ins = mm.transpose(bank[:, t * P:(t + 1) * P], x_tok[:, t, m * P:(m + 1) * P], ident)
                    if t == TT - 1:
                        ins.then_inc(to_dve.full, 1)

        def dve_turn_inputs(dve, step):
            dve.memset(eps_col[:, :], EPS).then_inc(dve_done, 1)
            dve.wait_ge(dve_done, step.next())
            dve.wait_ge(to_dve.full, to_dve.next_full())
            bank = to_dve.take()
            for i, group in enumerate(VECTOR_TILES):
                n = sum(r for _, r in group)
                c = dve.tensor_copy(cols[:, i, 0:n], bank[:, i * P:i * P + n])
                if i < 2:
                    c.then_inc(dve_done, 1)
                    dve.wait_ge(dve_done, step.next())
                else:
                    c.then_inc(to_dve.free, 1)
            dve.wait_ge(to_dve.free, to_dve.own_reads())
            dve.sem_inc(cols_ready.sem, 1)
            for m in range(DT):
                dve.wait_ge(to_dve.full, to_dve.next_full())
                bank = to_dve.take()
                dve.tensor_copy(resid[:, m, :], bank[:, :]).then_inc(to_dve.free, 1)
            dve.wait_ge(to_dve.free, to_dve.own_reads())
            dve.sem_inc(resid_ready.sem, 1)

        def act_silus(act, step):
            act.wait_ge(cols_ready.sem, cols_ready.next(act))
            act.activation(silus[:, 0:24], cols[:, 0, 96:120], ACT.Silu).then_inc(act_done, 1)
            act.wait_ge(act_done, step.next())
            act.sem_inc(silu_ready.sem, 1)

        A1, G1, A2, G2 = (small[:, i * 8:(i + 1) * 8] for i in range(4))

        def dve_first_factors(dve, step):
            dve_mod_bias(dve, step, mods, col("ada_b"), 1)
            for i, (factor, gain, m) in enumerate([(A1, "mix_pre_g", 8), (A2, "ffn_pre_g", 32)]):
                dve.scalar_tensor_tensor(factor, mods[:, m:m + 8, 0], 1.0, col(gain), ALU.add, ALU.mult)\
                    .then_inc(dve_done, 1)
                dve.wait_ge(dve_done, step.next())
            for factor, gain, m in [(G1, "mix_post_g", 16), (G2, "ffn_post_g", 40)]:
                dve.tensor_tensor(factor, mods[:, m:m + 8, 0], col(gain), ALU.mult).then_inc(dve_done, 1)
                dve.wait_ge(dve_done, step.next())

        n_sq, n_std = part(0, DT, T), part(4096, T)
        q, kk, v_tok = part(0, 2, T), part(1024, 2, T), part(2048, TT, 512)
        og, u_t, alr = part(4096, 4, T), part(6144, 4, T), part(8192, T)

        def act_project(act, step):
            for m in range(4):
                act.wait_ge(to_act.full, to_act.next_full())
                bank = to_act.take()
                act.activation((q if m < 2 else kk)[:, m % 2, :], bank[:, :], ACT.Copy).then_inc(to_act.free, 1)
            act.wait_ge(to_act.free, to_act.own_reads())
            act.sem_inc(gla_act.sem, 1)

        def act_project_v(act):
            for m in range(4):
                act.wait_ge(to_act.full, to_act.next_full())
                bank = to_act.take()
                act.activation(v_tok[:, m, :], bank[:, :], ACT.Copy).then_inc(to_act.free, 1)

        def act_project_rest(act, step):
            for m in range(4):
                act.wait_ge(to_act.full, to_act.next_full())
                bank = to_act.take()
                act.activation(og[:, m, :], bank[:, :], ACT.Silu).then_inc(to_act.free, 1)
            for m in range(4):
                act.wait_ge(to_act.full, to_act.next_full())
                bank = to_act.take()
                act.activation(u_t[:, m, :], bank[:, :], ACT.Copy).then_inc(to_act.free, 1)
            act.wait_ge(to_act.free, to_act.own_reads())
            act.sem_inc(gla_act.sem, 1)

        bsum, work, kinv = part(8704, 2, T), part(9728, 2, T), part(10752, 2, T)
        kte, states = part(11776, TT, 256), part(12800, NCHUNK, 2, P)
        probs = [part(14848, TT, P), part(15360, TT, P)]
        o_sb, o_sq = part(15872, T), part(8704, T)
        decays = sb("decays", [P, 2, NCHUNK])
        o_std = alr

        def pe_gla(pe, mm):
            pe.wait_ge(normed.sem, normed.next(pe, DT))
            pe_linear(pe, mm, to_dve, hidden, T, DT, 16)
            pe_linear(pe, mm, to_act, hidden, T, DT, 512)
            pe.wait_ge(gla_loaded.sem, gla_loaded.next(pe, 16))
            pe.wait_ge(alr_ready.sem, alr_ready.next(pe))
            for m in range(2):
                pe.wait_ge(to_dve.free, to_dve.room())
                bank = to_dve.fill()
                mm(bank[:, :], w_alpha[:, m * P:(m + 1) * P], alr[0:16, :]).then_inc(to_dve.full, 1)
            pe_linear_tokens(pe, mm, to_act, hidden, TT, DT, 512)
            pe_linear(pe, mm, to_act, hidden, T, DT, 512)
            pe_linear(pe, mm, to_act, hidden, T, DT, 512)
            pe.wait_ge(kte_ready.sem, kte_ready.next(pe))
            for m in range(2):
                pe.wait_ge(to_dve.free, to_dve.room())
                bank = to_dve.fill()
                for t in range(TT):
                    ins = mm.transpose(bank[:, t * P:(t + 1) * P], work[:, m, t * P:(t + 1) * P], ident)
                    if t == TT - 1:
                        ins.then_inc(to_dve.full, 1)
            pe.wait_ge(to_dve.free, to_dve.all_sent())
            pe.wait_ge(to_act.free, to_act.all_sent())
            for n in range(NCHUNK - 1):
                h = slice(64 * (n % 2), 64 * (n % 2) + 64)
                pe.wait_ge(to_dve.free, to_dve.room())
                bank = to_dve.fill()
                for pr in range(2):
                    ins = mm(bank[:, pr * 256:(pr + 1) * 256], kte[h, n // 2, pr * P:(pr + 1) * P],
                             v_tok[h, n // 2, pr * 256:(pr + 1) * 256])
                    if pr:
                        ins.then_inc(to_dve.full, 1)
            for h in range(GLA_HEADS):
                pr, half = h // 2, slice(64 * (h % 2), 64 * (h % 2) + 64)
                pe.wait_ge(to_dve.free, to_dve.room())
                bank = to_dve.fill()
                for t in range(TT):
                    tok = slice(t * P, (t + 1) * P)
                    ins = mm(bank[:, tok], kinv[half, pr, tok], q[half, pr, tok])
                    if t == TT - 1:
                        ins.then_inc(to_dve.full, 1)
            for h in range(GLA_HEADS):
                pr, half = h // 2, slice(64 * (h % 2), 64 * (h % 2) + 64)
                pe.wait_ge(probs_ready.sem, probs_ready.next(pe))
                if h == 0:
                    pe.wait_ge(state_ready.sem, state_ready.next(pe))
                pe.wait_ge(to_act.free, to_act.room())
                bank = to_act.fill()
                for t in range(TT):
                    mm(bank[:, t * P:(t + 1) * P], v_tok[:, t, h * P:(h + 1) * P], probs[h % 2][:, t, :],
                       t == 0, False)
                for n in range(1, NCHUNK):
                    ins = mm(bank[:, n * 64:(n + 1) * 64], states[half, n, pr, :],
                             q[half, pr, n * 64:(n + 1) * 64], False, n == NCHUNK - 1)
                    if n == NCHUNK - 1:
                        ins.then_inc(to_act.full, 1)
                pe.wait_ge(osq_ready.sem, osq_ready.next(pe))
                pe.wait_ge(to_act.free, to_act.room())
                bank = to_act.fill()
                mm(bank[:, :], ones, o_sq).then_inc(to_act.full, 1)

        def dve_gla(dve, step):
            dve.wait_ge(to_dve.full, to_dve.next_full())
            bank = to_dve.take()
            dve.tensor_copy(alr[0:16, :], bank[0:16, :]).then_inc(to_dve.free, 1)
            dve.wait_ge(to_dve.free, to_dve.own_reads())
            dve.sem_inc(alr_ready.sem, 1)
            for m in range(2):
                dve.wait_ge(to_dve.full, to_dve.next_full())
                bank = to_dve.take()
                dve.tensor_scalar(bsum[:, m, :], bank[:, :], col("b_alpha", m, 1), None, ALU.add)\
                   .then_inc(to_dve.free, 1)
            dve.wait_ge(to_dve.free, to_dve.own_reads())
            dve.sem_inc(gla_dve.sem, 1)
            dve.wait_ge(gla_act.sem, gla_act.next(dve, 2))
            for m in range(2):
                dve.scalar_tensor_tensor(bsum[:, m, :], bsum[:, m, :], 0.0, work[:, m, :], ALU.min, ALU.subtract)\
                    .then_inc(dve_done, 1)
                dve.wait_ge(dve_done, step.next())
                dve.tensor_tensor_scan(kinv[:, m, :], con("chunk_keep"), bsum[:, m, :], 0.0, ALU.mult, ALU.add)\
                    .then_inc(dve_done, 1)
                dve.wait_ge(dve_done, step.next())
            dve.tensor_copy(bsum, kinv).then_inc(dve_done, 1)
            dve.wait_ge(dve_done, step.next())
            c = bsum.rearrange("p m (n c) -> p (m n) c", c=CHUNK)
            dve.tensor_tensor(work.rearrange("p m (n c) -> p (m n) c", c=CHUNK),
                              c[:, :, CHUNK - 1:CHUNK].broadcast_to([P, 2 * NCHUNK, CHUNK]), c, ALU.subtract)\
                .then_inc(dve_done, 1)
            dve.wait_ge(dve_done, step.next())
            dve.sem_inc(gla_dve.sem, 1)
            dve.wait_ge(gla_act.sem, gla_act.next(dve))
            dve.tensor_copy(decays.rearrange("p m n -> p (m n)"), c[:, :, CHUNK - 1]).then_inc(dve_done, 1)
            dve.wait_ge(dve_done, step.next())
            dve.scalar_tensor_tensor(q, q, DK ** -0.5, bsum, ALU.mult, ALU.mult).then_inc(dve_done, 1)
            dve.wait_ge(dve_done, step.next())
            dve.tensor_tensor(kinv, kk, kinv, ALU.mult).then_inc(dve_done, 1)
            dve.wait_ge(dve_done, step.next())
            dve.tensor_tensor(work, kk, work, ALU.mult).then_inc(dve_done, 1)
            dve.wait_ge(dve_done, step.next())
            dve.sem_inc(kte_ready.sem, 1)
            for m in range(2):
                dve.wait_ge(to_dve.full, to_dve.next_full())
                bank = to_dve.take()
                dve.tensor_copy(kte[:, :, m * P:(m + 1) * P], bank[:, :].rearrange("p (t c) -> p t c", c=P))\
                   .then_inc(to_dve.free, 1)
            dve.memset(states[:, 0, :, :], 0.0).then_inc(dve_done, 1)
            dve.wait_ge(dve_done, step.next())
            for n in range(NCHUNK - 1):
                dve.wait_ge(to_dve.full, to_dve.next_full())
                bank = to_dve.take()
                for pr in range(2):
                    for i in range(2):
                        half = slice(64 * i, 64 * i + 64)
                        ins = dve.scalar_tensor_tensor(states[half, n + 1, pr, :], states[half, n, pr, :],
                                                       decays[half, pr, n:n + 1],
                                                       bank[half, pr * 256 + i * P:pr * 256 + (i + 1) * P],
                                                       ALU.mult, ALU.add)
                        if pr == 1 and i == 1:
                            ins.then_inc(to_dve.free, 1)
                            dve.wait_ge(to_dve.free, to_dve.own_reads())
                        else:
                            ins.then_inc(dve_done, 1)
                            dve.wait_ge(dve_done, step.next())
            dve.sem_inc(state_ready.sem, 1)
            for h in range(GLA_HEADS):
                dve.wait_ge(to_dve.full, to_dve.next_full())
                bank = to_dve.take()
                if h >= 2:
                    dve.wait_ge(o_ready.sem, o_ready.next(dve))
                dve.tensor_tensor(probs[h % 2], bank[:, :].rearrange("p (t c) -> p t c", c=P),
                                  con("gla_mask").rearrange("p (t c) -> p t c", t=1).broadcast_to([P, TT, P]),
                                  ALU.mult).then_inc(to_dve.free, 1)
                dve.wait_ge(to_dve.free, to_dve.own_reads())
                dve.sem_inc(probs_ready.sem, 1)
                if h >= 1:
                    dve_gla_out(dve, step, h - 1)
            dve_gla_out(dve, step, GLA_HEADS - 1)

        def dve_gla_out(dve, step, h):
            dve.wait_ge(ostd_ready.sem, ostd_ready.next(dve))
            dve.reciprocal(o_std, o_std).then_inc(dve_done, 1)
            dve.wait_ge(dve_done, step.next())
            dve.scalar_tensor_tensor(o_sb, o_sb, col("gla_norm_g"), o_std, ALU.mult, ALU.mult).then_inc(dve_done, 1)
            dve.wait_ge(dve_done, step.next())
            if h == 0:
                dve.wait_ge(gla_act.sem, gla_act.next(dve))
            dve.tensor_tensor(hidden[:, h, :], o_sb, og[:, h, :], ALU.mult).then_inc(dve_done, 1)
            dve.wait_ge(dve_done, step.next())
            dve.sem_inc(gla_out.sem, 1)

        def act_gla(act, step):
            act_project(act, step)
            act.wait_ge(gla_dve.sem, gla_dve.next(act))
            act.activation(work, bsum, ACT.Abs).then_inc(act_done, 1)
            act.wait_ge(act_done, step.next())
            act.activation(work, work, ACT.Exp, scale=-1.0).then_inc(act_done, 1)
            act.wait_ge(act_done, step.next())
            act.activation(work, work, ACT.Ln, bias=1.0).then_inc(act_done, 1)
            act.wait_ge(act_done, step.next())
            act.sem_inc(gla_act.sem, 1)
            act_project_v(act)
            act.wait_ge(gla_dve.sem, gla_dve.next(act))
            act.activation(kinv, bsum, ACT.Exp, scale=-1.0 / TAU).then_inc(act_done, 1)
            act.wait_ge(act_done, step.next())
            act.activation(bsum, bsum, ACT.Exp, scale=1.0 / TAU).then_inc(act_done, 1)
            act.wait_ge(act_done, step.next())
            act.activation(work, work, ACT.Exp, scale=1.0 / TAU).then_inc(act_done, 1)
            act.wait_ge(act_done, step.next())
            act.sem_inc(gla_act.sem, 1)
            act_project_rest(act, step)
            for h in range(GLA_HEADS):
                act.wait_ge(to_act.full, to_act.next_full())
                bank = to_act.take()
                if h >= 1:
                    act.wait_ge(gla_out.sem, gla_out.next(act))
                act.activation(o_sq, bank[:, :], ACT.Square).then_inc(act_done, 1)
                act.wait_ge(act_done, step.next())
                act.activation(o_sb, bank[:, :], ACT.Copy).then_inc(to_act.free, 1)
                act.wait_ge(to_act.free, to_act.own_reads())
                act.sem_inc(osq_ready.sem, 1)
                act.sem_inc(o_ready.sem, 1)
                act.wait_ge(to_act.full, to_act.next_full())
                bank = to_act.take()
                act.activation(o_std, bank[:, :], ACT.Sqrt, scale=1.0 / DV, bias=eps_col[:, 0:1]).then_inc(to_act.free, 1)
                act.wait_ge(to_act.free, to_act.own_reads())
                act.sem_inc(ostd_ready.sem, 1)

        S5_DT, S5_MAG, S5_TH = 0, 1, 2
        S5_C, S5_S, S5_T = 4, 13, 22
        b_pad = [part(i * 2048, S5_PAIRS, P) for i in range(2)]
        b_nat = [part(4096 + i * 256, S5_PAIRS, 16) for i in range(2)]
        c_nat = [part(4608 + i * 512, 4, P) for i in range(2)]
        b_bar = [part(5632 + i * 256, S5_PAIRS, 16) for i in range(2)]
        s5_b = [part(8192 + i * 2048, S5_PAIRS, P) for i in range(2)]
        s5_c = [part(12288 + i * 2048, S5_PAIRS, P) for i in range(2)]
        s5_tab = [[part((2 * b + i) * 512, T) for i in range(2)] for b in range(2)]
        w1, w2, w3, pool_tmp = (part(2048 + i * 512, T) for i in range(4))
        x_out = [[part(4096 + (2 * b + i) * 512, T) for i in range(2)] for b in range(2)]
        gate_tmp = part(0, 4, T)
        s5_parts = hidden[:, 4:8, :]
        base_c, base_s, base_t = (s5_parts[:, :, o:o + P].rearrange("p q (m n) -> p q m n", n=32)
                                  for o in (0, P, 3 * P))
        step_c, step_s = (s5_parts[:, :, o:o + 64].rearrange("p q (m n) -> p q m n", n=16)
                          for o in (2 * P, 2 * P + 64))
        mod_row2 = con("chunk_keep")
        y_banks = Banks(psum[0:2], sem("s5_y_banks_full"), sem("s5_y_banks_free"))
        mod_banks = Banks(psum[2:4], sem("mod_banks_full"), sem("mod_banks_free"))

        def pool_s5_steps(pool):
            for half in range(2):
                pool.dma_start(s5c[64 * half:64 * half + 64, S5_DT, :],
                               a["s5_log_dt"].rearrange("a (g two) -> two a g", two=2)[half]
                               .broadcast_to([64, S5_PAIRS]),
                               allow_slow_non_contiguous=True).then_inc(s5_steps.sem, 16)

        def pool_s5_loads(pool):
            pool.wait_ge(gla_out.sem, gla_out.next(pool, GLA_HEADS))
            for half in range(2):
                rows64 = slice(64 * half, 64 * half + 64)
                for i, name in enumerate(("s5_b_re", "s5_b_im")):
                    pool.dma_start(b_nat[i][rows64, :, :],
                                 a[name][0].rearrange("(g two) p h -> two p g h", two=2)[half])\
                      .then_inc(s5_loaded.sem, 16)
                for i, name in enumerate(("s5_c_re", "s5_c_im")):
                    pool.dma_start(c_nat[i][:, :, 64 * half:64 * half + 64],
                                 a[name][0].rearrange("(q g) h p -> (g h) q p", q=4)).then_inc(s5_loaded.sem, 16)

        def act_s5_angles(act, step):
            act.wait_ge(s5_steps.sem, s5_steps.next(act, 32))
            v = lambda i: s5c[:, i, :]
            act.activation(v(S5_DT), v(S5_DT), ACT.Exp).then_inc(act_done, 1)
            act.wait_ge(act_done, step.next())
            act.sem_inc(s5_cols.sem, 1)
            act.wait_ge(s5_dve.sem, s5_dve.next(act))
            act.activation(v(S5_MAG), v(S5_MAG), ACT.Exp).then_inc(act_done, 1)
            act.wait_ge(act_done, step.next())
            act.activation(v(S5_S), v(S5_T), ACT.Sin).then_inc(act_done, 1)
            act.wait_ge(act_done, step.next())
            act.activation(v(S5_C), v(S5_T + 1), ACT.Sin).then_inc(act_done, 1)
            act.wait_ge(act_done, step.next())
            act.sem_inc(s5_cols.sem, 1)

        def act_s5_setup(act, step):
            for i in range(2):
                for q4 in range(4):
                    act.wait_ge(to_act.full, to_act.next_full())
                    bank = to_act.take()
                    act.activation(s5_b[i][:, 4 * q4:4 * q4 + 4, :], bank[:, :].rearrange("p (m c) -> p m c", c=P),
                                   ACT.Copy).then_inc(to_act.free, 1)
            act.wait_ge(to_act.free, to_act.own_reads())
            act.sem_inc(s5_blocks.sem, 1)

        def dve_s5_angles(dve, step):
            v = lambda i: s5c[:, i, :]
            tt = lambda o, x, y, op: dve.tensor_tensor(o, x, y, op)
            ts = lambda o, x, s1, o1, s2=None, o2=None: (
                dve.tensor_scalar(o, x, s1, s2, o1, o2) if o2 is not None else dve.tensor_scalar(o, x, s1, None, o1))
            lr, li = col("s5_lambda_re"), col("s5_lambda_im")
            dve.wait_ge(s5_cols.sem, s5_cols.next(dve))
            tt(v(S5_TH), li, v(S5_DT), ALU.mult).then_inc(dve_done, 1)
            dve.wait_ge(dve_done, step.next())
            tt(v(S5_MAG), lr, v(S5_DT), ALU.mult).then_inc(dve_done, 1)
            dve.wait_ge(dve_done, step.next())
            MAGIC, C1 = 12582912.0, 6.28125
            C2, EDGE = 2 * np.pi - C1, 3.1415925
            for k in range(2):
                r, n = v(S5_T + k), v(S5_T + 2)
                ts(n, v(S5_TH), 1 / (2 * np.pi), ALU.mult, 0.25 * k, ALU.add).then_inc(dve_done, 1)
                dve.wait_ge(dve_done, step.next())
                ts(n, n, MAGIC, ALU.add).then_inc(dve_done, 1)
                dve.wait_ge(dve_done, step.next())
                ts(n, n, MAGIC, ALU.subtract).then_inc(dve_done, 1)
                dve.wait_ge(dve_done, step.next())
                dve.scalar_tensor_tensor(r, n, -C1, v(S5_TH), ALU.mult, ALU.add).then_inc(dve_done, 1)
                dve.wait_ge(dve_done, step.next())
                dve.scalar_tensor_tensor(r, n, -C2, r, ALU.mult, ALU.add).then_inc(dve_done, 1)
                dve.wait_ge(dve_done, step.next())
                ts(r, r, k * np.pi / 2, ALU.add, EDGE, ALU.min).then_inc(dve_done, 1)
                dve.wait_ge(dve_done, step.next())
                ts(r, r, -EDGE, ALU.max).then_inc(dve_done, 1)
                dve.wait_ge(dve_done, step.next())
            dve.sem_inc(s5_dve.sem, 1)
            dve.wait_ge(s5_cols.sem, s5_cols.next(dve))
            t0, t1, t2, t3 = (v(S5_T + i) for i in range(4))
            for level in range(9):
                c, s = v(S5_C + level), v(S5_S + level)
                if level:
                    pc, ps = v(S5_C + level - 1), v(S5_S + level - 1)
                    tt(t0, pc, pc, ALU.mult).then_inc(dve_done, 1)
                    dve.wait_ge(dve_done, step.next())
                    tt(t1, ps, ps, ALU.mult).then_inc(dve_done, 1)
                    dve.wait_ge(dve_done, step.next())
                    tt(c, t0, t1, ALU.subtract).then_inc(dve_done, 1)
                    dve.wait_ge(dve_done, step.next())
                    tt(s, pc, ps, ALU.mult).then_inc(dve_done, 1)
                    dve.wait_ge(dve_done, step.next())
                    ts(s, s, 2.0, ALU.mult).then_inc(dve_done, 1)
                    dve.wait_ge(dve_done, step.next())
                tt(t0, c, c, ALU.mult).then_inc(dve_done, 1)
                dve.wait_ge(dve_done, step.next())
                tt(t1, s, s, ALU.mult).then_inc(dve_done, 1)
                dve.wait_ge(dve_done, step.next())
                tt(t0, t0, t1, ALU.add).then_inc(dve_done, 1)
                dve.wait_ge(dve_done, step.next())
                ts(t0, t0, -0.5, ALU.mult, 1.5, ALU.add).then_inc(dve_done, 1)
                dve.wait_ge(dve_done, step.next())
                tt(c, c, t0, ALU.mult).then_inc(dve_done, 1)
                dve.wait_ge(dve_done, step.next())
                tt(s, s, t0, ALU.mult).then_inc(dve_done, 1)
                dve.wait_ge(dve_done, step.next())
            dve.sem_inc(s5_table.sem, 1)
            are, aim, den = t0, t1, t2
            tt(are, v(S5_MAG), v(S5_C), ALU.mult).then_inc(dve_done, 1)
            dve.wait_ge(dve_done, step.next())
            ts(are, are, -1.0, ALU.add).then_inc(dve_done, 1)
            dve.wait_ge(dve_done, step.next())
            tt(aim, v(S5_MAG), v(S5_S), ALU.mult).then_inc(dve_done, 1)
            dve.wait_ge(dve_done, step.next())
            tt(den, lr, lr, ALU.mult).then_inc(dve_done, 1)
            dve.wait_ge(dve_done, step.next())
            tt(t3, li, li, ALU.mult).then_inc(dve_done, 1)
            dve.wait_ge(dve_done, step.next())
            tt(den, den, t3, ALU.add).then_inc(dve_done, 1)
            dve.wait_ge(dve_done, step.next())
            dve.reciprocal(den, den).then_inc(dve_done, 1)
            dve.wait_ge(dve_done, step.next())
            fre, fim, t6 = v(S5_T + 4), v(S5_T + 5), v(S5_T + 6)
            tt(fre, are, lr, ALU.mult).then_inc(dve_done, 1)
            dve.wait_ge(dve_done, step.next())
            tt(t6, aim, li, ALU.mult).then_inc(dve_done, 1)
            dve.wait_ge(dve_done, step.next())
            tt(fre, fre, t6, ALU.add).then_inc(dve_done, 1)
            dve.wait_ge(dve_done, step.next())
            tt(fre, fre, den, ALU.mult).then_inc(dve_done, 1)
            dve.wait_ge(dve_done, step.next())
            tt(fim, aim, lr, ALU.mult).then_inc(dve_done, 1)
            dve.wait_ge(dve_done, step.next())
            tt(t6, are, li, ALU.mult).then_inc(dve_done, 1)
            dve.wait_ge(dve_done, step.next())
            tt(fim, fim, t6, ALU.subtract).then_inc(dve_done, 1)
            dve.wait_ge(dve_done, step.next())
            tt(fim, fim, den, ALU.mult).then_inc(dve_done, 1)
            dve.wait_ge(dve_done, step.next())

        def dve_s5_setup(dve, step):
            v = lambda i: s5c[:, i, :]
            tt = lambda o, x, y, op: dve.tensor_tensor(o, x, y, op)
            for i in range(2):
                dve.memset(b_pad[i], 0.0).then_inc(dve_done, 1)
                dve.wait_ge(dve_done, step.next())
                dve.memset(s5_c[i], 0.0).then_inc(dve_done, 1)
                dve.wait_ge(dve_done, step.next())
            for q4 in range(4):
                dve.tensor_scalar(s5_dd[:, q4, :], ident, col("s5_d", q4, 1), None, ALU.mult).then_inc(dve_done, 1)
                dve.wait_ge(dve_done, step.next())
            dve.wait_ge(s5_loaded.sem, s5_loaded.next(dve, 16 * 8))
            fre, fim = v(S5_T + 4), v(S5_T + 5)
            wide = lambda x: x.rearrange("p (g h) -> p g h", h=1).broadcast_to([P, S5_PAIRS, 16])
            tmp = part(12288 - 256, S5_PAIRS, 16)
            for o, f1, f2, op in ((0, fre, fim, ALU.subtract), (1, fim, fre, ALU.add)):
                tt(b_bar[o], b_nat[0], wide(f1), ALU.mult).then_inc(dve_done, 1)
                dve.wait_ge(dve_done, step.next())
                tt(tmp, b_nat[1], wide(f2), ALU.mult).then_inc(dve_done, 1)
                dve.wait_ge(dve_done, step.next())
                tt(b_bar[o], b_bar[o], tmp, op).then_inc(dve_done, 1)
                dve.wait_ge(dve_done, step.next())
            for i in range(2):
                for m in range(4):
                    for par in range(2):
                        half, c0 = slice(64 * par, 64 * par + 64), 32 * m + 16 * par
                        dve.tensor_copy(b_pad[i][half, m::4, c0:c0 + 16], b_bar[i][half, m::4, :])\
                            .then_inc(dve_done, 1)
                        dve.wait_ge(dve_done, step.next())
            dve.sem_inc(s5_dve.sem, 1)
            for i in range(2):
                dve.wait_ge(to_dve.full, to_dve.next_full())
                bank = to_dve.take()
                b4 = bank[:, :].rearrange("p (q c) -> p q c", c=P)
                for m in range(4):
                    for par in range(2):
                        half, c0 = slice(64 * par, 64 * par + 64), 32 * m + 16 * par
                        ins = dve.tensor_scalar(s5_c[i][half, m::4, c0:c0 + 16], b4[half, :, c0:c0 + 16],
                                                -1.0 if i else 1.0, None, ALU.mult)
                        if m == 3 and par == 1:
                            ins.then_inc(to_dve.free, 1)
                        else:
                            ins.then_inc(dve_done, 1)
                            dve.wait_ge(dve_done, step.next())
            dve.wait_ge(to_dve.free, to_dve.own_reads())
            dve.sem_inc(s5_blocks.sem, 1)

        def pe_s5(pe, mm):
            pe.wait_ge(s5_loaded.sem, s5_loaded.next(pe, 16 * 8))
            for i in range(2):
                pe.wait_ge(to_dve.free, to_dve.room())
                bank = to_dve.fill()
                for q4 in range(4):
                    ins = mm.transpose(bank[:, q4 * P:(q4 + 1) * P], c_nat[i][:, q4, :], ident)
                    if q4 == 3:
                        ins.then_inc(to_dve.full, 1)
            pe.wait_ge(s5_dve.sem, s5_dve.next(pe, 2))
            for i in range(2):
                for q4 in range(4):
                    pe.wait_ge(to_act.free, to_act.room())
                    bank = to_act.fill()
                    for m in range(4):
                        ins = mm.transpose(bank[:, m * P:(m + 1) * P], b_pad[i][:, 4 * q4 + m, :], ident)
                        if m == 3:
                            ins.then_inc(to_act.full, 1)
            pe.wait_ge(s5_blocks.sem, s5_blocks.next(pe, 2))
            held = None

            def outputs(p):
                nonlocal held
                q4 = p // 4
                if p % 4 == 0:
                    pe.wait_ge(y_banks.free, y_banks.room())
                    held = y_banks.fill()
                    mm(held[:, :], s5_dd[:, q4, :], u_t[:, q4, :], True, False)
                pe.wait_ge(s5_x.sem, s5_x.next(pe))
                for i in range(2):
                    ins = mm(held[:, :], s5_c[i][:, p, :], x_out[p % 2][i], False, p % 4 == 3 and i == 1)
                    if p % 4 == 3 and i == 1:
                        ins.then_inc(y_banks.full, 1)
                mm.done(s5_y.sem)

            pe.wait_ge(to_act.free, to_act.all_sent())
            for p in range(S5_PAIRS):
                for i in range(2):
                    pe.wait_ge(to_dve.free, to_dve.room())
                    bank = to_dve.fill()
                    mm(bank[:, :], s5_b[i][:, p, :], u_t[:, p // 4, :]).then_inc(to_dve.full, 1)
                if p < MOD_PANELS:
                    pe_mod_row(pe, mm, mod_banks, c_second, 2)
                if p:
                    outputs(p - 1)
                if p < MOD_PANELS:
                    pe_mod_turn(pe, mm, mod_banks, mod_row2, 2)
            outputs(S5_PAIRS - 1)
            pe.wait_ge(s5_gelu.sem, s5_gelu.next(pe, 4))
            pe.wait_ge(mod_banks.free, mod_banks.all_sent())
            pe_linear(pe, mm, to_act, hidden[:, 4:8, :], T, 4, 512)

        def pool_s5(pool, step):
            pool.wait_ge(s5_table.sem, s5_table.next(pool))
            for c, s, first, levels in ((base_c, base_s, 0, 5), (step_c, step_s, 5, 4)):
                pool.memset(c[:, :, :, 0:1], 1.0).then_inc(pool_done, 1)
                pool.memset(s[:, :, :, 0:1], 0.0).then_inc(pool_done, 1)
                pool.wait_ge(pool_done, step.next(2))
                for level in range(levels):
                    n = 1 << level
                    cl, sl = (s5c[:, i + first + level, :].rearrange("p (q m n) -> p q m n", q=4, n=1)
                              .broadcast_to([P, 4, 4, n]) for i in (S5_C, S5_S))
                    t0, t1 = base_t[:, :, :, 0:n], base_t[:, :, :, 16:16 + n]
                    c0, s0 = c[:, :, :, 0:n], s[:, :, :, 0:n]
                    pool.tensor_tensor(t0, c0, cl, ALU.mult).then_inc(pool_done, 1)
                    pool.tensor_tensor(t1, s0, sl, ALU.mult).then_inc(pool_done, 1)
                    pool.wait_ge(pool_done, step.next(2))
                    pool.tensor_tensor(c[:, :, :, n:2 * n], t0, t1, ALU.subtract).then_inc(pool_done, 1)
                    pool.wait_ge(pool_done, step.next())
                    pool.tensor_tensor(t0, c0, sl, ALU.mult).then_inc(pool_done, 1)
                    pool.tensor_tensor(t1, s0, cl, ALU.mult).then_inc(pool_done, 1)
                    pool.wait_ge(pool_done, step.next(2))
                    pool.tensor_tensor(s[:, :, :, n:2 * n], t0, t1, ALU.add).then_inc(pool_done, 1)
                    pool.wait_ge(pool_done, step.next())
            pool.wait_ge(s5_blocks.sem, s5_blocks.next(pool, 2))
            t0 = pool_tmp.rearrange("p (a b) -> p a b", b=32)
            for p in range(S5_PAIRS):
                q, m = p // 4, p % 4
                c, s = (x.rearrange("p (a b) -> p a b", b=32) for x in s5_tab[p % 2])
                cb, sb_ = (s5_parts[:, q, o + 32 * m:o + 32 * m + 32].rearrange("p (a b) -> p a b", a=1)
                           .broadcast_to([P, 16, 32]) for o in (0, P))
                ca, sa = (s5_parts[:, q, o + 16 * m:o + 16 * m + 16].rearrange("p (a b) -> p a b", b=1)
                          .broadcast_to([P, 16, 32]) for o in (2 * P, 2 * P + 64))
                if p >= 2:
                    pool.wait_ge(s5_table_used.sem, s5_table_used.next(pool))
                pool.tensor_tensor(t0, sa, sb_, ALU.mult).then_inc(pool_done, 1)
                pool.tensor_tensor(c, ca, cb, ALU.mult).then_inc(pool_done, 1)
                pool.wait_ge(pool_done, step.next(2))
                pool.tensor_tensor(c, c, t0, ALU.subtract).then_inc(pool_done, 1)
                pool.wait_ge(pool_done, step.next())
                pool.tensor_tensor(t0, sa, cb, ALU.mult).then_inc(pool_done, 1)
                pool.tensor_tensor(s, ca, sb_, ALU.mult).then_inc(pool_done, 1)
                pool.wait_ge(pool_done, step.next(2))
                pool.tensor_tensor(s, s, t0, ALU.add).then_inc(pool_done, 1)
                pool.wait_ge(pool_done, step.next())
                pool.sem_inc(s5_tab_ready.sem, 1)

        def dve_s5(dve, step):
            tt = lambda o, x, y, op: dve.tensor_tensor(o, x, y, op)
            for p in range(S5_PAIRS):
                c, s = s5_tab[p % 2]
                dve.wait_ge(s5_tab_ready.sem, s5_tab_ready.next(dve))
                mag = s5c[:, S5_MAG, p:p + 1].broadcast_to([P, T])
                dve.wait_ge(to_dve.full, to_dve.next_full())
                b_re = to_dve.take()[:, :]
                dve.wait_ge(to_dve.full, to_dve.next_full())
                b_im = to_dve.take()[:, :]
                tt(w1, b_re, c, ALU.mult).then_inc(dve_done, 1)
                tt(w2, b_im, s, ALU.mult).then_inc(dve_done, 1)
                dve.wait_ge(dve_done, step.next(2))
                tt(w1, w1, w2, ALU.add).then_inc(dve_done, 1)
                tt(w3, b_im, c, ALU.mult).then_inc(dve_done, 1)
                dve.wait_ge(dve_done, step.next(2))
                z_re, z_im = w2, w1
                dve.tensor_tensor_scan(z_re, mag, w1, 0.0, ALU.mult, ALU.add).then_inc(dve_done, 1)
                dve.wait_ge(dve_done, step.next())
                tt(w1, b_re, s, ALU.mult).then_inc(dve_done, 1)
                dve.wait_ge(dve_done, step.next())
                dve.sem_inc(to_dve.free, 2)
                tt(w3, w3, w1, ALU.subtract).then_inc(dve_done, 1)
                dve.wait_ge(dve_done, step.next())
                dve.tensor_tensor_scan(z_im, mag, w3, 0.0, ALU.mult, ALU.add).then_inc(dve_done, 1)
                x_re, x_im = x_out[p % 2]
                if p >= 2:
                    dve.wait_ge(s5_y.sem, s5_y.next(dve))
                tt(x_re, z_re, c, ALU.mult).then_inc(dve_done, 1)
                dve.wait_ge(dve_done, step.next(2))
                tt(w3, z_im, s, ALU.mult).then_inc(dve_done, 1)
                tt(x_im, z_re, s, ALU.mult).then_inc(dve_done, 1)
                dve.wait_ge(dve_done, step.next(2))
                tt(x_re, x_re, w3, ALU.subtract).then_inc(dve_done, 1)
                tt(w2, z_im, c, ALU.mult).then_inc(dve_done, 1)
                dve.wait_ge(dve_done, step.next(2))
                tt(x_im, x_im, w2, ALU.add).then_inc(dve_done, 1)
                dve.wait_ge(dve_done, step.next())
                dve.sem_inc(s5_x.sem, 1)
                dve.sem_inc(s5_table_used.sem, 1)
            dve_mod_bias(dve, step, mods2, col("b_mod_2"), 2)
            dve.wait_ge(s5_gate.sem, s5_gate.next(dve))
            dve.tensor_tensor(hidden[:, 4:8, :], hidden[:, 4:8, :], gate_tmp, ALU.mult).then_inc(dve_done, 1)
            dve.wait_ge(dve_done, step.next())
            dve.sem_inc(s5_out.sem, 1)

        def act_s5(act, step):
            for p in range(S5_PAIRS + 1):
                if p < MOD_PANELS:
                    act_mod_row(act, mod_banks, mod_row2, 2)
                if p and p % 4 == 0:
                    q4 = p // 4 - 1
                    act.wait_ge(y_banks.full, y_banks.next_full())
                    bank = y_banks.take()
                    act.activation(hidden[:, 4 + q4, :], bank[:, :], ACT.Gelu_apprx_tanh).then_inc(y_banks.free, 1)
                    act.wait_ge(y_banks.free, y_banks.own_reads())
                    act.sem_inc(s5_gelu.sem, 1)
                if p < MOD_PANELS:
                    act_mod_turn(act, mod_banks, mods2, p, 2)
            act.wait_ge(mod_banks.free, mod_banks.own_reads())
            act.sem_inc(mod_cols.sem, 1)
            for m in range(4):
                act.wait_ge(to_act.full, to_act.next_full())
                bank = to_act.take()
                act.activation(gate_tmp[:, m, :], bank[:, :], ACT.Sigmoid, bias=col("s5_glu_b", m, 1)).then_inc(to_act.free, 1)
            act.wait_ge(to_act.free, to_act.own_reads())
            act.sem_inc(s5_gate.sem, 1)

        mix = part(0, DT, T)
        m_sq, m_std = part(4096, DT, T), part(8192, T)

        def pe_project_out(pe, mm):
            pe.wait_ge(s5_out.sem, s5_out.next(pe))
            pe.wait_ge(gla_out.sem, gla_out.next(pe, GLA_HEADS))
            pe_linear(pe, mm, to_act, hidden, T, DT, 512)
            pe_linear(pe, mm, to_act, hidden, T, DT, 512)

        def dve_add_normed(dve, step, branch, std, gains):
            dve.wait_ge(std_ready.sem, std_ready.next(dve))
            dve.reciprocal(std, std).then_inc(dve_done, 1)
            dve.wait_ge(dve_done, step.next())
            for k in range(DT + 1):
                if k < DT:
                    dve.scalar_tensor_tensor(branch[:, k, :], branch[:, k, :], gains[:, k:k + 1], std,
                                             ALU.mult, ALU.mult).then_inc(dve_done, 1)
                if k:
                    dve.wait_ge(dve_done, step.next())
                    dve.tensor_tensor(resid[:, k - 1, :], resid[:, k - 1, :], branch[:, k - 1, :], ALU.add)\
                        .then_inc(resid_tile.sem, 1)
            dve.wait_ge(resid_tile.sem, resid_tile.next(dve, DT))
            dve.sem_inc(resid_ready.sem, 1)
        n2_sq, n2_std = part(0, DT, T), part(4096, T)

        hn_tok = part(0, TT, D)
        xg2 = [part(4096, DT, S), part(8192, DT, S)]
        xg = xg2[0]
        gb, ub, sg = part(5120, DT, S), part(6144, DT, S), part(7168, DT, S)
        sel = part(8192, TT, S)
        selg = con("chunk_keep").rearrange("p (t s) -> p t s", s=S)
        selgt = part(SELGT_AT, T)
        y_sb = part(Y_AT, D)
        bgu = part(10752, NE, 16)
        POS = NE + 2
        posm, gate = part(11264, POS, TT), part(11400, POS, TT)
        bdown = part(12288, D)
        router_w = part(13312, DT, NE)
        router_b = part(13568, NE)
        r_at = [13600]

        def r_part(*shape):
            v = part(r_at[0], *shape)
            r_at[0] += int(np.prod(shape))
            return v

        logits, cur, hot, cand, chosen, expo, im64 = (r_part(TT, NE) for _ in range(7))
        row_max, row_min, top, total = (r_part(TT) for _ in range(4))
        counts_f, extra_n, extra_c, x_e, x_b, x_t = (r_part(NE) for _ in range(6))
        cmp_t = r_part(16, NE)
        gate_t = part(15360 + 256, T)
        slot_gate = row_max[:, 0:1]
        assert r_at[0] <= 15616, r_at
        bgu_rows = part(5120, 2 * DFF)
        extra_e = sb("extra_expert", [1, 16], I32)
        extra_b = sb("extra_block", [1, 16], I32)

        router_loaded = signal("router_loaded")
        router_dve = signal("router_dve")
        router_act = signal("router_act")
        moe_sel = signal("moe_sel")
        moe_selg = signal("moe_selg")
        moe_gm = signal("moe_gm")
        moe_sig = signal("moe_sig")
        moe_act = signal("moe_act")
        moe_start = signal("moe_start")
        hn_ready = signal("hn_ready")
        hn_lo_ready = signal("hn_lo_ready")
        moe_panels = Panels(slots[0:MOE_SLOTS], [sem(f"moe_panel{i}_loaded") for i in range(MOE_SLOTS)],
                            [sem(f"moe_panel{i}_used") for i in range(MOE_SLOTS)])
        for c in moe_panels.loads:
            c.n = 1
        moe_gate = signal("moe_gate")
        moe_y_hi = signal("moe_y_hi")
        moe_y_lo = signal("moe_y_lo")
        moe_done = signal("moe_done")
        moe_a = Banks(psum[0:2], sem("moe_act_full"), sem("moe_act_free"))
        moe_d = Banks(psum[2:6], sem("moe_dve_full"), sem("moe_dve_free"))
        moe_t = Banks(psum[6:7], sem("moe_turned_full"), sem("moe_turned_free"))
        turn = sem("extra_turn")
        extra_w = sem("extra_weights")

        def pool_moe_loads(pool):
            pool.wait_ge(resid_ready.sem, resid_ready.next(pool, 2))
            pool.dma_start(router_w, a["router_w"][0].rearrange("(k p) e -> p k e", p=P)).then_inc(router_loaded.sem, 16)
            pool.dma_start(router_b, a["router_b"].broadcast_to([P, NE])).then_inc(router_loaded.sem, 16)
            pool.dma_start(bdown[0:NE, :], a["exp_b_down"][0]).then_inc(router_loaded.sem, 16)
            pool.dma_start(bgu_rows[0:NE, :], a["exp_b_gu"][0]).then_inc(router_loaded.sem, 16)

        def pe_route(pe, mm):
            pe.wait_ge(router_loaded.sem, router_loaded.next(pe, 64))
            pe.wait_ge(normed.sem, normed.next(pe, DT))
            for used in moe_panels.used:
                pe.sem_inc(used, 1)
            pe.wait_ge(to_dve.free, to_dve.room())
            bank = to_dve.fill()
            for t in range(TT):
                for k in range(DT):
                    ins = mm(bank[:, t * NE:(t + 1) * NE], hidden[:, k, t * P:(t + 1) * P],
                             router_w[:, k, :], k == 0, k == DT - 1)
                    if t == TT - 1 and k == DT - 1:
                        ins.then_inc(to_dve.full, 1)
            for t in range(TT):
                for g in range(2):
                    pe.wait_ge(to_act.free, to_act.room())
                    bank = to_act.fill()
                    for m in range(4):
                        ins = mm.transpose(bank[:, m * P:(m + 1) * P], hidden[:, 4 * g + m, t * P:(t + 1) * P], ident)
                        if m == 3:
                            ins.then_inc(to_act.full, 1)
            pe.wait_ge(to_act.free, to_act.room())
            bank = to_act.fill()
            for f in range(16):
                ins = mm.transpose(bank[:, f * NE:(f + 1) * NE], bgu_rows[0:NE, f * P:(f + 1) * P], ident[0:NE, 0:NE])
                if f == 15:
                    ins.then_inc(to_act.full, 1)
            pe.wait_ge(router_dve.sem, router_dve.next(pe, 2))
            pe.wait_ge(to_dve.free, to_dve.room())
            bank = to_dve.fill()
            for t in range(TT):
                for s in range(t + 1):
                    mm(bank[:, t * NE:(t + 1) * NE], con("upper") if s == t else ones, chosen[:, s, :], s == 0, s == t)
            for s in range(TT):
                ins = mm(bank[:, P:P + NE], ones, chosen[:, s, :], s == 0, s == TT - 1)
                if s == TT - 1:
                    ins.then_inc(to_dve.full, 1)
            pe.wait_ge(router_dve.sem, router_dve.next(pe))
            pe.wait_ge(to_dve.free, to_dve.room())
            bank = to_dve.fill()
            for t in range(TT):
                ins = mm.transpose(bank[0:NE, t * P:(t + 1) * P], cand[:, t, :], ident)
                if t == TT - 1:
                    ins.then_inc(to_dve.full, 1)
            pe.wait_ge(to_dve.free, to_dve.all_sent())
            pe.wait_ge(to_act.free, to_act.all_sent())
            for m in range(DT):
                pe.wait_ge(to_dve.free, to_dve.room())
                bank = to_dve.fill()
                mm(bank[:, :], bdown[0:NE, m * P:(m + 1) * P], gate_t[0:NE, :]).then_inc(to_dve.full, 1)
            pe.wait_ge(to_dve.free, to_dve.all_sent())

        def pool_split_tokens(pool):
            for t in range(TT):
                pool.wait_ge(hn_ready.sem, hn_ready.next(pool))
                pool.tensor_tensor(hn_lo[:, t, :], hn_tok[:, t, :], hn_hi[:, t, :].bitcast(F32), ALU.subtract)\
                    .then_inc(hn_lo_ready.sem, 1)

        def act_route(act, step):
            for t in range(TT):
                for g in range(2):
                    act.wait_ge(to_act.full, to_act.next_full())
                    bank = to_act.take()
                    act.activation(hn_tok[:, t, g * 512:(g + 1) * 512], bank[:, :], ACT.Copy).then_inc(to_act.free, 1)
                act.wait_ge(to_act.free, to_act.own_reads())
                act.activation(hn_hi[:, t, :], hn_tok[:, t, :], ACT.Copy).then_inc(hn_ready.sem, 1)
            act.wait_ge(to_act.full, to_act.next_full())
            bank = to_act.take()
            act.activation(bgu.rearrange("p e f -> p f e"), bank[:, :].rearrange("p (f e) -> p f e", e=NE),
                           ACT.Copy).then_inc(to_act.free, 1)
            act.wait_ge(to_act.free, to_act.own_reads())
            act.sem_inc(router_act.sem, 1)
            act.wait_ge(router_dve.sem, router_dve.next(act))
            act.activation(expo, expo, ACT.Exp).then_inc(act_done, 1)
            act.wait_ge(act_done, step.next())
            act.sem_inc(router_act.sem, 1)
            act.sem_inc(moe_a.free, len(moe_a.banks))

        def wide_e(x):
            return x.rearrange("p (t e) -> p t e", e=1).broadcast_to([P, TT, NE])

        def dve_route(dve, step):
            tt = lambda o, x, y, op: dve.tensor_tensor(o, x, y, op)
            ts = lambda o, x, s1, o1: dve.tensor_scalar(o, x, s1, None, o1)
            dve.wait_ge(router_loaded.sem, router_loaded.next(dve, 64))
            iota_e = con("iota", NE).rearrange("p (t e) -> p t e", t=1).broadcast_to([P, TT, NE])
            dve.wait_ge(to_dve.full, to_dve.next_full())
            bank = to_dve.take()
            dve.tensor_tensor(logits, bank[:, 0:P].rearrange("p (t e) -> p t e", e=NE),
                              router_b.rearrange("p (t e) -> p t e", t=1).broadcast_to([P, TT, NE]), ALU.add)\
               .then_inc(to_dve.free, 1)
            dve.wait_ge(to_dve.free, to_dve.own_reads())
            ts(im64, iota_e, -64.0, ALU.add).then_inc(dve_done, 1)
            dve.wait_ge(dve_done, step.next())
            dve.tensor_copy(cur, logits).then_inc(dve_done, 1)
            dve.wait_ge(dve_done, step.next())
            for i in range(TOPK):
                dve.tensor_reduce(row_max, cur, AX_X, ALU.max).then_inc(dve_done, 1)
                dve.wait_ge(dve_done, step.next())
                if i == 0:
                    dve.tensor_copy(top, row_max).then_inc(dve_done, 1)
                    dve.wait_ge(dve_done, step.next())
                    tt(expo, logits, wide_e(top), ALU.subtract).then_inc(dve_done, 1)
                    dve.wait_ge(dve_done, step.next())
                    dve.sem_inc(router_dve.sem, 1)
                tt(hot, cur, wide_e(row_max), ALU.is_equal).then_inc(dve_done, 1)
                dve.wait_ge(dve_done, step.next())
                tt(hot, hot, im64, ALU.mult).then_inc(dve_done, 1)
                dve.wait_ge(dve_done, step.next())
                dve.tensor_reduce(row_min, hot, AX_X, ALU.min).then_inc(dve_done, 1)
                dve.wait_ge(dve_done, step.next())
                tt(hot, im64, wide_e(row_min), ALU.is_equal).then_inc(dve_done, 1)
                dve.wait_ge(dve_done, step.next())
                if i == 0:
                    dve.tensor_copy(chosen, hot).then_inc(dve_done, 1)
                    dve.wait_ge(dve_done, step.next())
                else:
                    tt(chosen, chosen, hot, ALU.add).then_inc(dve_done, 1)
                    dve.wait_ge(dve_done, step.next())
                dve.scalar_tensor_tensor(cur, hot, NEG, cur, ALU.mult, ALU.add).then_inc(dve_done, 1)
                dve.wait_ge(dve_done, step.next())
            dve.sem_inc(router_dve.sem, 1)
            dve.wait_ge(router_act.sem, router_act.next(dve, 2))
            tt(cand, expo, chosen, ALU.mult).then_inc(dve_done, 1)
            dve.wait_ge(dve_done, step.next())
            dve.tensor_reduce(total, cand, AX_X, ALU.add).then_inc(dve_done, 1)
            dve.wait_ge(dve_done, step.next())
            dve.reciprocal(total, total).then_inc(dve_done, 1)
            dve.wait_ge(dve_done, step.next())
            tt(cand, cand, wide_e(total), ALU.mult).then_inc(dve_done, 1)
            dve.wait_ge(dve_done, step.next())
            dve.sem_inc(router_dve.sem, 1)
            dve.tensor_copy(gate[:, 0:NE, :].rearrange("p e t -> p t e"), cand).then_inc(dve_done, 1)
            dve.wait_ge(dve_done, step.next())
            dve.memset(gate[:, NE:POS, :], 0.0).then_inc(dve_done, 1)
            dve.wait_ge(dve_done, step.next())
            dve.wait_ge(to_dve.full, to_dve.next_full())
            bank = to_dve.take()
            tt(hot, bank[:, 0:P].rearrange("p (t e) -> p t e", e=NE), chosen, ALU.mult).then_inc(dve_done, 1)
            dve.wait_ge(dve_done, step.next())
            dve.tensor_copy(counts_f[0:1, :], bank[0:1, P:P + NE]).then_inc(to_dve.free, 1)
            dve.wait_ge(to_dve.free, to_dve.own_reads())
            ts(posm[:, 0:NE, :].rearrange("p e t -> p t e"), hot, -1.0, ALU.add).then_inc(dve_done, 1)
            dve.wait_ge(dve_done, step.next())
            dve.memset(posm[:, NE:POS, :], -1.0).then_inc(dve_done, 1)
            dve.wait_ge(dve_done, step.next())
            dve.wait_ge(to_dve.full, to_dve.next_full())
            bank = to_dve.take()
            dve.tensor_copy(gate_t[0:NE, :], bank[0:NE, :]).then_inc(to_dve.free, 1)
            dve.wait_ge(to_dve.free, to_dve.own_reads())
            for m in range(DT):
                dve.wait_ge(to_dve.full, to_dve.next_full())
                bank = to_dve.take()
                dve.tensor_copy(hidden[:, m, :], bank[:, :]).then_inc(to_dve.free, 1)
            dve.wait_ge(to_dve.free, to_dve.own_reads())
            n1, c1 = extra_n[0:1, :], extra_c[0:1, :]
            ts(n1, counts_f[0:1, :], float(S), ALU.is_gt).then_inc(dve_done, 1)
            dve.wait_ge(dve_done, step.next())
            for b in range(2, XBLOCKS):
                dve.tensor_scalar(x_t[0:1, :], counts_f[0:1, :], float(b * S), None, ALU.is_gt)\
                    .then_inc(dve_done, 1)
                dve.wait_ge(dve_done, step.next())
                tt(n1, n1, x_t[0:1, :], ALU.add).then_inc(dve_done, 1)
                dve.wait_ge(dve_done, step.next())
            dve.tensor_tensor_scan(c1, ones[0:1, 0:NE], n1, 0.0, ALU.mult, ALU.add).then_inc(dve_done, 1)
            dve.wait_ge(dve_done, step.next())
            cj = c1.rearrange("p (j e) -> p j e", j=1).broadcast_to([1, 16, NE])
            jj = con("iota", 16)[0:1, :].rearrange("p (j e) -> p j e", e=1).broadcast_to([1, 16, NE])
            ct = cmp_t[0:1, :, :]
            xe, xb, xt = x_e[0:1, 0:16], x_b[0:1, 0:16], x_t[0:1, 0:16]
            tt(ct, cj, jj, ALU.is_le)\
                .then_inc(dve_done, 1)
            dve.wait_ge(dve_done, step.next())
            dve.tensor_reduce(xe, ct, AX_X, ALU.add).then_inc(dve_done, 1)
            dve.wait_ge(dve_done, step.next())
            tt(ct, ct, n1.rearrange("p (j e) -> p j e", j=1).broadcast_to([1, 16, NE]), ALU.mult)\
                .then_inc(dve_done, 1)
            dve.wait_ge(dve_done, step.next())
            dve.tensor_reduce(xb, ct, AX_X, ALU.add).then_inc(dve_done, 1)
            dve.wait_ge(dve_done, step.next())
            tt(xb, con("iota", 16)[0:1, :], xb, ALU.subtract).then_inc(dve_done, 1)
            dve.wait_ge(dve_done, step.next())
            ts(xb, xb, 1.0, ALU.add).then_inc(dve_done, 1)
            dve.wait_ge(dve_done, step.next())
            ts(xt, xe, float(NE), ALU.is_lt).then_inc(dve_done, 1)
            dve.wait_ge(dve_done, step.next())
            tt(xb, xb, xt, ALU.mult).then_inc(dve_done, 1)
            dve.wait_ge(dve_done, step.next())
            tt(xe, xe, xt, ALU.mult).then_inc(dve_done, 1)
            dve.wait_ge(dve_done, step.next())
            dve.tensor_copy(extra_e[:, :], xe).then_inc(dve_done, 1)
            dve.wait_ge(dve_done, step.next())
            dve.tensor_copy(extra_b[:, :], xb).then_inc(dve_done, 1)
            dve.wait_ge(dve_done, step.next())
            dve.memset(y_hi[:, :].bitcast(F32), 0.0).then_inc(dve_done, 1)
            dve.wait_ge(dve_done, step.next())
            dve.memset(y_lo[:, :].bitcast(F32), 0.0).then_inc(dve_done, 1)
            dve.wait_ge(dve_done, step.next())
            dve.memset(tokens_r[:, :].bitcast(F32), 0.0).then_inc(dve_done, 1)
            dve.wait_ge(dve_done, step.next())
            dve.sem_inc(moe_d.free, len(moe_d.banks))
            dve.sem_inc(moe_t.free, len(moe_t.banks))
            for h in range(2):
                dve_select(dve, step, h, h)
            dve.sem_inc(moe_start.sem, 1)
            dve.sem_inc(moe_sel.sem, 1)

        PAIRS = 2

        iota_slots = con("iota").rearrange("p (t s) -> p t s", t=1).broadcast_to([P, TT, S])

        def slots_of(x):
            return x.rearrange("p (t s) -> p t s", s=1).broadcast_to([P, TT, S])

        def expert_column(x, e):
            v = x[:, bass.ds(e, 1), :]
            return v.rearrange("p e t -> p (e t)")

        def dve_select(dve, step, e, h):
            dve.tensor_tensor(sel2[:, :, h * S:(h + 1) * S], iota_slots, slots_of(expert_column(posm, e)),
                              ALU.is_equal).then_inc(dve_done, 1)
            dve.wait_ge(dve_done, step.next())

        def pe_gather(pe, mm):
            for g in range(4):
                pe.wait_ge(moe_a.free, moe_a.room())
                bank = moe_a.fill()
                for m in range(2):
                    col = slice((2 * g + m) * P, (2 * g + m + 1) * P)
                    dst = bank[:, m * 2 * S:(m + 1) * 2 * S]
                    for t in range(TT):
                        mm(dst, hn_hi[:, t, col], sel2[:, t, :], t == 0, False)
                        ins = mm(dst, hn_lo[:, t, col], sel2[:, t, :], False, t == TT - 1)
                        if m == 1 and t == TT - 1:
                            ins.then_inc(moe_a.full, 1)

        def act_gathered(act):
            for g in range(4):
                act.wait_ge(moe_a.full, moe_a.next_full())
                bank = moe_a.take()[:, :].rearrange("p (m h s) -> p m h s", m=2, h=2)
                act.activation(xg2[0][:, 2 * g:2 * g + 2, :], bank[:, :, 0, :], ACT.Copy)
                act.activation(xg2[1][:, 2 * g:2 * g + 2, :], bank[:, :, 1, :], ACT.Copy).then_inc(moe_a.free, 1)

        def pe_up(pe, mm, x, n_panels):
            for _ in range(n_panels):
                s, w = moe_panels.use(DT, 512)
                pe.wait_ge(moe_panels.loaded[s], moe_panels.arrived(s))
                pe.wait_ge(moe_d.free, moe_d.room())
                bank = moe_d.fill()
                for f in range(4):
                    for k in range(DT):
                        ins = mm(bank[:, f * S:(f + 1) * S], w[:, k, f * P:(f + 1) * P],
                                 x[:, k, :], k == 0, k == DT - 1)
                        if f == 3 and k == DT - 1:
                            ins.then_inc(moe_d.full, 1)
                mm.done(moe_panels.used[s])

        def pe_moe(pe, mm):
            pe.wait_ge(moe_start.sem, moe_start.next(pe))
            pe.wait_ge(moe_sel.sem, moe_sel.next(pe))
            pe.wait_ge(hn_lo_ready.sem, hn_lo_ready.next(pe, TT))
            pe_gather(pe, mm)
            pe.wait_ge(moe_a.free, moe_a.all_sent())
            counts = [moe_a.sent, moe_d.sent, moe_t.sent, moe_sel.count(pe), moe_selg.count(pe), moe_act.count(pe),
                      *moe_panels.arrivals]
            turns = [8, 24, 2, 1, 2, 2] + [3 * 16] * MOE_SLOTS
            with pe.Fori(0, NE // (2 * PAIRS)) as turn_no:
                for c, n in zip(counts, turns):
                    c.enter(turn_no, PAIRS * n)
                for _ in range(PAIRS):
                    pe.wait_ge(moe_a.free, moe_a.all_sent(but=2))
                    for h in range(2):
                        pe_up(pe, mm, xg2[h], 3)
                        pe.wait_ge(moe_a.free, moe_a.all_sent())
                        pe_give_out(pe, mm, 0, DT // 2)
                        pe_up(pe, mm, xg2[h], 1)
                        if h == 1:
                            pe.wait_ge(moe_sel.sem, moe_sel.next(pe))
                            pe_gather(pe, mm)
                        pe_give_out(pe, mm, DT // 2, DT)
                        pe.wait_ge(moe_selg.sem, moe_selg.next(pe))
                        pe.wait_ge(moe_t.free, moe_t.room())
                        bank = moe_t.fill()
                        for t in range(TT):
                            ins = mm.transpose(bank[:, t * P:(t + 1) * P], selg[:, t, :], ident)
                            if t == TT - 1:
                                ins.then_inc(moe_t.full, 1)
                        pe.wait_ge(moe_act.sem, moe_act.next(pe))
                        for half in range(2):
                            s, w = moe_panels.use(DT, 512)
                            pe.wait_ge(moe_panels.loaded[s], moe_panels.arrived(s))
                            pe.wait_ge(moe_a.free, moe_a.room())
                            bank = moe_a.fill()
                            for k in range(DT):
                                ins = mm(bank[:, :], ub[:, k, :], w[:, k, :], k == 0, k == DT - 1)
                                if k == DT - 1:
                                    ins.then_inc(moe_a.full, 1)
                            mm.done(moe_panels.used[s])
                mm.settle()
                for c in counts:
                    c.leave(NE // (2 * PAIRS))
            pe.wait_ge(moe_a.free, moe_a.all_sent())
            pe_give_out(pe, mm, 0, DT)
            pe.wait_ge(moe_d.free, moe_d.all_sent())

        def pe_give_out(pe, mm, m0, m1):
            for m in range(m0, m1):
                pe.wait_ge(moe_d.free, moe_d.room())
                bank = moe_d.fill()
                mm(bank[:, :], y_hi[:, m * P:(m + 1) * P], tokens_r[:, :], True, False)
                mm(bank[:, :], y_lo[:, m * P:(m + 1) * P], tokens_r[:, :], False, True).then_inc(moe_d.full, 1)

        def sp_moe(sp):
            with sp.Fori(0, NE // (2 * PAIRS)) as turn_no:
                for c in moe_panels.loads:
                    c.enter(turn_no, PAIRS * 3)
                for q in range(PAIRS):
                    pair = turn_no * PAIRS + q
                    for h in range(2):
                        e = pair * 2 + h
                        for p in range(4):
                            moe_panels.load(sp, expert_dram(a["exp_w_gu"], e)[:, p * 512:(p + 1) * 512])
                        for p in range(2):
                            moe_panels.load(sp, expert_dram(a["exp_w_down"], e)[:, p * 512:(p + 1) * 512])
                for c in moe_panels.loads:
                    c.leave(NE // (2 * PAIRS))

        def expert_dram(w, e):
            return w[0, bass.ds(e, 1), :, :].rearrange("e r c -> (e r) c")

        def act_moe(act, step):
            counts = [step.count, moe_a.read, moe_gm.count(act), moe_y_lo.count(act), moe_gate.count(act)]
            act_gathered(act)
            with act.Fori(0, NE // (2 * PAIRS)) as turn_no:
                for c, n in zip(counts, [2, 8, 2, 4, 2]):
                    c.enter(turn_no, PAIRS * n)
                for _ in range(PAIRS):
                    for h in range(2):
                        act.wait_ge(moe_gm.sem, moe_gm.next(act))
                        act.activation(sg, gb, ACT.Sigmoid, scale=ALPHA).then_inc(act_done, 1)
                        act.wait_ge(act_done, step.next())
                        act.sem_inc(moe_sig.sem, 1)
                        if h == 1:
                            act_gathered(act)
                        act.wait_ge(moe_gate.sem, moe_gate.next(act))
                        for half in range(2):
                            act.wait_ge(moe_a.full, moe_a.next_full())
                            bank = moe_a.take()
                            act.activation(y_hi[:, half * 512:(half + 1) * 512], bank[:, :], ACT.Copy,
                                           scale=slot_gate).then_inc(moe_y_hi.sem, 1)
                        act.wait_ge(moe_y_lo.sem, moe_y_lo.next(act, 2))
                        act.sem_inc(moe_a.free, 2)
                for c in counts:
                    c.leave(NE // (2 * PAIRS))
            act.wait_ge(moe_a.free, moe_a.own_reads())

        def bias_of(e, first):
            v = bgu[:, bass.ds(e, 1), first:first + 4].rearrange("p e f -> p (e f)")
            return v.rearrange("p (f s) -> p f s", s=1).broadcast_to([P, 4, S])

        def dve_moe(dve, step):
            counts = [step.count, moe_d.read, moe_sig.count(dve), moe_y_hi.count(dve), moe_t.read]
            with dve.Fori(0, NE // (2 * PAIRS)) as turn_no:
                for c, n in zip(counts, [16, 24, 2, 4, 2]):
                    c.enter(turn_no, PAIRS * n)
                for q in range(PAIRS):
                    pair = turn_no * PAIRS + q
                    for h in range(2):
                        e = pair * 2 + h
                        for g in range(2):
                            dve.wait_ge(moe_d.full, moe_d.next_full())
                            bank = moe_d.take()
                            dve.tensor_tensor(gb[:, 4 * g:4 * g + 4, :], bank[:, :].rearrange("p (f s) -> p f s", s=S),
                                              bias_of(e, 4 * g), ALU.add).then_inc(moe_d.free, 1)
                        dve.wait_ge(moe_d.free, moe_d.own_reads())
                        dve.tensor_scalar(gb, gb, LIMIT, None, ALU.min).then_inc(dve_done, 1)
                        dve.wait_ge(dve_done, step.next())
                        dve.sem_inc(moe_gm.sem, 1)
                        if h == 0:
                            for i in range(2):
                                dve_select(dve, step, pair * 2 + 2 + i, i)
                            dve.sem_inc(moe_sel.sem, 1)
                        dve.tensor_tensor(selg, iota_slots, slots_of(expert_column(posm, e)), ALU.is_equal)\
                            .then_inc(dve_done, 1)
                        dve.wait_ge(dve_done, step.next())
                        dve.tensor_tensor(selg, selg, slots_of(expert_column(gate, e)), ALU.mult).then_inc(dve_done, 1)
                        dve.wait_ge(dve_done, step.next())
                        dve.sem_inc(moe_selg.sem, 1)
                        for g in range(2):
                            dve.wait_ge(moe_d.full, moe_d.next_full())
                            bank = moe_d.take()
                            dve.tensor_tensor(ub[:, 4 * g:4 * g + 4, :], bank[:, :].rearrange("p (f s) -> p f s", s=S),
                                              bias_of(e, 8 + 4 * g), ALU.add).then_inc(moe_d.free, 1)
                            if g == 0:
                                dve_give_out(dve, moe_d, 0, DT // 2)
                        dve.wait_ge(moe_d.free, moe_d.own_reads())
                        dve.tensor_scalar(ub, ub, LIMIT, -LIMIT, ALU.min, ALU.max).then_inc(dve_done, 1)
                        dve.wait_ge(dve_done, step.next())
                        dve.scalar_tensor_tensor(ub, ub, 1.0, gb, ALU.add, ALU.mult).then_inc(dve_done, 1)
                        dve.wait_ge(dve_done, step.next())
                        dve.wait_ge(moe_sig.sem, moe_sig.next(dve))
                        dve.tensor_tensor(ub, ub, sg, ALU.mult).then_inc(dve_done, 1)
                        dve.wait_ge(dve_done, step.next())
                        dve.sem_inc(moe_act.sem, 1)
                        dve_give_out(dve, moe_d, DT // 2, DT)
                        dve.wait_ge(moe_t.full, moe_t.next_full())
                        bank = moe_t.take()
                        dve.tensor_reduce(slot_gate, bank[:, :], AX_X, ALU.add).then_inc(dve_done, 1)
                        dve.wait_ge(dve_done, step.next())
                        dve.sem_inc(moe_gate.sem, 1)
                        dve.tensor_scalar(tokens_r[:, :], bank[:, :], 0.0, None, ALU.is_gt).then_inc(moe_t.free, 1)
                        for half in range(2):
                            bank = moe_a.banks[half]
                            dve.wait_ge(moe_y_hi.sem, moe_y_hi.next(dve))
                            cc = slice(half * 512, (half + 1) * 512)
                            dve.scalar_tensor_tensor(y_lo[:, cc], bank[:, :], slot_gate, y_hi[:, cc].bitcast(F32),
                                                     ALU.mult, ALU.subtract).then_inc(moe_y_lo.sem, 1)
                for c in counts:
                    c.leave(NE // (2 * PAIRS))
            dve_give_out(dve, moe_d, 0, DT)
            dve.wait_ge(moe_d.free, moe_d.own_reads())

        def dve_give_out(dve, banks, m0, m1):
            for m in range(m0, m1):
                dve.wait_ge(banks.full, banks.next_full())
                bank = banks.take()
                dve.tensor_tensor(hidden[:, m, :], hidden[:, m, :], bank[:, :], ALU.add).then_inc(banks.free, 1)

        STAGES, LOADS = 11, 16 * 6

        def extra_blocks(eng, taken, skipped=None, first=0):
            with eng.Fori(first, 16) as j:
                block_no = eng.value_load(extra_b[0:1, bass.ds(j, 1)], min_val=0, max_val=XBLOCKS - 1)
                with eng.If(block_no > 0):
                    e = eng.value_load(extra_e[0:1, bass.ds(j, 1)], min_val=0, max_val=NE - 1)
                    taken(j, e, block_no)
                if skipped is not None:
                    with eng.Else():
                        skipped(j)
                eng.end_ifs()

        def stage(j, s):
            return j * STAGES + s + 1

        def sp_extra(sp):
            def load(e, i):
                w = expert_dram(a["exp_w_gu"] if i < 4 else a["exp_w_down"], e)
                src = w[:, (i % 4) * 512:(i % 4 + 1) * 512].rearrange("(k p) c -> p k c", p=P)
                return sp.dma_start(slots[i % 4][:, :].rearrange("p (k c) -> p k c", k=DT), src)

            sp.wait_ge(moe_start.sem, moe_start.next(sp))
            block_no = sp.value_load(extra_b[0:1, 0:1], min_val=0, max_val=XBLOCKS - 1)
            with sp.If(block_no > 0):
                e = sp.value_load(extra_e[0:1, 0:1], min_val=0, max_val=NE - 1)
                for i in range(6):
                    if i < 4:
                        sp.wait_ge(moe_panels.used[i], moe_panels.loads[i].value())
                    else:
                        sp.wait_ge(turn, stage(0, 4))
                    load(e, i).then_inc(extra_w, 16)
            with sp.Else():
                sp.sem_inc(extra_w, LOADS)
            sp.end_ifs()
            sp.wait_ge(moe_done.sem, moe_done.next(sp, 3))

            def taken(j, e, b):
                sp.wait_ge(turn, stage(j, 0))
                for i in range(6):
                    if i == 4:
                        sp.wait_ge(turn, stage(j, 4))
                    load(e, i).then_inc(extra_w, 16)

            def skipped(j):
                sp.wait_ge(turn, stage(j, 0))
                sp.sem_inc(extra_w, LOADS)

            extra_blocks(sp, taken, skipped, first=1)

        def dve_extra(dve, step):
            dve.sem_inc(moe_done.sem, 1)
            dve.wait_ge(moe_done.sem, moe_done.next(dve, 3))
            dve.sem_inc(turn, 1)

            def taken(j, e, b):
                dve.wait_ge(turn, stage(j, 0))
                pos = total
                chain = TurnOrder(j, 9)
                dve.tensor_scalar(pos, expert_column(posm, e), con("block_start")[:, bass.ds(b, 1)], None, ALU.subtract)\
                    .then_inc(extra_dve, 1)
                dve.wait_ge(extra_dve, chain.next())
                dve.tensor_tensor(sel, iota_slots, slots_of(pos), ALU.is_equal).then_inc(extra_dve, 1)
                dve.wait_ge(extra_dve, chain.next())
                dve.tensor_tensor(selg, sel, slots_of(expert_column(gate, e)), ALU.mult).then_inc(extra_dve, 1)
                dve.wait_ge(extra_dve, chain.next())
                dve.sem_inc(turn, 1)
                dve.wait_ge(turn, stage(j, 4))
                for g in range(2):
                    dve.tensor_tensor(gb[:, 4 * g:4 * g + 4, :], psum[3 + g][:, :].rearrange("p (f s) -> p f s", s=S),
                                      bias_of(e, 4 * g), ALU.add)
                    ins = dve.tensor_tensor(ub[:, 4 * g:4 * g + 4, :], psum[5 + g][:, :].rearrange("p (f s) -> p f s", s=S),
                                            bias_of(e, 8 + 4 * g), ALU.add)
                ins.then_inc(extra_dve, 1)
                dve.wait_ge(extra_dve, chain.next())
                dve.tensor_scalar(gb, gb, LIMIT, None, ALU.min).then_inc(extra_dve, 1)
                dve.wait_ge(extra_dve, chain.next())
                dve.tensor_scalar(ub, ub, LIMIT, -LIMIT, ALU.min, ALU.max).then_inc(extra_dve, 1)
                dve.wait_ge(extra_dve, chain.next())
                dve.scalar_tensor_tensor(ub, ub, 1.0, gb, ALU.add, ALU.mult).then_inc(extra_dve, 1)
                dve.wait_ge(extra_dve, chain.next())
                dve.sem_inc(turn, 1)
                dve.wait_ge(turn, stage(j, 6))
                dve.tensor_tensor(ub, ub, sg, ALU.mult).then_inc(extra_dve, 1)
                dve.wait_ge(extra_dve, chain.next())
                dve.sem_inc(turn, 1)
                dve.wait_ge(turn, stage(j, 10))
                for m in range(DT):
                    ins = dve.tensor_tensor(hidden[:, m, :], hidden[:, m, :], psum[m][:, :], ALU.add)
                ins.then_inc(extra_dve, 1)
                dve.wait_ge(extra_dve, chain.next())
                chain.end()
                dve.sem_inc(turn, 1)

            def skipped(j):
                dve.sem_inc(extra_dve, 9)
                dve.sem_inc(turn, STAGES)

            extra_blocks(dve, taken, skipped)
            dve.wait_ge(turn, 16 * STAGES + 1)

        def pe_extra(pe, mm):
            pe.sem_inc(moe_done.sem, 1)
            pe.wait_ge(moe_done.sem, moe_done.next(pe, 3))

            def taken(j, e, b):
                pe.wait_ge(turn, stage(j, 1))
                for g in range(2):
                    for m in range(4):
                        for t in range(TT):
                            mm(psum[g][:, m * S:(m + 1) * S], hn_tok[:, t, (4 * g + m) * P:(4 * g + m + 1) * P],
                               sel[:, t, :], t == 0, t == TT - 1)
                for t in range(TT):
                    ins = mm.transpose(psum[2][:, t * P:(t + 1) * P], selg[:, t, :], ident)
                    if t == TT - 1:
                        ins.then_inc(turn, 1)
                pe.wait_ge(turn, stage(j, 3))
                pe.wait_ge(extra_w, j * LOADS + 16 * 4)
                for i in range(4):
                    w = slots[i][:, :].rearrange("p (k c) -> p k c", k=DT)
                    for f in range(4):
                        for k in range(DT):
                            last = i == 3 and f == 3 and k == DT - 1
                            ins = mm(psum[3 + i][:, f * S:(f + 1) * S], w[:, k, f * P:(f + 1) * P],
                                     xg[:, k, :], k == 0, k == DT - 1)
                            if last:
                                ins.then_inc(turn, 1)
                pe.wait_ge(turn, stage(j, 7))
                pe.wait_ge(extra_w, j * LOADS + LOADS)
                for i in range(2):
                    w = slots[i][:, :].rearrange("p (k c) -> p k c", k=DT)
                    for k in range(DT):
                        ins = mm(psum[i][:, :], ub[:, k, :], w[:, k, :], k == 0, k == DT - 1)
                        if i == 1 and k == DT - 1:
                            ins.then_inc(turn, 1)
                pe.wait_ge(turn, stage(j, 9))
                for m in range(DT):
                    ins = mm(psum[m][:, :], y_sb[:, m * P:(m + 1) * P], selgt)
                    if m == DT - 1:
                        ins.then_inc(turn, 1)

            extra_blocks(pe, taken)

        def act_extra(act, step):
            act.sem_inc(moe_done.sem, 1)
            act.wait_ge(moe_done.sem, moe_done.next(act, 3))

            def taken(j, e, b):
                chain = TurnOrder(j, 3)
                act.wait_ge(turn, stage(j, 2))
                for g in range(2):
                    act.activation(xg[:, 4 * g:4 * g + 4, :], psum[g][:, :].rearrange("p (m s) -> p m s", s=S), ACT.Copy)
                act.activation(selgt, psum[2][:, :], ACT.Copy).then_inc(extra_act, 1)
                act.wait_ge(extra_act, chain.next())
                act.sem_inc(turn, 1)
                act.wait_ge(turn, stage(j, 5))
                act.activation(sg, gb, ACT.Sigmoid, scale=ALPHA).then_inc(extra_act, 1)
                act.wait_ge(extra_act, chain.next())
                act.sem_inc(turn, 1)
                act.wait_ge(turn, stage(j, 8))
                act.activation(y_sb[:, 0:512], psum[0][:, :], ACT.Copy)
                act.activation(y_sb[:, 512:1024], psum[1][:, :], ACT.Copy).then_inc(extra_act, 1)
                act.wait_ge(extra_act, chain.next())
                chain.end()
                act.sem_inc(turn, 1)

            def skipped(j):
                act.sem_inc(extra_act, 3)

            extra_blocks(act, taken, skipped)

        extra_dve, extra_act = sem("extra_dve_order"), sem("extra_act_order")

        panels2 = Panels(slots[0:4], [sem(f"panel2_{i}_loaded") for i in range(4)],
                         [sem(f"panel2_{i}_used") for i in range(4)])
        freed = [slots[i][:, :] for i in (4, 5)]
        xs_tok, y_tok = (v.rearrange("p (t d) -> p t d", d=D) for v in freed)
        row_vecs = sb("row_vectors", [P, 88])
        dt_bias, a_log, ssm_d, sink = row_vecs[:, 0:32], row_vecs[:, 32:64], row_vecs[:, 64:80], row_vecs[:, 80:88]
        qk_gain = sb("qk_gain", [P, 2])
        rows2_loaded = signal("rows2_loaded")
        ctx_loaded = signal("ctx_loaded")
        rope_loaded = signal("rope_loaded")
        A1X, A1C, A2X = (small[:, 32 + 8 * i:40 + 8 * i] for i in range(3))

        hc = part(0, DT, CTX)
        ctx_tok = part(2048, CT, D)
        ctx_t = part(4096, DT, CTX)
        c_sq, c_std = part(6144, DT, CTX), part(8192, CTX)
        x_sq, x_std = part(8704, DT, T), part(12800, T)

        def sp_second_loads(sp):
            sp.wait_ge(turn, 16 * STAGES + 1)
            sp.dma_start(ctx_tok, a["ctx_2"][0].rearrange("(t p) d -> p t d", p=P)).then_inc(ctx_loaded.sem, 16)
            w = a["w_in_2"][0]
            load = lambda src: panels2.load(sp, src)
            load(w[:, 3328:3360])
            for p in range(3):
                load(w[:, 1792 + p * 512:1792 + (p + 1) * 512])
            for p in range(2):
                load(w[:, 768 + p * 512:768 + (p + 1) * 512])
            for c0 in (0, 3360):
                load(w[:, c0:c0 + 512])
                load(w[:, c0 + 512:c0 + 768])
            for half in range(2):
                c = slice(half * 512, (half + 1) * 512)
                for i, name in enumerate(("w_oa_2", "w_ob_2", "w_oc_2")):
                    g0 = 4128 + i * D + half * 512
                    load(w[:, g0:g0 + 512])
                    load(a[name][0][:, c])
            for half in range(2):
                load(a["w_out_2"][0][:, half * 512:(half + 1) * 512])
            for c0, c1 in FFN_PANELS:
                load(a["ffn_w_gate_2"][0][:, c0:c1])
                load(a["ffn_w_up_2"][0][:, c0:c1])
            for half in range(2):
                for r0, r1 in DOWN_ROWS:
                    load(a["ffn_w_down_2"][0][r0 * P:r1 * P, half * 512:(half + 1) * 512])

        FFN_PANELS = [(c, min(c + 512, DFF2)) for c in range(0, DFF2, 512)]
        DOWN_ROWS = [(r, min(r + 8, FT2)) for r in range(0, FT2, 8)]

        def pool_row_loads(pool):
            for dst, name in ((dt_bias, "ssm_dt_bias_2"), (a_log, "ssm_A_log_2"), (ssm_d, "ssm_D_2"), (sink, "a_sink_2")):
                v = flat(name)
                pool.dma_start(dst, v.rearrange("(a n) -> a n", a=1).broadcast_to([P, v.shape[0]]))\
                    .then_inc(rows2_loaded.sem, 16)
            for i, name in enumerate(QK_NORMS):
                for half in range(2):
                    pool.dma_start(qk_gain[64 * half:64 * half + 64, i:i + 1], flat(name).rearrange("(p n) -> p n", n=1),
                                   allow_slow_non_contiguous=True).then_inc(rows2_loaded.sem, 16)

        def pe_second_norms(pe, mm):
            pe.wait_ge(ctx_loaded.sem, ctx_loaded.next(pe, 16))
            for m in range(DT):
                pe.wait_ge(to_dve.free, to_dve.room())
                bank = to_dve.fill()
                for t in range(CT):
                    ins = mm.transpose(bank[:, t * P:(t + 1) * P], ctx_tok[:, t, m * P:(m + 1) * P], ident)
                    if t == CT - 1:
                        ins.then_inc(to_dve.full, 1)
            pe_norm(pe, mm, c_sq, CTX, DT)
            pe_norm(pe, mm, x_sq, T, DT)

        def dve_second_norms(dve, step):
            for m in range(DT):
                dve.wait_ge(to_dve.full, to_dve.next_full())
                bank = to_dve.take()
                dve.tensor_copy(ctx_t[:, m, :], bank[:, 0:CTX]).then_inc(to_dve.free, 1)
            dve.wait_ge(to_dve.free, to_dve.own_reads())
            for factor, gain, m, which in ((A1X, "norm1_2", 8, 0), (A1C, "norm1_2", 8, 1), (A2X, "norm2_2", 32, 0)):
                dve.scalar_tensor_tensor(factor, mods2[:, m:m + 8, which], 1.0, col(gain), ALU.add, ALU.mult)\
                    .then_inc(dve_done, 1)
                dve.wait_ge(dve_done, step.next())
            dve.sem_inc(resid_ready.sem, 1)
            dve_norm(dve, step, ctx_t, hc, c_std, DT, A1C)
            dve_norm(dve, step, resid, hidden, x_std, DT, A1X)

        def act_second_norms(act, step):
            act.wait_ge(resid_ready.sem, resid_ready.next(act, 3))
            act_norm(act, step, ctx_t, c_sq, c_std, CTX, DT, D, [mods2[:, k, 1:2] for k in range(DT)], hc)
            act_norm(act, step, resid[:, :, :], x_sq, x_std, T, DT, D, [mods2[:, k, 0:1] for k in range(DT)], hidden,
                     after=resid_tile)

        NC, NH = TT + CT, SSM_HEADS
        ctx_xs = part(2048, CT, D)
        b_t, c_t = part(4096, 2, T), part(5120, 2, T)
        b_tok, b_ctx = part(6144, TT, 256), part(7168, CT, 256)
        h_state = [part(7680 + i * 1024, NH, SSM_P) for i in range(2)]
        s_at = [9728]

        def s_part(*shape):
            v = part(s_at[0], *shape)
            s_at[0] += int(np.prod(shape))
            return v

        d_t, d_ta, acs, e_acs, w_end, e_tot = (s_part(2, NC * NH) for _ in range(6))
        SSM_TMP = 10880
        assert s_at[0] <= SSM_TMP
        conv_x = part(SSM_TMP, 4, T)
        conv_ctx = part(SSM_TMP + 2048, 4, CTX)
        conv = [part(SSM_TMP + 3072 + i * T, T) for i in range(2)]
        decay = [part(SSM_TMP + i * 1024, 8, P) for i in range(2)]
        cb = part(SSM_TMP + 2048, 2, P)
        xdt, xw = part(SSM_TMP + 2304, D), part(SSM_TMP + 3328, D)
        y_part = part(SSM_TMP + 4352, T)

        dt_z = signal("dt_z")
        dt_act = signal("dt_act")
        dt_dve = signal("dt_dve")
        conv_ready = signal("conv_ready")
        conv_silu = signal("conv_silu")
        xs_ready = signal("xs_ready")
        ssm_x = signal("ssm_x")
        ssm_seg = signal("ssm_seg")
        ssm_exp = signal("ssm_exp")
        ssm_probs = signal("ssm_probs")
        ssm_h = signal("ssm_h")
        z_ready = signal("z_ready")
        z_used = signal("z_used")
        y_sq = signal("y_sq")
        y_normed = signal("y_normed")
        ys_ready = signal("ys_ready")

        def by_dir(x):
            return x.rearrange("p d (c h) -> p d c h", h=NH)

        def pe_dt(pe, mm):
            pe.wait_ge(normed.sem, normed.next(pe, 2 * DT))
            s, w = panels2.use(DT, 32)
            pe.wait_ge(panels2.loaded[s], panels2.arrived(s))
            pe.wait_ge(to_dve.free, to_dve.room())
            bank = to_dve.fill()
            for c in range(NC):
                src, t = (hidden, c) if c < TT else (hc, c - TT)
                for k in range(DT):
                    ins = mm(bank[:, c * 32:(c + 1) * 32], src[:, k, t * P:(t + 1) * P],
                             w[:, k, :], k == 0, k == DT - 1)
                    if c == NC - 1 and k == DT - 1:
                        ins.then_inc(to_dve.full, 1)
            mm.done(panels2.used[s])

        def pe_dt_sums(pe, mm):
            pe.wait_ge(dt_dve.sem, dt_dve.next(pe))
            pe.wait_ge(to_dve.free, to_dve.room())
            bank = to_dve.fill()
            n = NC * NH
            mm(bank[:, 0:n], con("upper"), d_ta[:, 0, :])
            mm(bank[:, n:2 * n], con("lower"), d_ta[:, 1, :])
            mm(bank[:, 2 * n:4 * n], ones, d_ta.rearrange("p d n -> p (d n)")).then_inc(to_dve.full, 1)

        def dve_dt(dve, step):
            dve.wait_ge(rows2_loaded.sem, rows2_loaded.next(dve, 16 * 8))
            dve.wait_ge(to_dve.full, to_dve.next_full())
            bank = to_dve.take()
            out4 = by_dir(d_t)
            for d in range(2):
                ins = dve.tensor_tensor(out4[:, d, :, :], bank[:, 0:32 * NC].rearrange("p (c x) -> p c x", x=32)[:, :, d * NH:(d + 1) * NH],
                                        dt_bias[:, d * NH:(d + 1) * NH].rearrange("p (c h) -> p c h", c=1).broadcast_to([P, NC, NH]),
                                        ALU.add)
                if d:
                    ins.then_inc(to_dve.free, 1)
                else:
                    ins.then_inc(dve_done, 1)
                    dve.wait_ge(dve_done, step.next())
            dve.wait_ge(to_dve.free, to_dve.own_reads())
            dve.sem_inc(dt_z.sem, 1)
            dve.wait_ge(dt_act.sem, dt_act.next(dve))
            dve.scalar_tensor_tensor(d_t, d_t, 0.0, acs, ALU.max, ALU.add).then_inc(dve_done, 1)
            dve.wait_ge(dve_done, step.next())
            for d in range(2):
                dve.scalar_tensor_tensor(by_dir(d_ta)[:, d, :, :], by_dir(d_t)[:, d, :, :], -1.0,
                                         a_log[:, d * NH:(d + 1) * NH].rearrange("p (c h) -> p c h", c=1).broadcast_to([P, NC, NH]),
                                         ALU.mult, ALU.mult).then_inc(dve_done, 1)
                dve.wait_ge(dve_done, step.next())
            dve.sem_inc(dt_dve.sem, 1)

        def dve_dt_sums(dve, step):
            n = NC * NH
            dve.wait_ge(to_dve.full, to_dve.next_full())
            bank = to_dve.take()
            flat2 = lambda x: x.rearrange("p d n -> p (d n)")
            dve.tensor_copy(flat2(acs), bank[:, 0:2 * n]).then_inc(dve_done, 1)
            dve.wait_ge(dve_done, step.next())
            dve.tensor_copy(flat2(e_tot), bank[:, 2 * n:4 * n]).then_inc(to_dve.free, 1)
            dve.wait_ge(to_dve.free, to_dve.own_reads())
            dve.tensor_tensor(w_end, e_tot, acs, ALU.subtract).then_inc(dve_done, 1)
            dve.wait_ge(dve_done, step.next())
            dve.sem_inc(dt_z.sem, 1)
            dve.wait_ge(dt_act.sem, dt_act.next(dve))
            dve.tensor_tensor(w_end, w_end, d_t, ALU.mult).then_inc(dve_done, 1)
            dve.wait_ge(dve_done, step.next())

        def act_dt(act, step):
            act.wait_ge(dt_z.sem, dt_z.next(act))
            act.activation(acs, d_t, ACT.Abs).then_inc(act_done, 1)
            act.wait_ge(act_done, step.next())
            act.activation(acs, acs, ACT.Exp, scale=-1.0).then_inc(act_done, 1)
            act.wait_ge(act_done, step.next())
            act.activation(acs, acs, ACT.Ln, bias=1.0).then_inc(act_done, 1)
            act.wait_ge(act_done, step.next())
            act.activation(a_log, a_log, ACT.Exp).then_inc(act_done, 1)
            act.wait_ge(act_done, step.next())
            act.sem_inc(dt_act.sem, 1)

        def act_dt_sums(act, step):
            act.wait_ge(dt_z.sem, dt_z.next(act))
            act.activation(e_acs, acs, ACT.Exp).then_inc(act_done, 1)
            act.wait_ge(act_done, step.next())
            act.activation(w_end, w_end, ACT.Exp).then_inc(act_done, 1)
            act.wait_ge(act_done, step.next())
            act.activation(e_tot, e_tot, ACT.Exp).then_inc(act_done, 1)
            act.wait_ge(act_done, step.next())
            act.sem_inc(dt_act.sem, 1)

        def conv_tiles(panel):
            tiles = []
            for m in range(4):
                j = 4 * panel + m
                tiles.append(((conv_x[:, m, :] if panel < 2 else (b_t if m < 2 else c_t)[:, m % 2, :]), T, j))
                if j < 10:
                    tiles.append((conv_ctx[:, m, :], CTX, j))
            return tiles

        def pe_xbc(pe, mm):
            for panel in range(3):
                s, w = panels2.use(DT, 512)
                pe.wait_ge(panels2.loaded[s], panels2.arrived(s))
                for _, n, j in conv_tiles(panel):
                    src = hidden if n == T else hc
                    m = j % 4
                    pe.wait_ge(to_dve.free, to_dve.room())
                    bank = to_dve.fill()
                    for k in range(DT):
                        ins = mm(bank[:, 0:n], w[:, k, m * P:(m + 1) * P], src[:, k, :], k == 0, k == DT - 1)
                        if k == DT - 1:
                            ins.then_inc(to_dve.full, 1)
                mm.done(panels2.used[s])
                if panel == 0:
                    pe_dt_sums(pe, mm)
                for dst, n, j in conv_tiles(panel):
                    pe.wait_ge(conv_silu.sem, conv_silu.next(pe))
                    if j >= 10:
                        continue
                    pe.wait_ge(to_act.free, to_act.room())
                    bank = to_act.fill()
                    for t in range(n // P):
                        ins = mm.transpose(bank[:, t * P:(t + 1) * P], dst[:, t * P:(t + 1) * P], ident)
                        if t == n // P - 1:
                            ins.then_inc(to_act.full, 1)
            pe.wait_ge(to_act.free, to_act.all_sent())

        def dve_conv(dve, step, bank, dst, n, w, bias):
            dve.tensor_scalar(dst[:, 0:n], bank[:, 0:n], w[1], bias, ALU.mult, ALU.add).then_inc(dve_done, 1)
            dve.wait_ge(dve_done, step.next())
            dve.scalar_tensor_tensor(dst[:, 1:n], bank[:, 0:n - 1], w[0], dst[:, 1:n], ALU.mult, ALU.add)\
                .then_inc(dve_done, 1)
            dve.wait_ge(dve_done, step.next())
            dve.scalar_tensor_tensor(dst[:, 0:n - 1], bank[:, 1:n], w[2], dst[:, 0:n - 1], ALU.mult, ALU.add)\
               .then_inc(to_dve.free, 1)
            dve.wait_ge(to_dve.free, to_dve.own_reads())
            dve.sem_inc(conv_ready.sem, 1)

        def dve_xbc(dve, step):
            n_done = 0
            for panel in range(3):
                for _, n, j in conv_tiles(panel):
                    dve.wait_ge(to_dve.full, to_dve.next_full())
                    bank = to_dve.take()
                    if n_done >= 2:
                        dve.wait_ge(conv_silu.sem, conv_silu.next(dve))
                    dve_conv(dve, step, bank, conv[n_done % 2], n,
                             [col("ssm_conv_w_2", 12 * i + j, 1) for i in range(3)], col("ssm_conv_b_2", j, 1))
                    n_done += 1
                if panel == 0:
                    dve_dt_sums(dve, step)
            dve.wait_ge(conv_silu.sem, conv_silu.next(dve, 2))

        def act_xbc(act, step):
            n_done = 0
            for panel in range(3):
                for dst, n, j in conv_tiles(panel):
                    act.wait_ge(conv_ready.sem, conv_ready.next(act))
                    act.activation(dst, conv[n_done % 2][:, 0:n], ACT.Silu).then_inc(act_done, 1)
                    act.wait_ge(act_done, step.next())
                    act.sem_inc(conv_silu.sem, 1)
                    n_done += 1
                if panel == 0:
                    act_dt_sums(act, step)
                for _, n, j in conv_tiles(panel):
                    if j >= 10:
                        continue
                    act.wait_ge(to_act.full, to_act.next_full())
                    bank = to_act.take()
                    if j < 8:
                        dst = (xs_tok if n == T else ctx_xs)[:, :, j * P:(j + 1) * P]
                    else:
                        dst = (b_tok if n == T else b_ctx)[:, :, (j - 8) * P:(j - 7) * P]
                    act.activation(dst, bank[:, 0:n].rearrange("p (t c) -> p t c", c=P), ACT.Copy).then_inc(to_act.free, 1)
            act.wait_ge(to_act.free, to_act.own_reads())
            act.sem_inc(xs_ready.sem, 1)

        def ssm_units():
            for d in range(2):
                for c in (range(NC - CT, NC) if d == 0 else range(NC - 1, NC - CT - 1, -1)):
                    yield d, c
                for c in (range(TT) if d == 0 else range(TT - 1, -1, -1)):
                    yield d, c

        def head_cols(x, d, c, g=None):
            h0, n = (0, NH) if g is None else (8 * g, 8)
            return x[:, d, c * NH + h0:c * NH + h0 + n]

        def over(x, n):
            return x.rearrange("p (h n) -> p h n", n=1).broadcast_to([P, x.shape[1], n])

        def pe_ssm(pe, mm):
            for d, c in ssm_units():
                tri = con("upper") if d == 0 else con("lower")
                own = c < TT
                if own:
                    chunk = slice(c * P, (c + 1) * P)
                    pe.wait_ge(to_dve.free, to_dve.room())
                    bank = to_dve.fill()
                    for g in range(2):
                        ins = mm(bank[:, g * P:(g + 1) * P], b_t[:, g, chunk], c_t[:, g, chunk])
                        if g:
                            ins.then_inc(to_dve.full, 1)
                    for q4 in range(4):
                        pe.wait_ge(to_dve.free, to_dve.room())
                        bank = to_dve.fill()
                        for i in range(4):
                            h = 4 * q4 + i
                            ins = mm(bank[:, i * P:(i + 1) * P], head_cols(d_ta, d, c)[:, h:h + 1].broadcast_to([P, P]),
                                     tri)
                            if i == 3:
                                ins.then_inc(to_dve.full, 1)
                    pe.wait_ge(ssm_h.sem, ssm_h.next(pe))
                    for g in range(2):
                        pe.wait_ge(to_dve.free, to_dve.room())
                        bank = to_dve.fill()
                        mm(bank[:, :], c_t[:, g, chunk],
                           h_state[d][:, 8 * g:8 * g + 8, :].rearrange("p h x -> p (h x)")).then_inc(to_dve.full, 1)
                pe.wait_ge(ssm_x.sem, ssm_x.next(pe))
                for g in range(2):
                    pe.wait_ge(to_dve.free, to_dve.room())
                    bank = to_dve.fill()
                    bt = (b_tok[:, c, :] if own else b_ctx[:, c - TT, :])[:, g * P:(g + 1) * P]
                    mm(bank[:, :], bt, xw[:, g * 512:(g + 1) * 512]).then_inc(to_dve.full, 1)
                if own:
                    for g in range(2):
                        pe.wait_ge(ssm_probs.sem, ssm_probs.next(pe))
                        pe.wait_ge(to_dve.free, to_dve.room())
                        bank = to_dve.fill()
                        for i in range(8):
                            ins = mm(bank[:, i * 64:(i + 1) * 64], decay[g][:, i, :],
                                     xdt[:, (8 * g + i) * 64:(8 * g + i + 1) * 64])
                            if i == 7:
                                ins.then_inc(to_dve.full, 1)

        def dve_ssm(dve, step):
            tt = lambda o, x, y, op: dve.tensor_tensor(o, x, y, op)
            dve.wait_ge(xs_ready.sem, xs_ready.next(dve))
            heads = lambda x: x.rearrange("p (h x) -> p h x", x=SSM_P)
            for i in range(2):
                dve.memset(h_state[i], 0.0).then_inc(dve_done, 1)
                dve.wait_ge(dve_done, step.next())
            for d, c in ssm_units():
                own = c < TT
                xs = heads(xs_tok[:, c, :] if own else ctx_xs[:, c - TT, :])
                tt(heads(xw), xs, over(head_cols(w_end, d, c), SSM_P), ALU.mult).then_inc(dve_done, 1)
                dve.wait_ge(dve_done, step.next())
                if own:
                    tt(heads(xdt), xs, over(head_cols(d_t, d, c), SSM_P), ALU.mult).then_inc(dve_done, 1)
                    dve.wait_ge(dve_done, step.next())
                dve.sem_inc(ssm_x.sem, 1)
                y_g = lambda g: y_tok[:, c, g * 512:(g + 1) * 512].rearrange("p (h x) -> p h x", x=SSM_P)
                if own:
                    dve.wait_ge(to_dve.full, to_dve.next_full())
                    bank = to_dve.take()
                    dve.tensor_tensor(cb, bank[:, 0:256].rearrange("p (g i) -> p g i", g=2),
                                      con("upper" if d == 0 else "lower").rearrange("p (g i) -> p g i", g=1).broadcast_to([P, 2, P]),
                                      ALU.mult).then_inc(to_dve.free, 1)
                    for g in range(2):
                        for i in range(2):
                            dve.wait_ge(to_dve.full, to_dve.next_full())
                            bank = to_dve.take()
                            dve.tensor_tensor(decay[g][:, 4 * i:4 * i + 4, :], over(head_cols(acs, d, c, g)[:, 4 * i:4 * i + 4], P),
                                              bank[:, :].rearrange("p (h i) -> p h i", i=P), ALU.subtract).then_inc(to_dve.free, 1)
                        dve.wait_ge(to_dve.free, to_dve.own_reads())
                        dve.tensor_scalar(decay[g], decay[g], 0.0, None, ALU.max).then_inc(dve_done, 1)
                        dve.wait_ge(dve_done, step.next())
                        dve.sem_inc(ssm_seg.sem, 1)
                    if c == (0 if d == 0 else TT - 1):
                        dve.sem_inc(ssm_h.sem, 1)
                    for g in range(2):
                        dve.wait_ge(to_dve.full, to_dve.next_full())
                        bank = to_dve.take()
                        dst = y_g(g) if d == 0 else y_part.rearrange("p (h x) -> p h x", x=SSM_P)
                        dve.tensor_tensor(dst, bank[:, :].rearrange("p (h x) -> p h x", x=SSM_P),
                                          over(head_cols(e_acs, d, c, g), SSM_P), ALU.mult).then_inc(to_dve.free, 1)
                        dve.wait_ge(to_dve.free, to_dve.own_reads())
                        if d == 1:
                            tt(y_g(g), y_g(g), dst, ALU.add).then_inc(dve_done, 1)
                            dve.wait_ge(dve_done, step.next())
                for g in range(2):
                    h = h_state[d][:, 8 * g:8 * g + 8, :]
                    tt(h, h, over(head_cols(e_tot, d, c, g), SSM_P), ALU.mult).then_inc(dve_done, 1)
                    dve.wait_ge(dve_done, step.next())
                    dve.wait_ge(to_dve.full, to_dve.next_full())
                    bank = to_dve.take()
                    dve.tensor_tensor(h, h, bank[:, :].rearrange("p (h x) -> p h x", x=SSM_P), ALU.add).then_inc(to_dve.free, 1)
                    dve.wait_ge(to_dve.free, to_dve.own_reads())
                if own:
                    if c != (TT - 1 if d == 0 else 0):
                        dve.sem_inc(ssm_h.sem, 1)
                    for g in range(2):
                        dve.wait_ge(to_dve.full, to_dve.next_full())
                        bank = to_dve.take()
                        dve.tensor_tensor(y_g(g), y_g(g), bank[:, :].rearrange("p (h x) -> p h x", x=SSM_P), ALU.add)\
                           .then_inc(to_dve.free, 1)
                    dve.wait_ge(to_dve.free, to_dve.own_reads())
            for t in range(TT):
                tt(heads(xs_tok[:, t, :]), heads(xs_tok[:, t, :]), over(ssm_d, SSM_P), ALU.mult)\
                    .then_inc(dve_done, 1)
                dve.wait_ge(dve_done, step.next())
                tt(y_tok[:, t, :], y_tok[:, t, :], xs_tok[:, t, :], ALU.add).then_inc(dve_done, 1)
                dve.wait_ge(dve_done, step.next())
            for half in range(2):
                for t in range(TT):
                    dve.wait_ge(z_ready.sem, z_ready.next(dve))
                    cc = slice(half * 512, (half + 1) * 512)
                    tt(y_tok[:, t, cc], y_tok[:, t, cc], z_buf[t % 2], ALU.mult).then_inc(dve_done, 1)
                    dve.wait_ge(dve_done, step.next())
                    dve.sem_inc(z_used.sem, 1)
            dve.wait_ge(y_sq.sem, y_sq.next(dve))
            dve.reciprocal(y_rms, y_rms).then_inc(dve_done, 1)
            dve.wait_ge(dve_done, step.next())
            for t in range(TT):
                dve.tensor_scalar(y_tok[:, t, :], y_tok[:, t, :], y_rms[:, t:t + 1], None, ALU.mult)\
                    .then_inc(dve_done, 1)
                dve.wait_ge(dve_done, step.next())
            dve.sem_inc(y_normed.sem, 1)

        z_buf = [part(SSM_TMP + i * T, T) for i in range(2)]
        y_sqr = part(SSM_TMP + 1024, D)
        y_rms = part(SSM_TMP + 2048, TT)
        ys_t = freed[0].rearrange("p (m t) -> p m t", t=T)

        def pool_ssm(pool, step):
            for d, c in ssm_units():
                if c < TT:
                    for g in range(2):
                        pool.wait_ge(ssm_exp.sem, ssm_exp.next(pool))
                        pool.tensor_tensor(decay[g], decay[g], cb[:, g:g + 1, :].broadcast_to([P, 8, P]), ALU.mult)\
                            .then_inc(pool_done, 1)
                        pool.wait_ge(pool_done, step.next())
                        pool.sem_inc(ssm_probs.sem, 1)

        def act_ssm(act, step):
            for d, c in ssm_units():
                if c < TT:
                    for g in range(2):
                        act.wait_ge(ssm_seg.sem, ssm_seg.next(act))
                        act.activation(decay[g], decay[g], ACT.Exp, scale=-1.0).then_inc(act_done, 1)
                        act.wait_ge(act_done, step.next())
                        act.sem_inc(ssm_exp.sem, 1)
            for half in range(2):
                for t in range(TT):
                    act.wait_ge(to_act.full, to_act.next_full())
                    bank = to_act.take()
                    n = half * TT + t
                    if n >= 2:
                        act.wait_ge(z_used.sem, z_used.next(act))
                    act.activation(z_buf[t % 2], bank[:, :], ACT.Silu).then_inc(to_act.free, 1)
                    act.wait_ge(to_act.free, to_act.own_reads())
                    act.sem_inc(z_ready.sem, 1)
            act.wait_ge(z_used.sem, z_used.next(act, 2))
            for t in range(TT):
                act.activation(y_sqr, y_tok[:, t, :], ACT.Square, accum_out=y_rms[:, t:t + 1]).then_inc(act_done, 1)
                act.wait_ge(act_done, step.next())
            act.activation(y_rms, y_rms, ACT.Sqrt, scale=1.0 / D, bias=eps_col[:, 0:1]).then_inc(act_done, 1)
            act.wait_ge(act_done, step.next())
            act.sem_inc(y_sq.sem, 1)
            for m in range(DT):
                act.wait_ge(to_act.full, to_act.next_full())
                bank = to_act.take()
                act.activation(ys_t[:, m, :], bank[:, :], ACT.Copy, scale=col("ssm_norm_2", m, 1)).then_inc(to_act.free, 1)
            act.wait_ge(to_act.free, to_act.own_reads())
            act.sem_inc(ys_ready.sem, 1)

        def pe_ssm_out(pe, mm):
            for half in range(2):
                s, w = panels2.use(DT, 512)
                pe.wait_ge(panels2.loaded[s], panels2.arrived(s))
                for t in range(TT):
                    pe.wait_ge(to_act.free, to_act.room())
                    bank = to_act.fill()
                    for k in range(DT):
                        ins = mm(bank[:, :], hidden[:, k, t * P:(t + 1) * P], w[:, k, :], k == 0, k == DT - 1)
                        if k == DT - 1:
                            ins.then_inc(to_act.full, 1)
                mm.done(panels2.used[s])
            pe.wait_ge(y_normed.sem, y_normed.next(pe))
            for m in range(DT):
                pe.wait_ge(to_act.free, to_act.room())
                bank = to_act.fill()
                for t in range(TT):
                    ins = mm.transpose(bank[:, t * P:(t + 1) * P], y_tok[:, t, m * P:(m + 1) * P], ident)
                    if t == TT - 1:
                        ins.then_inc(to_act.full, 1)

        def pool_rope_load(pool):
            pool.wait_ge(ys_ready.sem, ys_ready.next(pool))
            pool.dma_start(rope.rearrange("p a t -> p (a t)"), a["rope"]).then_inc(rope_loaded.sem, 16)

        q_t, k_t, k_sw = part(2048, 4, T), part(4096, T), part(4608, T)
        kc_t, kc_sw = part(5120, CTX), part(5376, CTX)
        v_all = part(5632, TT + CT, P)
        rope = part(6400, 2, T)
        p_sb = [part(7424 + i * 768, 768) for i in range(2)]
        pt_sb = [part(8960 + i * 768, 768) for i in range(2)]
        att_tok = part(10496, T)
        rot = part(11008, T)
        att_small = part(11520, 64)
        neg_max, row_sum, row_inv, tmp_max = (att_small[:, i * 8:(i + 1) * 8] for i in range(4))
        ya_t, yc_t = part(11648, 4, T), part(13696, 4, T)
        nrm_sq, nrm_std = part(7424, T), part(8192, T)
        att_pairs = [psum_all[:, 0:2, :].rearrange("p a b -> p (a b)"), psum_all[:, 2:4, :].rearrange("p a b -> p (a b)")]
        pt_banks, y_bank, turn_bank = psum[4:6], psum[6], psum[7]

        kv_ready = signal("kv_ready")
        head_sq = signal("head_sq")
        head_std = signal("head_std")
        head_norm = signal("head_norm")
        roped = signal("roped")
        att_in = signal("att_in")
        s_full = signal("scores_full")
        max_ready = signal("max_ready")
        p_ready = signal("p_ready")
        pt_full = signal("pt_full")
        pt_act = signal("pt_act")
        pt_dve = signal("pt_dve")
        y_full = signal("y_full")
        sink_in = signal("sink_in")
        sink_exp = signal("sink_exp")
        att_scaled = signal("att_scaled")
        att_turned = signal("att_turned")
        att_out = signal("att_out")
        att_done = signal("att_done")

        def att_units(kind):
            for n in range(TT):
                lo, hi = (max(0, n - 1), min(TT, n + 2)) if kind == 0 else (0, TT)
                for h in range(ATT_HEADS):
                    yield n, h, lo, (hi - lo) * P, list(range(lo, hi)) + list(range(TT, TT + CT))

        def pe_att_in(pe, mm, kind):
            if kind == 0:
                pe.wait_ge(ys_ready.sem, ys_ready.next(pe))
                pe.wait_ge(rope_loaded.sem, rope_loaded.next(pe, 16))
            s, w = panels2.use(DT, 512)
            pe.wait_ge(panels2.loaded[s], panels2.arrived(s))
            for m in range(4):
                pe.wait_ge(to_act.free, to_act.room())
                bank = to_act.fill()
                for k in range(DT):
                    ins = mm(bank[:, :], w[:, k, m * P:(m + 1) * P], hidden[:, k, :], k == 0, k == DT - 1)
                    if k == DT - 1:
                        ins.then_inc(to_act.full, 1)
            mm.done(panels2.used[s])
            s, w = panels2.use(DT, 256)
            pe.wait_ge(panels2.loaded[s], panels2.arrived(s))
            for src, n in ((hidden, T), (hc, CTX)):
                pe.wait_ge(to_act.free, to_act.room())
                bank = to_act.fill()
                for k in range(DT):
                    ins = mm(bank[:, 0:n], w[:, k, 0:P], src[:, k, :], k == 0, k == DT - 1)
                    if k == DT - 1:
                        ins.then_inc(to_act.full, 1)
            for src, n in ((hidden, TT), (hc, CT)):
                pe.wait_ge(to_act.free, to_act.room())
                bank = to_act.fill()
                for t in range(n):
                    for k in range(DT):
                        ins = mm(bank[:, t * P:(t + 1) * P], src[:, k, t * P:(t + 1) * P],
                                 w[:, k, P:2 * P], k == 0, k == DT - 1)
                        if k == DT - 1 and t == n - 1:
                            ins.then_inc(to_act.full, 1)
            mm.done(panels2.used[s])
            pe.wait_ge(kv_ready.sem, kv_ready.next(pe))
            if kind == 1:
                for v, n in HEADS_NORMED:
                    pe.wait_ge(head_sq.sem, head_sq.next(pe))
                    pe.wait_ge(to_act.free, to_act.room())
                    bank = to_act.fill()
                    mm(bank[:, 0:n], con("head_sum"), nrm_sq[:, 0:n]).then_inc(to_act.full, 1)
                pe.wait_ge(head_norm.sem, head_norm.next(pe, len(HEADS_NORMED)))
            for v in (*[q_t[:, m, :] for m in range(4)], k_t):
                pe.wait_ge(to_dve.free, to_dve.room())
                bank = to_dve.fill()
                mm(bank[:, :], con("rotate"), v).then_inc(to_dve.full, 1)
            pe.wait_ge(roped.sem, roped.next(pe))
            for v, n in ((k_t, T), (kc_t, CTX)):
                pe.wait_ge(to_act.free, to_act.room())
                bank = to_act.fill()
                mm(bank[:, 0:n], con("swap"), v).then_inc(to_act.full, 1)
            pe.wait_ge(to_act.free, to_act.all_sent())
            pe.wait_ge(to_dve.free, to_dve.all_sent())

        HEADS_NORMED = [(q_t[:, m, :], T) for m in range(4)] + [(k_t, T), (kc_t, CTX)]

        def act_att_in(act, step, kind):
            if kind == 1:
                act.wait_ge(att_done.sem, att_done.next(act))
            for dst, n in (*[(q_t[:, m, :], T) for m in range(4)], (k_t, T), (kc_t, CTX),
                           (v_all[:, 0:TT, :].rearrange("p t c -> p (t c)"), T),
                           (v_all[:, TT:TT + CT, :].rearrange("p t c -> p (t c)"), CTX)):
                act.wait_ge(to_act.full, to_act.next_full())
                bank = to_act.take()
                act.activation(dst, bank[:, 0:n], ACT.Copy).then_inc(to_act.free, 1)
            act.wait_ge(to_act.free, to_act.own_reads())
            act.sem_inc(kv_ready.sem, 1)
            if kind == 1:
                for i, (v, n) in enumerate(HEADS_NORMED):
                    act.activation(nrm_sq[:, 0:n], v, ACT.Square).then_inc(act_done, 1)
                    act.wait_ge(act_done, step.next())
                    act.sem_inc(head_sq.sem, 1)
                    act.wait_ge(to_act.full, to_act.next_full())
                    bank = to_act.take()
                    if i:
                        act.wait_ge(head_norm.sem, head_norm.next(act))
                    act.activation(nrm_std[:, 0:n], bank[:, 0:n], ACT.Sqrt, scale=1.0 / HD, bias=eps_col[:, 0:1]).then_inc(to_act.free, 1)
                    act.wait_ge(to_act.free, to_act.own_reads())
                    act.sem_inc(head_std.sem, 1)
            for dst, n in ((k_sw, T), (kc_sw, CTX)):
                act.wait_ge(to_act.full, to_act.next_full())
                bank = to_act.take()
                act.activation(dst, bank[:, 0:n], ACT.Copy).then_inc(to_act.free, 1)
            act.wait_ge(to_act.free, to_act.own_reads())
            act.sem_inc(att_in.sem, 1)

        def dve_att_in(dve, step, kind):
            dve.wait_ge(kv_ready.sem, kv_ready.next(dve))
            if kind == 0:
                dve.wait_ge(rope_loaded.sem, rope_loaded.next(dve, 16))
            if kind == 1:
                for i, (v, n) in enumerate(HEADS_NORMED):
                    dve.wait_ge(head_std.sem, head_std.next(dve))
                    dve.reciprocal(nrm_std[:, 0:n], nrm_std[:, 0:n]).then_inc(dve_done, 1)
                    dve.wait_ge(dve_done, step.next())
                    gain = qk_gain[:, 0:1] if i < 4 else qk_gain[:, 1:2]
                    dve.scalar_tensor_tensor(v, v, gain, nrm_std[:, 0:n], ALU.mult, ALU.mult).then_inc(dve_done, 1)
                    dve.wait_ge(dve_done, step.next())
                    dve.sem_inc(head_norm.sem, 1)
            for v in (*[q_t[:, m, :] for m in range(4)], k_t):
                dve.wait_ge(to_dve.full, to_dve.next_full())
                bank = to_dve.take()
                dve.tensor_tensor(rot, bank[:, :], rope[:, 1, :], ALU.mult).then_inc(to_dve.free, 1)
                dve.wait_ge(to_dve.free, to_dve.own_reads())
                dve.tensor_tensor(v, v, rope[:, 0, :], ALU.mult).then_inc(dve_done, 1)
                dve.wait_ge(dve_done, step.next())
                dve.tensor_tensor(v, v, rot, ALU.add).then_inc(dve_done, 1)
                dve.wait_ge(dve_done, step.next())
            dve.sem_inc(roped.sem, 1)

        def split_tiles(tiles):
            k = (len(tiles) + 1) // 2
            return tiles[:k], tiles[k:]

        def pe_att(pe, mm, kind):
            units_ = list(att_units(kind))
            U = len(units_)
            base = kind * U

            def scores(u):
                n, h, lo, w, tiles = units_[u]
                half, j = slice(64 * (h % 2), 64 * (h % 2) + 64), h // 4
                keys, ckeys = (k_t, kc_t) if h % 2 == j else (k_sw, kc_sw)
                pair = att_pairs[u % 2]
                if base + u >= 2:
                    pe.wait_ge(p_ready.sem, base + u - 1)
                qb = q_t[half, h // 2, n * P:(n + 1) * P]
                mm(pair[:, 512 - w:512], qb, keys[half, lo * P:lo * P + w])
                mm(pair[:, 512:768], qb, ckeys[half, :]).then_inc(s_full.sem, 1)

            def turns(u):
                pe.wait_ge(p_ready.sem, base + u + 1)
                if base + u >= 1:
                    pe.wait_ge(pt_act.sem, base + u)
                    pe.wait_ge(pt_dve.sem, base + u)
                tiles = units_[u][4]
                at = 0
                for b, part_tiles in enumerate(split_tiles(tiles)):
                    for i in range(len(part_tiles)):
                        last = i == len(part_tiles) - 1
                        ins = mm.transpose(pt_banks[b][:, i * P:(i + 1) * P], p_sb[u % 2][:, at * P:(at + 1) * P],
                                           ident)
                        if last:
                            ins.then_inc(pt_full.sem, 1)
                        at += 1

            def values(u):
                n, h, lo, w, tiles = units_[u]
                pe.wait_ge(pt_act.sem, base + u + 1)
                pe.wait_ge(pt_dve.sem, base + u + 1)
                if h == 0 and kind * TT + n >= 1:
                    pe.wait_ge(att_scaled.sem, kind * TT + n)
                j = h // 4
                for i, t in enumerate(tiles):
                    ins = mm(y_bank[:, h * HD:(h + 1) * HD], pt_sb[u % 2][:, i * P:(i + 1) * P],
                             v_all[:, t, j * HD:(j + 1) * HD], i == 0, i == len(tiles) - 1)
                    if h == ATT_HEADS - 1 and i == len(tiles) - 1:
                        ins.then_inc(y_full.sem, 1)

            def turn_out(n):
                pe.wait_ge(att_scaled.sem, kind * TT + n + 1)
                if kind * TT + n >= 1:
                    pe.wait_ge(att_turned.sem, kind * TT + n)
                for m in range(4):
                    ins = mm.transpose(turn_bank[:, m * P:(m + 1) * P], att_tok[:, m * P:(m + 1) * P], ident)
                    if m == 3:
                        ins.then_inc(att_out.sem, 1)

            pe.wait_ge(att_in.sem, att_in.next(pe))
            for i in range(U + 2):
                if i < U:
                    scores(i)
                if i >= 2:
                    values(i - 2)
                if 1 <= i <= U:
                    turns(i - 1)
                if i >= 4 and (i - 4) % ATT_HEADS == ATT_HEADS - 1:
                    turn_out((i - 4) // ATT_HEADS)
            turn_out(TT - 1)

        def dve_att(dve, step, kind):
            units_ = list(att_units(kind))
            U = len(units_)
            scale = HD ** -0.5

            def maximum(u):
                n, h, lo, w, tiles = units_[u]
                pair = att_pairs[u % 2]
                dve.wait_ge(s_full.sem, s_full.next(dve))
                if kind == 0:
                    if n > 0:
                        dve.tensor_tensor(pair[:, 512 - w:640 - w], pair[:, 512 - w:640 - w], con("prev_mask"), ALU.add)\
                            .then_inc(dve_done, 1)
                        dve.wait_ge(dve_done, step.next())
                    if n < TT - 1:
                        dve.tensor_tensor(pair[:, 384:512], pair[:, 384:512], con("next_mask"), ALU.add)\
                            .then_inc(dve_done, 1)
                        dve.wait_ge(dve_done, step.next())
                dve.tensor_reduce(tmp_max[:, 0:1], pair[:, 512 - w:768], AX_X, ALU.max).then_inc(dve_done, 1)
                dve.wait_ge(dve_done, step.next())
                if kind == 0:
                    dve.scalar_tensor_tensor(tmp_max[:, 0:1], tmp_max[:, 0:1], scale, sink[:, h:h + 1], ALU.mult, ALU.max)\
                        .then_inc(dve_done, 1)
                    dve.wait_ge(dve_done, step.next())
                dve.tensor_scalar(neg_max[:, h:h + 1], tmp_max[:, 0:1], -1.0 if kind == 0 else -scale, None, ALU.mult)\
                    .then_inc(dve_done, 1)
                dve.wait_ge(dve_done, step.next())
                dve.sem_inc(max_ready.sem, 1)

            def copy(u):
                tiles = units_[u][4]
                first, second = split_tiles(tiles)
                dve.wait_ge(pt_full.sem, pt_full.next(dve, 2))
                k, m = len(first), len(second)
                dve.tensor_copy(pt_sb[u % 2][:, k * P:(k + m) * P], pt_banks[1][:, 0:m * P]).then_inc(dve_done, 1)
                dve.wait_ge(dve_done, step.next())
                dve.sem_inc(pt_dve.sem, 1)

            def block_out(n):
                dve.wait_ge(y_full.sem, y_full.next(dve))
                if kind == 0:
                    dve.tensor_tensor(row_inv, neg_max, sink, ALU.add).then_inc(dve_done, 1)
                    dve.wait_ge(dve_done, step.next())
                    dve.sem_inc(sink_in.sem, 1)
                    dve.wait_ge(sink_exp.sem, sink_exp.next(dve))
                    dve.tensor_tensor(row_sum, row_sum, row_inv, ALU.add).then_inc(dve_done, 1)
                    dve.wait_ge(dve_done, step.next())
                dve.reciprocal(row_inv, row_sum).then_inc(dve_done, 1)
                dve.wait_ge(dve_done, step.next())
                if kind * TT + n >= 1:
                    dve.wait_ge(att_turned.sem, att_turned.next(dve))
                dve.tensor_tensor(att_tok.rearrange("p (h x) -> p h x", x=HD),
                                  y_bank[:, :].rearrange("p (h x) -> p h x", x=HD), over(row_inv, HD), ALU.mult)\
                    .then_inc(dve_done, 1)
                dve.wait_ge(dve_done, step.next())
                dve.sem_inc(att_scaled.sem, 1)

            for i in range(U + 2):
                if i < U and i % ATT_HEADS != 0:
                    maximum(i)
                if 1 <= i <= U:
                    copy(i - 1)
                if i >= ATT_HEADS and i % ATT_HEADS == 0:
                    block_out(i // ATT_HEADS - 1)
                if i < U and i % ATT_HEADS == 0:
                    maximum(i)

        def act_att(act, step, kind):
            units_ = list(att_units(kind))
            U = len(units_)
            y_dst = ya_t if kind == 0 else yc_t

            def exps(u):
                n, h, lo, w, tiles = units_[u]
                act.wait_ge(max_ready.sem, max_ready.next(act))
                if kind * U + u >= 2:
                    pt_full_wait(act, kind * U + u - 1)
                act.activation(p_sb[u % 2][:, 0:w + CTX], att_pairs[u % 2][:, 512 - w:768], ACT.Exp,
                               bias=neg_max[:, h:h + 1], scale=HD ** -0.5, accum_out=row_sum[:, h:h + 1])\
                    .then_inc(act_done, 1)
                act.wait_ge(act_done, step.next())
                act.sem_inc(p_ready.sem, 1)

            def copy(u):
                first, _ = split_tiles(units_[u][4])
                pt_full_wait(act, kind * U + u + 1)
                act.activation(pt_sb[u % 2][:, 0:len(first) * P], pt_banks[0][:, 0:len(first) * P], ACT.Copy)\
                    .then_inc(act_done, 1)
                act.wait_ge(act_done, step.next())
                act.sem_inc(pt_act.sem, 1)

            def block_out(n):
                act.wait_ge(att_out.sem, att_out.next(act))
                act.activation(y_dst[:, :, n * P:(n + 1) * P], turn_bank[:, :].rearrange("p (m t) -> p m t", t=P), ACT.Copy)\
                    .then_inc(act_done, 1)
                act.wait_ge(act_done, step.next())
                act.sem_inc(att_turned.sem, 1)

            def sink_term():
                if kind == 0:
                    act.wait_ge(sink_in.sem, sink_in.next(act))
                    act.activation(row_inv, row_inv, ACT.Exp).then_inc(act_done, 1)
                    act.wait_ge(act_done, step.next())
                    act.sem_inc(sink_exp.sem, 1)

            for i in range(U + 2):
                if i < U and i % ATT_HEADS != 0:
                    exps(i)
                if 1 <= i <= U:
                    copy(i - 1)
                if i >= ATT_HEADS and i % ATT_HEADS == 0:
                    sink_term()
                if i < U and i % ATT_HEADS == 0:
                    exps(i)
                if i >= 4 and (i - 4) % ATT_HEADS == ATT_HEADS - 1:
                    block_out((i - 4) // ATT_HEADS)
            block_out(TT - 1)
            act.sem_inc(att_done.sem, 1)

        def pt_full_wait(act, units_turned):
            act.wait_ge(pt_full.sem, 2 * units_turned)

        g_buf = [part(2048 + i * 2048, 4, T) for i in range(2)]
        merged = freed[1].rearrange("p (m t) -> p m t", t=T)
        m_tmp = part(6400, T)
        gate_ready = signal("gate_ready")
        gate_used = signal("gate_used")
        merged_ready = signal("merged_ready")

        def branches():
            return ((ya_t, 4), (ys_t, DT), (yc_t, 4))

        def pe_merge(pe, mm):
            pe.wait_ge(att_done.sem, att_done.next(pe, 2))
            for half in range(2):
                for y, k_tiles in branches():
                    for src, kt, banks in ((hidden, DT, to_act), (y, k_tiles, to_dve)):
                        s, w = panels2.use(kt, 512)
                        pe.wait_ge(panels2.loaded[s], panels2.arrived(s))
                        for m in range(4):
                            pe.wait_ge(banks.free, banks.room())
                            bank = banks.fill()
                            for k in range(kt):
                                ins = mm(bank[:, :], w[:, k, m * P:(m + 1) * P], src[:, k, :], k == 0, k == kt - 1)
                                if k == kt - 1:
                                    ins.then_inc(banks.full, 1)
                        mm.done(panels2.used[s])
            mm.settle()
            pe.wait_ge(merged_ready.sem, merged_ready.next(pe))
            for half in range(2):
                pe_linear2(pe, mm, to_dve, merged, DT, 512)

        def pe_linear2(pe, mm, banks, x, k_tiles, width):
            s, w = panels2.use(k_tiles, width)
            pe.wait_ge(panels2.loaded[s], panels2.arrived(s))
            for m in range(width // P):
                pe.wait_ge(banks.free, banks.room())
                bank = banks.fill()
                for k in range(k_tiles):
                    ins = mm(bank[:, :], w[:, k, m * P:(m + 1) * P], x[:, k, :], k == 0, k == k_tiles - 1)
                    if k == k_tiles - 1:
                        ins.then_inc(banks.full, 1)
            mm.done(panels2.used[s])

        def act_merge(act, step):
            for i in range(6):
                if i >= 2:
                    act.wait_ge(gate_used.sem, gate_used.next(act))
                for m in range(4):
                    act.wait_ge(to_act.full, to_act.next_full())
                    bank = to_act.take()
                    act.activation(g_buf[i % 2][:, m, :], bank[:, :], ACT.Sigmoid).then_inc(to_act.free, 1)
                act.wait_ge(to_act.free, to_act.own_reads())
                act.sem_inc(gate_ready.sem, 1)

        def dve_merge(dve, step):
            for i in range(6):
                half, branch = i // 3, i % 3
                dve.wait_ge(gate_ready.sem, gate_ready.next(dve))
                for m in range(4):
                    dve.wait_ge(to_dve.full, to_dve.next_full())
                    bank = to_dve.take()
                    dst = merged[:, 4 * half + m, :] if branch == 0 else m_tmp
                    dve.tensor_tensor(dst, g_buf[i % 2][:, m, :], bank[:, :], ALU.mult).then_inc(to_dve.free, 1)
                    dve.wait_ge(to_dve.free, to_dve.own_reads())
                    if branch:
                        dve.tensor_tensor(merged[:, 4 * half + m, :], merged[:, 4 * half + m, :], m_tmp, ALU.add)\
                            .then_inc(dve_done, 1)
                        dve.wait_ge(dve_done, step.next())
                dve.sem_inc(gate_used.sem, 1)
            dve.sem_inc(merged_ready.sem, 1)
            dve_gated_residual(dve, 16)
            dve.sem_inc(resid_ready.sem, 1)

        def dve_gated_residual(dve, first):
            for m in range(DT):
                dve.wait_ge(to_dve.full, to_dve.next_full())
                bank = to_dve.take()
                dve.scalar_tensor_tensor(resid[:, m, :], bank[:, :], mods2[:, first + m, 0:1], resid[:, m, :],
                                         ALU.mult, ALU.add).then_inc(to_dve.free, 1)
                dve.wait_ge(to_dve.free, to_dve.own_reads())
                dve.sem_inc(resid_tile.sem, 1)
            dve.wait_ge(resid_tile.sem, resid_tile.next(dve, DT))

        f_sq, f_std = part(0, DT, T), part(4096, T)
        act_t = part(4608, FT2, T)
        f_conv = part(0, 2, 4 * T)
        ffn_gate = signal("ffn_gate")

        def conv_buf(i):
            return f_conv[:, (i // 4) % 2, (i % 4) * T:(i % 4 + 1) * T]

        def pe_ffn(pe, mm):
            pe_norm(pe, mm, f_sq, T, DT)
            pe.wait_ge(normed.sem, normed.next(pe, DT))
            for c0, c1 in FFN_PANELS:
                for _ in range(2):
                    pe_linear2(pe, mm, to_dve, hidden, DT, c1 - c0)
            mm.settle()
            pe.wait_ge(to_dve.free, to_dve.all_sent())
            for half in range(2):
                banks = []
                for _ in range(4):
                    pe.wait_ge(to_dve.free, to_dve.room())
                    banks.append(to_dve.fill())
                for r0, r1 in DOWN_ROWS:
                    s, w = panels2.use(r1 - r0, 512)
                    pe.wait_ge(panels2.loaded[s], panels2.arrived(s))
                    for m in range(4):
                        for k in range(r0, r1):
                            ins = mm(banks[m][:, :], w[:, k - r0, m * P:(m + 1) * P],
                                     act_t[:, k, :], k == 0, k == FT2 - 1)
                            if k == FT2 - 1:
                                ins.then_inc(to_dve.full, 1)
                    mm.done(panels2.used[s])
                mm.settle()

        def act_ffn(act, step):
            act_norm(act, step, resid[:, :, :], f_sq, f_std, T, DT, D, [mods2[:, 24 + k, 0:1] for k in range(DT)], hidden,
                     after=resid_tile)
            for f in range(FT2):
                act.wait_ge(conv_ready.sem, conv_ready.next(act))
                act.activation(conv_buf(f), conv_buf(f), ACT.Silu).then_inc(act_done, 1)
                act.wait_ge(act_done, step.next())
                act.sem_inc(ffn_gate.sem, 1)

        def dve_ffn(dve, step):
            dve_norm(dve, step, resid, hidden, f_std, DT, A2X)
            for c0, c1 in FFN_PANELS:
                tiles = range(c0 // P, c1 // P)
                for f in tiles:
                    dve.wait_ge(to_dve.full, to_dve.next_full())
                    bank = to_dve.take()
                    dve_conv(dve, step, bank, conv_buf(f), T, [col("ffn_conv_w_2", FT2 * i + f, 1) for i in range(3)],
                             col("ffn_conv_b_2", f, 1))
                for f in tiles:
                    dve.wait_ge(to_dve.full, to_dve.next_full())
                    bank = to_dve.take()
                    dve.wait_ge(ffn_gate.sem, ffn_gate.next(dve))
                    dve.tensor_tensor(act_t[:, f, :], conv_buf(f), bank[:, :], ALU.mult).then_inc(to_dve.free, 1)
            dve.wait_ge(to_dve.free, to_dve.own_reads())
            dve_gated_residual(dve, 40)
            dve.sem_inc(resid_ready.sem, 1)

        o_sq2, o_std2 = part(0, DT, T), part(4096, T)
        out_tok = part(4608, TT, D)
        final_ready = signal("final_ready")
        out_ready = signal("out_ready")
        out_stored = signal("out_stored")

        def pe_out(pe, mm):
            pe_norm(pe, mm, o_sq2, T, DT)
            pe.wait_ge(final_ready.sem, final_ready.next(pe))
            for t in range(TT):
                for g in range(2):
                    pe.wait_ge(to_act.free, to_act.room())
                    bank = to_act.fill()
                    for m in range(4):
                        ins = mm.transpose(bank[:, m * P:(m + 1) * P], hidden[:, 4 * g + m, t * P:(t + 1) * P], ident)
                        if m == 3:
                            ins.then_inc(to_act.full, 1)

        def act_out(act, step):
            act_norm(act, step, resid[:, :, :], o_sq2, o_std2, T, DT, D, after=resid_tile)
            for t in range(TT):
                for g in range(2):
                    act.wait_ge(to_act.full, to_act.next_full())
                    bank = to_act.take()
                    act.activation(out_tok[:, t, g * 512:(g + 1) * 512], bank[:, :], ACT.Copy).then_inc(to_act.free, 1)
                act.wait_ge(to_act.free, to_act.own_reads())
                act.sem_inc(out_ready.sem, 1)

        def dve_out(dve, step):
            dve.wait_ge(std_ready.sem, std_ready.next(dve))
            dve.reciprocal(o_std2, o_std2).then_inc(dve_done, 1)
            dve.wait_ge(dve_done, step.next())
            for k in range(DT):
                dve.scalar_tensor_tensor(hidden[:, k, :], resid[:, k, :], col("final_norm_2", k, 1), o_std2, ALU.mult, ALU.mult)\
                    .then_inc(dve_done, 1)
                dve.wait_ge(dve_done, step.next())
            dve.sem_inc(final_ready.sem, 1)

        def sp_out(sp):
            for t in range(TT):
                sp.wait_ge(out_ready.sem, out_ready.next(sp))
                sp.dma_start(out[0, t * P:(t + 1) * P, :], out_tok[:, t, :]).then_inc(out_stored.sem, 16)
            sp.wait_ge(out_stored.sem, out_stored.next(sp, 16 * TT))

        block = ctx.enter_context(nc.Block())

        @block.sync
        def _(sp):
            sp_first_loads(sp)
            sp_moe(sp)
            sp_extra(sp)
            sp_second_loads(sp)
            sp_out(sp)

        @block.gpsimd
        def _(pool):
            step = Order()
            pool_s5_steps(pool)
            pool_row_loads(pool)
            pool_s5_loads(pool)
            pool_s5(pool, step)
            pool_moe_loads(pool)
            pool_split_tokens(pool)
            pool_ssm(pool, step)
            pool_rope_load(pool)

        @block.tensor
        def _(pe):
            mm = Matmuls(pe)
            pe_turn_inputs(pe, mm)
            pe.wait_ge(silu_ready.sem, silu_ready.next(pe))
            pe_first_mods(pe, mm)
            pe_norm(pe, mm, n_sq, T, DT)
            pe_gla(pe, mm)
            pe_s5(pe, mm)
            pe_project_out(pe, mm)
            pe_norm(pe, mm, m_sq, T, DT)
            pe_norm(pe, mm, n2_sq, T, DT)
            pe_route(pe, mm)
            pe_moe(pe, mm)
            pe_extra(pe, mm)
            pe_norm(pe, mm, m_sq, T, DT)
            pe_second_norms(pe, mm)
            pe_dt(pe, mm)
            pe_xbc(pe, mm)
            pe_ssm(pe, mm)
            pe_ssm_out(pe, mm)
            for kind in range(2):
                pe_att_in(pe, mm, kind)
                pe_att(pe, mm, kind)
            pe_merge(pe, mm)
            pe_ffn(pe, mm)
            pe_out(pe, mm)
            mm.settle()

        @block.scalar
        def _(act):
            step = Order()
            act.sem_inc(to_act.free, len(to_act.banks))
            act.sem_inc(y_banks.free, len(y_banks.banks))
            act.sem_inc(mod_banks.free, len(mod_banks.banks))
            act_first_loads(act)
            act_silus(act, step)
            act_s5_angles(act, step)
            act_first_mods(act)
            act.wait_ge(resid_ready.sem, resid_ready.next(act))
            act_norm(act, step, resid[:, :, :], n_sq, n_std, T, DT, D,
                     [mods[:, k, :] for k in range(DT)], hidden)
            act_gla(act, step)
            act_s5_setup(act, step)
            act_s5(act, step)
            act_norm(act, step, mix, m_sq, m_std, T, DT, D, copied=True)
            act_norm(act, step, resid[:, :, :], n2_sq, n2_std, T, DT, D,
                     [mods[:, 24 + k, :] for k in range(DT)], hidden, after=resid_tile)
            act_route(act, step)
            act_moe(act, step)
            act_extra(act, step)
            act.wait_ge(turn, 16 * STAGES + 1)
            act_norm(act, step, hidden[:, :, :], m_sq, m_std, T, DT, D)
            act_second_norms(act, step)
            act_dt(act, step)
            act_xbc(act, step)
            act_ssm(act, step)
            for kind in range(2):
                act_att_in(act, step, kind)
                act_att(act, step, kind)
            act_merge(act, step)
            act_ffn(act, step)
            act_out(act, step)

        @block.vector
        def _(dve):
            step = Order()
            dve.sem_inc(to_dve.free, len(to_dve.banks))
            dve_turn_inputs(dve, step)
            dve_s5_angles(dve, step)
            dve_first_factors(dve, step)
            dve_norm(dve, step, resid, hidden, n_std, DT, A1)
            dve_gla(dve, step)
            dve_s5_setup(dve, step)
            dve_s5(dve, step)
            dve_add_normed(dve, step, mix, m_std, G1)
            dve_norm(dve, step, resid, hidden, n2_std, DT, A2)
            dve_route(dve, step)
            dve_moe(dve, step)
            dve_extra(dve, step)
            dve_add_normed(dve, step, hidden, m_std, G2)
            dve_second_norms(dve, step)
            dve_dt(dve, step)
            dve_xbc(dve, step)
            dve_ssm(dve, step)
            for kind in range(2):
                dve_att_in(dve, step, kind)
                dve_att(dve, step, kind)
            dve_merge(dve, step)
            dve_ffn(dve, step)
            dve_out(dve, step)


INPUTS = ["x", "c", "ada_w", "ada_b", "mix_pre_g", "mix_post_g", "ffn_pre_g", "ffn_post_g", "w_in", "w_alpha",
          "b_alpha", "gla_norm_g", "s5_lambda_re", "s5_lambda_im", "s5_log_dt", "s5_b_re", "s5_b_im", "s5_c_re",
          "s5_c_im", "s5_d", "s5_glu_w", "s5_glu_b", "w_out", "router_w", "router_b", "exp_w_gu", "exp_b_gu",
          "exp_w_down", "exp_b_down", "c_2", "ctx_2", "c_ctx_2", "w_mod_2", "b_mod_2", "norm1_2", "norm2_2",
          "w_in_2", "a_sink_2", "ssm_conv_w_2", "ssm_conv_b_2", "ssm_A_log_2", "ssm_dt_bias_2", "ssm_D_2",
          "ssm_norm_2", "c_q_norm_2", "c_k_norm_2", "w_oa_2", "w_ob_2", "w_oc_2", "w_out_2", "ffn_w_up_2",
          "ffn_w_gate_2", "ffn_conv_w_2", "ffn_conv_b_2", "ffn_w_down_2", "final_norm_2"]


def kernel(**inputs):
    from concourse import bacc
    from concourse.bass_utils import run_bass_kernel_spmd

    nc = bacc.Bacc("TRN2", target_bir_lowering=False, num_devices=1)
    table, where, rope = constants()
    arrays, a = {}, {}
    for name, v in [*((n, inputs[n]) for n in INPUTS), ("const", table), ("rope", rope)]:
        v = np.ascontiguousarray(v)
        arrays[f"in_{name}"] = v
        a[name] = nc.dram_tensor(f"in_{name}", v.shape, mybir.dt.from_np(v.dtype), kind="ExternalInput").ap()
    out = nc.dram_tensor("out", (1, T, D), F32, kind="ExternalOutput").ap()
    build(nc, a, table, where, out)
    r = run_bass_kernel_spmd(nc, [arrays], core_ids=[0])
    return r.results[0]["out"]
```
